# Optimizing a Trainium2 kernel written in Bass

```python
import math
import jax, jax.numpy as jnp
from jax import lax
import numpy as np

D_MODEL = 1024
BATCH = 1
SEQ = 512
DEPTH = 2

GRID_W = 64
CTX_LEN = 256
HEAD_DIM = 64
BLOCK = 128
EPS = 1e-6
ROPE_THETA = 10000.0
NEG_INF = -1e30

A_HEADS = 4
A_KV_HEADS = 2
WINDOW = 128
B_HEADS = 4
B_Q_RANK = 192
B_KV_RANK = 128
B_NOPE = 64
B_ROPE = 32
B_V = 64
C_HEADS = 4
C_QK = 32
C_V = 64
D_HEADS = 4
D_KV_HEADS = 2
N_EXPERTS = 16
CAPACITY_FACTOR = 2
D_EXPERT = 1024

A_COLS = A_HEADS * HEAD_DIM + 2 * A_KV_HEADS * HEAD_DIM
B_COLS = B_Q_RANK + B_KV_RANK + B_ROPE
C_COLS = 4 * C_HEADS * C_QK + C_HEADS * C_V
D_COLS = D_HEADS * HEAD_DIM + 2 * D_KV_HEADS * HEAD_DIM
IN_COLS = A_COLS + B_COLS + C_COLS + D_COLS
COL_SPLITS = (A_COLS, A_COLS + B_COLS, A_COLS + B_COLS + C_COLS)
MIX_WIDTH = A_HEADS * HEAD_DIM + B_HEADS * B_V + C_HEADS * C_V + D_HEADS * HEAD_DIM

kernel_name = "hybrid_parallel_heads_diffusion_block"

def rmsnorm(x, g):
    xf = x.astype(jnp.float32)
    y = xf * lax.rsqrt(jnp.mean(xf * xf, axis=-1, keepdims=True) + EPS)
    return (y * g.astype(jnp.float32)).astype(x.dtype)

def modulate(x, g, shift, scale):
    return rmsnorm(x, g) * (1 + scale) + shift

def adaln_params(cond, w_mod, b_mod):
    m = jax.nn.silu(cond) @ w_mod + b_mod
    return [t[..., None, :] for t in jnp.split(m, 6, axis=-1)]

def axial_rope_table(n_tokens, rot_dim):
    rows = n_tokens // GRID_W
    row = jnp.repeat(jnp.arange(rows), GRID_W)
    col = jnp.tile(jnp.arange(GRID_W), rows)
    quarter = rot_dim // 4
    inv_freq = ROPE_THETA ** (-jnp.arange(quarter, dtype=jnp.float32) / quarter)
    ang = jnp.concatenate([row[:, None] * inv_freq, col[:, None] * inv_freq], axis=-1)
    return jnp.cos(ang), jnp.sin(ang)

def apply_rope(x, table):
    cos, sin = table
    cos = cos[None, :, None, :].astype(x.dtype)
    sin = sin[None, :, None, :].astype(x.dtype)
    half = x.shape[-1] // 2
    x1, x2 = x[..., :half], x[..., half:]
    return jnp.concatenate([x1 * cos - x2 * sin, x1 * sin + x2 * cos], axis=-1)

def split_heads(t, n):
    return t.reshape(t.shape[0], t.shape[1], n, -1)

def merge_heads(t):
    return t.reshape(t.shape[0], t.shape[1], -1)

def dense_attention(q, k, v, scale, sink=None):
    b, sq, hq, dk = q.shape
    hkv = k.shape[2]
    g = hq // hkv
    nb = sq // BLOCK
    qb = q.reshape(b, nb, BLOCK, hkv, g, dk).transpose(1, 0, 2, 3, 4, 5)

    def one_block(qblk):
        s = jnp.einsum('bqhgd,bkhd->bhgqk', qblk, k).astype(jnp.float32) * scale
        if sink is not None:
            s_sink = jnp.broadcast_to(sink.astype(jnp.float32).reshape(1, hkv, g, 1, 1), s.shape[:-1] + (1,))
            p = jax.nn.softmax(jnp.concatenate([s, s_sink], axis=-1), axis=-1)[..., :-1]
        else:
            p = jax.nn.softmax(s, axis=-1)
        return jnp.einsum('bhgqk,bkhd->bqhgd', p.astype(v.dtype), v)

    o = lax.map(one_block, qb)
    return o.transpose(1, 0, 2, 3, 4, 5).reshape(b, sq, hq, v.shape[-1])

def window_attention_sink(q, k, v, k_ctx, v_ctx, sink, scale):
    b, s_len, hq, d = q.shape
    hkv = k.shape[2]
    g = hq // hkv
    nb = s_len // BLOCK
    pad = ((0, 0), (BLOCK, BLOCK), (0, 0), (0, 0))
    kp = jnp.pad(k, pad).reshape(b, nb + 2, BLOCK, hkv, d)
    vp = jnp.pad(v, pad).reshape(b, nb + 2, BLOCK, hkv, d)
    kb = jnp.concatenate([kp[:, :-2], kp[:, 1:-1], kp[:, 2:]], axis=2)
    vb = jnp.concatenate([vp[:, :-2], vp[:, 1:-1], vp[:, 2:]], axis=2)
    qb = q.reshape(b, nb, BLOCK, hkv, g, d)
    s_band = jnp.einsum('bnqhgd,bnkhd->bnhgqk', qb, kb).astype(jnp.float32) * scale
    qpos = jnp.arange(BLOCK)[:, None]
    kpos = jnp.arange(3 * BLOCK)[None, :] - BLOCK
    abs_k = (jnp.arange(nb) * BLOCK)[:, None, None] + kpos[None]
    valid = (jnp.abs(kpos - qpos) <= WINDOW)[None] & (abs_k >= 0) & (abs_k < s_len)
    s_band = jnp.where(valid[None, :, None, None], s_band, NEG_INF)
    s_ctx = jnp.einsum('bnqhgd,bkhd->bnhgqk', qb, k_ctx).astype(jnp.float32) * scale
    s_sink = jnp.broadcast_to(sink.astype(jnp.float32).reshape(1, 1, hkv, g, 1, 1), s_band.shape[:-1] + (1,))
    n_ctx = k_ctx.shape[1]
    p = jax.nn.softmax(jnp.concatenate([s_ctx, s_band, s_sink], axis=-1), axis=-1).astype(v.dtype)
    o = (jnp.einsum('bnhgqk,bkhd->bnqhgd', p[..., :n_ctx], v_ctx)
         + jnp.einsum('bnhgqk,bnkhd->bnqhgd', p[..., n_ctx:n_ctx + 3 * BLOCK], vb))
    return o.reshape(b, s_len, hq, d)

def mixer_a_qkv(p, rope):
    q, k, v = jnp.split(p, [A_HEADS * HEAD_DIM, (A_HEADS + A_KV_HEADS) * HEAD_DIM], axis=-1)
    q, k, v = split_heads(q, A_HEADS), split_heads(k, A_KV_HEADS), split_heads(v, A_KV_HEADS)
    if rope is not None:
        q, k = apply_rope(q, rope), apply_rope(k, rope)
    return q, k, v

def mixer_b_qkv(p, q_norm, w_uq, kv_norm, w_ukv, rope):
    cq, ckv, k_rope = jnp.split(p, [B_Q_RANK, B_Q_RANK + B_KV_RANK], axis=-1)
    q = split_heads(rmsnorm(cq, q_norm) @ w_uq, B_HEADS)
    kv = split_heads(rmsnorm(ckv, kv_norm) @ w_ukv, B_HEADS)
    q_nope, q_rope = q[..., :B_NOPE], q[..., B_NOPE:]
    k_nope, v = kv[..., :B_NOPE], kv[..., B_NOPE:]
    k_rope = k_rope[:, :, None, :]
    if rope is not None:
        q_rope, k_rope = apply_rope(q_rope, rope), apply_rope(k_rope, rope)
    k = jnp.concatenate([k_nope, jnp.broadcast_to(k_rope, k_nope.shape[:-1] + (B_ROPE,))], axis=-1)
    return jnp.concatenate([q_nope, q_rope], axis=-1), k, v

def mixer_c_qkv(p, rope):
    q, k, v = jnp.split(p, [2 * C_HEADS * C_QK, 4 * C_HEADS * C_QK], axis=-1)
    q, k = split_heads(q, 2 * C_HEADS), split_heads(k, 2 * C_HEADS)
    if rope is not None:
        q, k = apply_rope(q, rope), apply_rope(k, rope)
    v = jnp.repeat(split_heads(v, C_HEADS), 2, axis=2)
    return q, k, v

def diff_combine(o, lam_params, subln, layer):
    b, s_len = o.shape[:2]
    o = o.reshape(b, s_len, C_HEADS, 2, C_V)
    lam_init = 0.8 - 0.6 * math.exp(-0.3 * layer)
    lp = lam_params.astype(jnp.float32)
    lam = jnp.exp(jnp.sum(lp[0] * lp[1])) - jnp.exp(jnp.sum(lp[2] * lp[3])) + lam_init
    out = o[:, :, :, 0] - lam.astype(o.dtype) * o[:, :, :, 1]
    return merge_heads(rmsnorm(out, subln) * (1 - lam_init))

def mixer_d_qkv(p, q_norm, k_norm, rope):
    q, k, v = jnp.split(p, [D_HEADS * HEAD_DIM, (D_HEADS + D_KV_HEADS) * HEAD_DIM], axis=-1)
    q = rmsnorm(split_heads(q, D_HEADS), q_norm)
    k = rmsnorm(split_heads(k, D_KV_HEADS), k_norm)
    v = split_heads(v, D_KV_HEADS)
    if rope is not None:
        q, k = apply_rope(q, rope), apply_rope(k, rope)
    return q, k, v

def token_mixers(hl, hc, layer, with_ctx_out, w_in, a_sink, b_q_norm, b_w_uq, b_kv_norm, b_w_ukv,
                 c_lambda, c_subln, d_q_norm, d_k_norm, w_out, rope64, rope32):
    pa, pb, pc, pd = jnp.split(hl @ w_in, COL_SPLITS, axis=-1)
    ca, cb, cc, cd = jnp.split(hc @ w_in, COL_SPLITS, axis=-1)
    qa, ka, va = mixer_a_qkv(pa, rope64)
    qac, kac, vac = mixer_a_qkv(ca, None)
    qb, kb, vb = mixer_b_qkv(pb, b_q_norm, b_w_uq, b_kv_norm, b_w_ukv, rope32)
    qbc, kbc, vbc = mixer_b_qkv(cb, b_q_norm, b_w_uq, b_kv_norm, b_w_ukv, None)
    qc, kc, vc = mixer_c_qkv(pc, rope32)
    qcc, kcc, vcc = mixer_c_qkv(cc, None)
    qd, kd, vd = mixer_d_qkv(pd, d_q_norm, d_k_norm, rope64)
    qdc, kdc, vdc = mixer_d_qkv(cd, d_q_norm, d_k_norm, None)
    scale64 = HEAD_DIM ** -0.5
    scale_b = (B_NOPE + B_ROPE) ** -0.5
    scale_c = C_QK ** -0.5
    cat = lambda t_ctx, t_lat: jnp.concatenate([t_ctx, t_lat], axis=1)
    oa = window_attention_sink(qa, ka, va, kac, vac, a_sink, scale64)
    ob = dense_attention(qb, cat(kbc, kb), cat(vbc, vb), scale_b)
    oc = diff_combine(dense_attention(qc, cat(kcc, kc), cat(vcc, vc), scale_c), c_lambda, c_subln, layer)
    od = dense_attention(qd, cat(kdc, kd), cat(vdc, vd), scale64)
    out_lat = jnp.concatenate([merge_heads(oa), merge_heads(ob), oc, merge_heads(od)], axis=-1) @ w_out
    if not with_ctx_out:
        return out_lat, None
    oac = dense_attention(qac, kac, vac, scale64, sink=a_sink)
    obc = dense_attention(qbc, kbc, vbc, scale_b)
    occ = diff_combine(dense_attention(qcc, kcc, vcc, scale_c), c_lambda, c_subln, layer)
    odc = dense_attention(qdc, kdc, vdc, scale64)
    out_ctx = jnp.concatenate([merge_heads(oac), merge_heads(obc), occ, merge_heads(odc)], axis=-1) @ w_out
    return out_lat, out_ctx

def expert_choice_ffn(h, w_router, w_gate, w_up, w_down):
    b, n, d = h.shape
    cap = CAPACITY_FACTOR * n // N_EXPERTS
    logits = jnp.einsum('bnd,de->ben', h, w_router).astype(jnp.float32)
    affinity = jax.nn.softmax(logits, axis=1)
    gates, idx = lax.top_k(affinity, cap)
    xs = jax.vmap(lambda hb, ib: hb[ib])(h, idx)
    a = jnp.einsum('becd,edf->becf', xs, w_gate)
    u = jnp.einsum('becd,edf->becf', xs, w_up)
    y = jnp.einsum('becf,efd->becd', jax.nn.silu(a) * u, w_down) * gates[..., None].astype(h.dtype)
    return jax.vmap(lambda yb, ib: jnp.zeros((n, d), yb.dtype).at[ib.reshape(-1)].add(yb.reshape(-1, d)))(y, idx)

def setup_inputs(seed: int = 0) -> dict:
    key = jax.random.key(seed)
    ks = jax.random.split(key, 24)
    D, L = D_MODEL, DEPTH

    def nrm(i, shape, s):
        return jax.random.normal(ks[i], shape, jnp.float32) * s

    def gain(i, shape):
        return 1.0 + nrm(i, shape, 0.02)

    return {
        "x": nrm(0, (BATCH, SEQ, D), 1.0),
        "c": nrm(1, (BATCH, D), 1.0),
        "ctx": nrm(2, (BATCH, CTX_LEN, D), 1.0),
        "c_ctx": nrm(3, (D,), 1.0),
        "w_mod": nrm(4, (L, D, 6 * D), 0.5 * D ** -0.5),
        "b_mod": nrm(5, (L, 6 * D), 0.02),
        "g_attn": gain(6, (L, D)),
        "g_ffn": gain(7, (L, D)),
        "w_in": nrm(8, (L, D, IN_COLS), D ** -0.5),
        "a_sink": nrm(9, (L, A_HEADS), 0.5),
        "b_q_norm": gain(10, (L, B_Q_RANK)),
        "b_w_uq": nrm(11, (L, B_Q_RANK, B_HEADS * (B_NOPE + B_ROPE)), B_Q_RANK ** -0.5),
        "b_kv_norm": gain(12, (L, B_KV_RANK)),
        "b_w_ukv": nrm(13, (L, B_KV_RANK, B_HEADS * (B_NOPE + B_V)), B_KV_RANK ** -0.5),
        "c_lambda": nrm(14, (L, 4, C_QK), 0.1),
        "c_subln": gain(15, (L, C_V)),
        "d_q_norm": gain(16, (L, HEAD_DIM)),
        "d_k_norm": gain(17, (L, HEAD_DIM)),
        "w_out": nrm(18, (L, MIX_WIDTH, D), MIX_WIDTH ** -0.5),
        "w_router": nrm(19, (L, D, N_EXPERTS), D ** -0.5),
        "w_gate": nrm(20, (L, N_EXPERTS, D, D_EXPERT), D ** -0.5),
        "w_up": nrm(21, (L, N_EXPERTS, D, D_EXPERT), D ** -0.5),
        "w_down": nrm(22, (L, N_EXPERTS, D_EXPERT, D), D_EXPERT ** -0.5),
        "g_final": gain(23, (D,)),
    }

def reference(x, c, ctx, c_ctx, w_mod, b_mod, g_attn, g_ffn, w_in, a_sink, b_q_norm, b_w_uq,
              b_kv_norm, b_w_ukv, c_lambda, c_subln, d_q_norm, d_k_norm, w_out, w_router,
              w_gate, w_up, w_down, g_final):
    n_tokens = x.shape[1]
    rope64 = axial_rope_table(n_tokens, HEAD_DIM)
    rope32 = axial_rope_table(n_tokens, C_QK)
    xl, xc = x, ctx
    for l in range(DEPTH):
        last = l == DEPTH - 1
        sh_a, sc_a, gt_a, sh_f, sc_f, gt_f = adaln_params(c, w_mod[l], b_mod[l])
        csh_a, csc_a, cgt_a, csh_f, csc_f, cgt_f = adaln_params(c_ctx, w_mod[l], b_mod[l])
        hl = modulate(xl, g_attn[l], sh_a, sc_a)
        hc = modulate(xc, g_attn[l], csh_a, csc_a)
        out_lat, out_ctx = token_mixers(hl, hc, l, not last, w_in[l], a_sink[l], b_q_norm[l], b_w_uq[l],
                                        b_kv_norm[l], b_w_ukv[l], c_lambda[l], c_subln[l], d_q_norm[l],
                                        d_k_norm[l], w_out[l], rope64, rope32)
        xl = xl + gt_a * out_lat
        hl = modulate(xl, g_ffn[l], sh_f, sc_f)
        xl = xl + gt_f * expert_choice_ffn(hl, w_router[l], w_gate[l], w_up[l], w_down[l])
        if not last:
            xc = xc + cgt_a * out_ctx
            hc = modulate(xc, g_ffn[l], csh_f, csc_f)
            xc = xc + cgt_f * expert_choice_ffn(hc, w_router[l], w_gate[l], w_up[l], w_down[l])
    return rmsnorm(xl, g_final)


_drawn_inputs = setup_inputs


def setup_inputs(seed=0):
    import zlib

    import numpy as np

    out = dict(_drawn_inputs(seed))
    spreads = {}
    factors = {'g_attn': 8.0,
     'g_ffn': 5.832,
     'a_sink': 8.0,
     'b_q_norm': 8.0,
     'b_w_uq': 2.691,
     'b_kv_norm': 8.0,
     'c_lambda': 2.997,
     'c_subln': 8.0,
     'd_q_norm': 8.0,
     'd_k_norm': 8.0,
     'g_final': 2.905}
    for name, (base, spread) in spreads.items():
        noise = np.random.default_rng([zlib.crc32(name.encode()), seed]).standard_normal(out[name].shape)
        drawn = base * np.exp(spread * noise) if base else spread * noise
        out[name] = __import__('jax').numpy.asarray(drawn.astype(out[name].dtype))
    for name, factor in factors.items():
        out[name] = (out[name] * factor).astype(out[name].dtype)
    return out
```

```python
import math
from contextlib import ExitStack

import concourse.bass as bass
import numpy as np
from concourse import mybir

f32 = mybir.dt.float32
u32 = mybir.dt.uint32
ALU = mybir.AluOpType
ACT = mybir.ActivationFunctionType
AX = mybir.AxisListType

P = 128
D, L = 1024, 2
KD = D // P
CTX, LAT = 256, 512
TC, TL = CTX // P, LAT // P
TT = TC + TL
NTOK = CTX + LAT
EPS = 1e-6
NEG = -1e30
GRID_W = 64
HD = 64
B_NOPE, B_ROPE, B_QR, B_KVR = 64, 32, 192, 128
B_QK = B_NOPE + B_ROPE
C_QK = 32
IN_COLS = 2144
NE, FE = 16, 1024
CAP_L, CAP_C = 2 * LAT // NE, 2 * CTX // NE
QUAD = 4
NQ = NE // QUAD

SECTIONS = [("B", 512, B_QR, 352), ("A", 0, 256, 512), ("C1", 864, 256, 512),
            ("C2", 1376, 0, 256), ("D", 1632, 256, 512)]
STEPS = [(sec, t) for sec in range(len(SECTIONS)) for t in range(TT)]
NSTEP = len(STEPS)

SLOTS = 20
SCALE = [HD ** -0.5] * 4 + [B_QK ** -0.5] * 4 + [C_QK ** -0.5] * 8 + [HD ** -0.5] * 4
KTILE = [0] * 4 + [1, 2, 3, 4] + [5] * 4 + [6] * 4 + [7] * 4
LAST_SLOT = [0, 1, 2, 3, 4, 5, 6, 7, 9, 11, 13, 15, 16, 17, 18, 19]
TURNS = len(LAST_SLOT)
VCOL = [0] * 4 + [128, 128, 256, 256] + [384, 384, 512, 512] + [640] * 4
OCOL = [0, 256, 512, 768]
LAG = 2
OT_AT, OP_AT, QT_AT = (4, 5), (7, 9), (12, 14, 16)


def keys_of(t, slot):
    if t < TC:
        return list(range(TC))
    if slot < 4:
        b = t - TC
        return list(range(TC)) + [TC + j for j in range(max(b - 1, 0), min(b + 1, TL - 1) + 1)]
    return list(range(TT))


def runs_of(kt):
    runs = []
    for n, k in enumerate(kt):
        if runs and runs[-1][0] + runs[-1][2] == k * P and n % 4:
            runs[-1][2] += P
        else:
            runs.append([k * P, n * P, P])
    return runs


def attention_plan(tiles):
    n = len(tiles) * SLOTS
    ready = {i * SLOTS + s + LAG: i * TURNS + v for i in range(len(tiles)) for v, s in enumerate(LAST_SLOT)}
    plan, waiting = [], None
    for s in range(n + LAG + 2):
        v = ready.get(s)
        i, at = divmod(s, SLOTS)
        jobs = []
        if at in QT_AT and i + 1 < len(tiles):
            jobs.append(("Q", i + 1, QT_AT.index(at)))
        if i and s < n:
            if at in OT_AT:
                jobs.append(("T", i - 1, OT_AT.index(at)))
            if at in OP_AT:
                jobs.append(("O", i - 1, OP_AT.index(at)))
        mult = None
        if v is not None or s >= n:
            mult, waiting = waiting, v
        plan.append((s if s < n else None, v, mult, jobs))
    last = len(tiles) - 1
    plan.append((None, None, None, [("T", last, 0), ("T", last, 1), ("O", last, 0), ("O", last, 1)]))
    return plan


def uses_act(sec, t):
    return not (SECTIONS[sec][0] == "C1" and t >= TC)


def uses_dve(sec, t):
    name = SECTIONS[sec][0]
    return name in ("B", "D") or (name in ("A", "C1") and t >= TC)


ACT_DONE = np.cumsum([uses_act(*s) for s in STEPS])
DVE_DONE = np.cumsum([uses_dve(*s) for s in STEPS])


def k_jobs(tau):
    out = []
    if 0 <= tau < NSTEP and SECTIONS[STEPS[tau][0]][0] in ("A", "C1", "D"):
        out.append(tau)
    if 0 <= tau - 2 < TT:
        out.append(tau - 2)
    return out


K_ORDER = [j for tau in range(NSTEP + 3) for j in k_jobs(tau)]


def jobs_of_quad(with_ctx):
    out = [("S", 0), ("S", 1)] + ([("S", 2)] if with_ctx else [])
    out += [("G", k) for k in range(KD)] + [("H", f) for f in range(KD)]
    tiles = list(range(TT)) if with_ctx else list(range(TC, TT))
    out += [("C", (t, h)) for h in range(2) for t in tiles]
    return out


def stage_of(st):
    return (0, 0, 1, 1, 0, 0, 1, 1, 2, 2, 2, 2)[st], (0, 0, 0, 0, 1, 1, 1, 1, 0, 0, 1, 1)[st], st % 2


def jobs_through_values(plan, i):
    n = 3
    for _, _, _, jobs in plan:
        for j in jobs:
            n += 1
            if j == ("T", i, 1):
                return n


def backbone_program(nc, A, out):
    ctx = ExitStack()
    with ctx:
        def sb(name, cols, dt=f32, rows=P):
            return ctx.enter_context(nc.sbuf_tensor(name, [rows, cols], dt))

        def sem(name):
            return ctx.enter_context(nc.semaphore(name))

        def view(tensor, p0, n, col, *dims):
            w = tensor.shape[1]
            return bass.AP(tensor, p0 * w + col, [[w, n], *[list(d) for d in dims]])

        X = sb("X", TT * D)
        ident = sb("ident", P)
        iota = sb("iota", LAT)
        mask = sb("mask", 2 * P)
        modrow = sb("modrow", L * 3 * 512)
        modcol = sb("modcol", L * 96)
        eff = sb("eff", L * 32)
        gtb = sb("gtb", 2 * D)
        rope = sb("rope", 3 * TL * 48)
        gD = sb("gD", L * 384)
        gC = sb("gC", L * 64)
        gcol = sb("gcol", L * 16)
        bgcol = sb("bgcol", L * 3)
        sinkn = sb("sinkn", L * 4)
        sink = sb("sink", L * 8)
        lam = sb("lam", L * 8)
        wrt = sb("wrt", L * KD * NE)
        wuq = sb("wuq", 2 * 384)
        wukv = sb("wukv", 512)
        sc = sb("sc", 2 * KD)
        scm = sb("scm", KD * 32)
        ss = sb("ss", 16)
        pw = sb("pw", 24)
        mx = sb("mx", 2 * SLOTS)
        nb = sb("nb", 2 * SLOTS)
        rs = sb("rs", 2 * SLOTS)
        rr = sb("rr", 2 * SLOTS)
        esk = sb("esk", 2 * 4)
        kk = sb("kk", 8)
        LI = sb("LI", 16)
        LG = sb("LG", 16)
        AR = 36864
        ar = sb("arena", AR)

        LAMP = 22528
        M_RING = 6144
        XN, HT0, WIN, PX = 0, 17664, 23808, 32000
        JUNK, T1, T2, T0 = PX, PX + 1024, PX + 1408, PX + 1792
        T1, T2, T0 = PX + 1024, PX + 1536, PX + 2048
        KN = PX + 2560
        BN = PX + 3328
        KR = PX + 3648
        CQT, CKVT = PX + 3744, PX + 4000
        SQ = PX + 4128
        KT, VV, QN = 0, 6144, 10752
        QNW = 1152
        QN_AT = {"A": 0, "B": 256, "C1": 640, "D": 896}
        QT, WOUT, PB, PT, OS = 17664, 23808, 32000, 32000 + 3072, 22784
        RING, XN2, XST, HID, HIDT, STL, SEL = 0, 16384, 22528, 25600, 28672, 31744, 33024
        HT2, AFF, VAL, DUP, LGT, PRB = 25600, 34304, 34816, 34944, 35072, 35840
        SLOT = 2048
        idx = sb("idx", 64, u32)
        pwa, pwr = sb("pwa", 8), sb("pwr", 8)
        TMP = 36608
        tmp = ar[:, TMP:TMP + 256]

        psS = [ctx.enter_context(nc.psum_tensor(f"psS{i}", [P, 1024], f32)) for i in range(2)]
        psT = ctx.enter_context(nc.psum_tensor("psT", [P, 1024], f32))
        psO = ctx.enter_context(nc.psum_tensor("psO", [P, 512], f32))
        psM = ctx.enter_context(nc.psum_tensor("psM", [P, 512], f32))
        BANKS = [(psS[0], 0), (psS[0], 512), (psS[1], 0), (psS[1], 512), (psT, 0), (psT, 512), (psO, 0), (psM, 0)]

        def bank(b, p0=0, n=P, col=0, w=512):
            t, c = BANKS[b]
            return t[p0:p0 + n, c + col:c + col + w]

        def bankv(b, p0, n, col, *dims):
            t, c = BANKS[b]
            return view(t, p0, n, c + col, *dims)

        s_const, s_x, s_bm = sem("consts_loaded"), sem("tokens_loaded"), sem("bias_loaded")
        s_bm0 = sem("bias_cleared")
        s_mused, s_scm, s_mrow, s_mT, s_mcol = (sem(n) for n in (
            "mod_slots_used", "silu_ready", "mod_row_ready", "mod_transposed", "mod_columns_ready"))
        s_silu = sem("silu_done")
        s_dve = sem("dve_chain")
        s_pin, s_pout = sem("pow_base_ready"), sem("pow_done")
        s_lamx = sem("lambda_exponents")
        s_fin0 = sem("final_squares")
        s_out = sem("out_stored")
        s_fin = sem("final_ready")

        def sems(l, names):
            return {n: sem(f"{n}_{l}") for n in names.split()}

        Z = [sems(l, "sq xn ht htev gt gtev win0 win1 proj pact pdve dsq bsq bn bt btev bs bsa bsd kn kpe kt "
                     "S nb P mixed T PTa PTd O Og mj me fxn_sq fxn fht fhtev wused st jp ja jd silu prod y qd") for l in range(L)]
        once = {n: sem(n) for n in "wb wo qz lg lgev lt pe_ex prb at dup dupT ffn_done xready".split()}
        for z in Z:
            z.update(once)
        s_w = [sem(f"ring_slot{i}") for i in range(8)]

        block = ctx.enter_context(nc.Block())
        PLANS = [attention_plan(list(range(TT))), attention_plan(list(range(TC, TT)))]
        TILES = [list(range(TT)), list(range(TC, TT))]

        NCONST = 7 + 12 * L
        gfin = ar[:, XN:XN + D]

        @block.sync
        def _(sp):
            def load(dst, src, s, columns=False):
                sp.dma_start(dst, src, allow_slow_non_contiguous=columns).then_inc(s, 16)

            load(sc[:, 0:KD], A["c"].rearrange("b (k p) -> p (b k)", p=P), s_const, True)
            load(sc[:, KD:2 * KD], A["c_ctx"].rearrange("(k p) -> p k", p=P), s_const, True)
            load(ident[:, :], A["ident"], s_const)
            load(iota[:, :], A["iota"], s_const)
            load(mask[:, :], A["mask"], s_const)
            load(rope[:, :], A["rope"], s_const)
            load(sinkn[:, :], A["a_sink"].rearrange("l h -> (l h)").partition_broadcast(P), s_const)
            for l in range(L):
                for h in range(4):
                    load(gD[:, l * 384 + h * 64:l * 384 + h * 64 + 64], A["d_q_norm"][l, :].partition_broadcast(P), s_const)
                for h in range(2):
                    load(gD[:, l * 384 + 256 + h * 64:l * 384 + 320 + h * 64], A["d_k_norm"][l, :].partition_broadcast(P), s_const)
                load(gC[:, l * 64:l * 64 + 64], A["c_subln"][l, :].partition_broadcast(P), s_const)
                load(gcol[:, l * 16:l * 16 + 8], A["g_attn"][l, :].rearrange("(k p) -> p k", p=P), s_const, True)
                load(gcol[:, l * 16 + 8:l * 16 + 16], A["g_ffn"][l, :].rearrange("(k p) -> p k", p=P), s_const, True)
                load(bgcol[0:96, l * 3:l * 3 + 2], A["b_q_norm"][l, :].rearrange("(k p) -> p k", p=96), s_const, True)
                load(bgcol[:, l * 3 + 2:l * 3 + 3], A["b_kv_norm"][l, :].rearrange("(p k) -> p k", k=1), s_const, True)
                load(ar[:, LAMP + l * 128:LAMP + l * 128 + 128], A["c_lambda"][l].rearrange("a b -> (a b)").partition_broadcast(P), s_const)
            sp.wait_ge(s_bm0, 1)
            for j in range(4):
                for s in range(2):
                    load(view(ar, 32 * j + s, 1, PX, (1536, L), (512, 3), (1, 512)),
                         A["b_mod"].rearrange("l (r j n) -> j l r n", r=3, j=4)[j:j + 1], s_bm)

            def mod_chunk(n):
                l, r, k = n // 24, n // 8 % 3, n % 8
                if n >= 8:
                    sp.wait_ge(s_mused, n - 7)
                load(ar[:, M_RING + (n % 8) * SLOT:M_RING + (n % 8 + 1) * SLOT],
                     A["w_mod"][l, k * P:(k + 1) * P, r * 2048:(r + 1) * 2048], s_w[n % 8])

            for n in range(8):
                mod_chunk(n)
            load(X[:, 0:TC * D].rearrange("p (t d) -> p t d", t=TC), A["ctx"][0].rearrange("(t p) d -> p t d", p=P), s_x)
            load(X[:, TC * D:].rearrange("p (t d) -> p t d", t=TL), A["x"][0].rearrange("(t p) d -> p t d", p=P), s_x)
            for l in range(L):
                load(wrt[:, l * P:(l + 1) * P].rearrange("p (k e) -> p k e", k=KD),
                     A["w_router"][l].rearrange("(k p) e -> p k e", p=P), s_x)
            for n in range(8, 48):
                mod_chunk(n)

            for l in range(L):
                z = Z[l]
                if l:
                    sp.wait_ge(Z[l - 1]["ffn_done"], l)
                load(wuq[0:96, :].rearrange("p (k n) -> p k n", k=2), A["b_w_uq"][l].rearrange("(k p) n -> p k n", p=96), z["wb"])
                load(wukv[:, :], A["b_w_ukv"][l], z["wb"])
                for sec, (_, c0, _, nc_) in enumerate(SECTIONS):
                    if sec >= 2:
                        sp.wait_ge(z["proj"], (sec - 1) * TT)
                    at = WIN + sec % 2 * 4096
                    load(ar[:, at:at + KD * nc_].rearrange("p (k n) -> p k n", k=KD),
                         A["w_in"][l, :, c0:c0 + nc_].rearrange("(k p) n -> p k n", p=P), z[f"win{sec % 2}"])
                sp.wait_ge(z["proj"], NSTEP)
                load(ar[:, WOUT:WOUT + KD * D].rearrange("p (k n) -> p k n", k=KD),
                     A["w_out"][l].rearrange("(k p) n -> p k n", p=P), z["wo"])
                with sp.Fori(0, NQ) as q:
                    for st in range(12):
                        m, hf, kh = stage_of(st)
                        w = A[("w_gate", "w_up", "w_down")[m]][l]
                        sp.wait_ge(z["wused"], q * 12 + (st + 1))
                        for e in range(QUAD):
                            slot = st % 2 * QUAD + e
                            load(ar[:, RING + slot * SLOT:RING + (slot + 1) * SLOT].rearrange("p (k n) -> p k n", k=4),
                                 w[bass.ds(q * QUAD + e, 1), kh * 512:(kh + 1) * 512, hf * 512:(hf + 1) * 512]
                                 .rearrange("e (k p) n -> p (e k) n", p=P), s_w[slot])
            sp.wait_ge(Z[L - 1]["ffn_done"], L)
            load(gfin, A["g_final"].partition_broadcast(P), s_x)
            for t in range(TL):
                sp.wait_ge(s_fin, t + 1)
                load(out[0, t * P:(t + 1) * P, :], ar[:, XN2 + t * D:XN2 + (t + 1) * D], s_out)
            sp.wait_ge(s_out, 16 * TL)

        POWS = [1 + 2 * TT + len(TILES[l]) + 1 for l in range(L)]

        @block.gpsimd
        def _(pool):
            nc.gpsimd.memset(ar[:, PX:PX + L * 1536], 0.0).then_inc(s_bm0, 1)
            done = 0

            def powers(n):
                nonlocal done
                base = done
                with pool.Fori(0, n) as i:
                    pool.wait_ge(s_pin, i + (base + 1))
                    nc.gpsimd.tensor_tensor(pw[:, 8:16], pw[:, 0:8], pw[:, 16:24], ALU.pow).then_inc(s_pout, 1)
                done += n

            for l in range(L):
                z = Z[l]
                powers(1 + 2 * TT)
                pool.wait_ge(z["proj"], NSTEP)
                nc.gpsimd.memset(ar[:, QT:QT + 2 * SLOTS * P], 0.0).then_inc(z["qz"], 1)
                powers(len(TILES[l]) + 1)
            powers(1)

        @block.tensor
        def _(pe):
            def mm(o, lhsT, rhs, start=True, stop=True):
                return nc.tensor.matmul(o, lhsT, rhs, start=start, stop=stop)

            def tr(o, in_, n=P):
                return nc.tensor.transpose(o, in_, ident[0:n, 0:n])

            pe.wait_ge(s_scm, 1)
            for n in range(48):
                l, r, k = n // 24, n // 8 % 3, n % 8
                pe.wait_ge(s_w[n % 8], 16 * (n // 8 + 1))
                for j in range(4):
                    a = M_RING + (n % 8) * SLOT + j * 512
                    last = mm(bank(l * 3 + r, 32 * j, 32), scm[:, k * 32:(k + 1) * 32], ar[:, a:a + 512], k == 0, k == 7)
                last.then_inc(s_mused, 1)
            for n in range(6):
                pe.wait_ge(s_mrow, n + 1)
                if n >= 2:
                    pe.wait_ge(s_mcol, n - 1)
                for t in range(4):
                    last = tr(bank(6 + n % 2, col=t * P, w=P), modrow[:, n * 512 + t * P:n * 512 + (t + 1) * P])
                last.then_inc(s_mT, 1)

            for l in range(L):
                z = Z[l]
                def gates(sec, got, sent, b0, before=()):
                    for n in range(4):
                        s, jj = n // 2, n % 2
                        for w in before:
                            w()
                        j = 2 * (sec % 2) + jj
                        mm(bank(b0 + n), view(ident, 0, P, 32 * j + s, (0, P)),
                           modrow[:, l * 1536 + sec // 2 * 512:l * 1536 + sec // 2 * 512 + 512]).then_inc(z[sent], 1)

                if l == 0:
                    pe.wait_ge(s_mcol, 6)
                gates(2, "gtev", "gt", 4)
                for n in range(TT * 2):
                    t, g = n // 2, n % 2
                    pe.wait_ge(z["xn"], t + 1)
                    if n >= 4:
                        pe.wait_ge(z["htev"], n - 3)
                    for c in range(4):
                        a = XN + t * D + (4 * g + c) * P
                        last = tr(bank(n % 4, col=c * P, w=P), ar[:, a:a + P])
                    last.then_inc(z["ht"], 1)
                pe.wait_ge(z["htev"], TT * 2)
                pe.wait_ge(z["gtev"], 4)
                for tau in range(NSTEP + 4):
                    if tau < NSTEP:
                        sec, t = STEPS[tau]
                        _, _, nq, ncol = SECTIONS[sec]
                        skip = nq if (l == L - 1 and t < TC) else 0
                        if t == 0:
                            pe.wait_ge(z[f"win{sec % 2}"], 16 * (sec // 2 + 1))
                        if tau >= 3:
                            if ACT_DONE[tau - 3]:
                                pe.wait_ge(z["pact"], int(ACT_DONE[tau - 3]))
                            if DVE_DONE[tau - 3]:
                                pe.wait_ge(z["pdve"], int(DVE_DONE[tau - 3]))
                        for k in range(KD):
                            a = WIN + sec % 2 * 4096 + k * ncol
                            h = HT0 + k * NTOK + t * P
                            last = mm(bank(tau % 3, col=skip, w=ncol - skip), ar[:, h:h + P], ar[:, a + skip:a + ncol],
                                      k == 0, k == KD - 1)
                        last.then_inc(z["proj"], 1)
                    b = tau - 1
                    if 0 <= b < TT:
                        pe.wait_ge(z["bn"], b + 1)
                        if b:
                            pe.wait_ge(z["btev"], b)
                        noq = l == L - 1 and b < TC
                        if not noq:
                            for j in range(2):
                                tr(bank(5, 0, 96, j * P, P), ar[:, BN + 96 * j:BN + 96 * (j + 1)])
                        tr(bank(5, col=256, w=P), ar[:, BN + 192:BN + 320]).then_inc(z["bt"], 1)
                    b = tau - 2
                    if 0 <= b < TT:
                        pe.wait_ge(z["btev"], b + 1)
                        if b:
                            pe.wait_ge(z["bsa"], b)
                            pe.wait_ge(z["bsd"], b)
                        else:
                            pe.wait_ge(z["wb"], 32 * (l + 1))
                        noq = l == L - 1 and b < TC
                        if not noq:
                            for j in range(2):
                                mm(bank(6, w=384), ar[0:96, CQT + j * P:CQT + (j + 1) * P], wuq[0:96, j * 384:(j + 1) * 384],
                                   j == 0, j == 1)
                        mm(bank(7), ar[:, CKVT:CKVT + P], wukv[:, :]).then_inc(z["bs"], 1)
                    for i in k_jobs(tau - 1):
                        n = K_ORDER.index(i)
                        name = SECTIONS[STEPS[i][0]][0]
                        pe.wait_ge(z["kn"], n + 1)
                        if n >= 2:
                            pe.wait_ge(z["kt"], n - 1)
                        kb = KN + n % 2 * 384
                        if name == "B":
                            for h in range(4):
                                last = tr(bank(3 + n % 2, 0, 96, h * P, P), ar[:, kb + h * 96:kb + (h + 1) * 96])
                        else:
                            for h in range(2 if name == "C1" else 1):
                                last = tr(bank(3 + n % 2, col=h * P, w=P), ar[:, kb + h * P:kb + (h + 1) * P])
                        last.then_inc(z["kpe"], 1)
                tiles, mj = TILES[l], 0

                def job(kind, i, r):
                    nonlocal mj
                    t = tiles[i]
                    if mj:
                        pe.wait_ge(z["me"], mj)
                    else:
                        pe.wait_ge(z["bsd"], TT)
                        pe.wait_ge(z["bsa"], TT)
                    qn = QN + t * QNW
                    if kind == "Q":
                        blocks = [[("A", 0, P), ("A", P, P), ("C1", 0, P), ("C1", P, P)],
                                  [("B", 96 * h, 96) for h in range(4)], [("D", 0, P), ("D", P, P)]][r]
                        for c, (name, a, w) in enumerate(blocks):
                            a += qn + QN_AT[name]
                            last = tr(bank(7, 0, w, c * P, P), ar[:, a:a + w])
                    elif kind == "T":
                        pe.wait_ge(z["Og"], 4 * (i + 1))
                        for c in range(4):
                            a = OS + (4 * r + c) * P
                            last = tr(bank(7, col=c * P, w=P), ar[:, a:a + P])
                    else:
                        if i == 0 and r == 0:
                            pe.wait_ge(z["wo"], 16 * (l + 1))
                        for k in range(KD):
                            a = WOUT + k * D + r * 512
                            last = mm(bank(7), ar[:, qn + k * P:qn + (k + 1) * P], ar[:, a:a + 512], k == 0, k == KD - 1)
                    last.then_inc(z["mj"], 1)
                    mj += 1

                pe.wait_ge(z["kt"], len(K_ORDER))
                pe.wait_ge(z["pact"], int(ACT_DONE[-1]))
                pe.wait_ge(z["pdve"], int(DVE_DONE[-1]))
                for r in range(3):
                    job("Q", 0, r)
                for s, v, pv, jobs in PLANS[l]:
                    if s is not None:
                        i, slot = divmod(s, SLOTS)
                        if slot == 0:
                            pe.wait_ge(z["me"], 3 if i == 0 else 7 * i - 1)
                        if s >= 2:
                            pe.wait_ge(z["P"], s - 1)
                        rows = 96 if 4 <= slot < 8 else P
                        qa = QT + i % 2 * SLOTS * P + slot * P
                        for k0, c0, n in runs_of(keys_of(tiles[i], slot)):
                            a = KT + KTILE[slot] * NTOK + k0
                            last = mm(psS[s % 2][:, c0:c0 + n], ar[0:rows, qa:qa + P], ar[0:rows, a:a + n])
                        last.then_inc(z["S"], 1)
                    if v is not None:
                        i, u = divmod(v, TURNS)
                        s0 = i * SLOTS + LAST_SLOT[u]
                        pe.wait_ge(z["P"], s0 + 1)
                        if 8 <= u < 12:
                            pe.wait_ge(z["mixed"], 4 * i + u - 7)
                            s0 -= 1
                        if v:
                            pe.wait_ge(z["PTa"], v)
                            pe.wait_ge(z["PTd"], v)
                        for n, _ in enumerate(keys_of(tiles[i], LAST_SLOT[u])):
                            a = PB + s0 % 4 * NTOK + n * P
                            last = tr(psT[:, n * P:(n + 1) * P], ar[:, a:a + P])
                        last.then_inc(z["T"], 1)
                    if pv is not None:
                        i, u = divmod(pv, TURNS)
                        pe.wait_ge(z["PTa"], pv + 1)
                        pe.wait_ge(z["PTd"], pv + 1)
                        if u % 4 == 0 and pv:
                            pe.wait_ge(z["Og"], i * 4 + u // 4)
                        kt = keys_of(tiles[i], LAST_SLOT[u])
                        for n, k in enumerate(kt):
                            a, b = PT + pv % 2 * NTOK + n * P, VV + k * 768 + VCOL[u]
                            last = mm(psO[:, u % 4 * P:(u % 4 + 1) * P], ar[:, a:a + P], ar[:, b:b + P], n == 0, n == len(kt) - 1)
                        last.then_inc(z["O"], 1)
                    for j in jobs:
                        job(*j)
                pe.wait_ge(z["me"], mj)
                pe.sem_inc(z["wused"], 2)

                gates(5, "", "fht", 0)
                pe.wait_ge(z["fhtev"], 4)
                tl = TILES[l]
                for n in range(len(tl) * 2):
                    t, g = tl[n // 2], n % 2
                    pe.wait_ge(z["fxn"], n // 2 + 1)
                    if n >= 4:
                        pe.wait_ge(z["fhtev"], n + 1)
                    for c in range(4):
                        a = XN2 + t * D + (4 * g + c) * P
                        last = tr(bank(n % 4, col=c * P, w=P), ar[:, a:a + P])
                    last.then_inc(z["fht"], 1)
                pe.wait_ge(z["fhtev"], 4 + 2 * len(tl))
                streams = [0, 1] if l == 0 else [0]
                for s in streams:
                    c0, n = ((CTX, LAT), (0, CTX))[s]
                    for k in range(KD):
                        last = mm(bank(s, 0, NE, 0, n), wrt[:, l * P + k * NE:l * P + (k + 1) * NE],
                                  ar[:, HT2 + k * NTOK + c0:HT2 + k * NTOK + c0 + n], k == 0, k == KD - 1)
                last.then_inc(z["lg"], 1)
                pe.wait_ge(z["lgev"], l + 1)
                for t in tl:
                    last = tr(bank(2, col=t * NE, w=NE), ar[0:NE, LGT + t * P:LGT + (t + 1) * P], NE)
                last.then_inc(z["lt"], 1)
                pe.wait_ge(z["prb"], l + 1)
                for t in tl:
                    o = bank(3, 0, NE, (t - TC) * P, P) if t >= TC else bank(4, 0, NE, t * P, P)
                    last = tr(o, ar[:, PRB + t * NE:PRB + (t + 1) * NE])
                last.then_inc(z["at"], 1)
                for n in range(2):
                    pe.wait_ge(z["dup"], 2 * l + n + 1)
                    tr(bank(5 + n, 0, P, 0, 48), ar[0:48, DUP + n * P:DUP + n * P + P], 48).then_inc(z["dupT"], 1)

                wc = l == 0
                JL = jobs_of_quad(wc)
                NJ = len(JL)
                GW = 384 if wc else 256
                with pe.Fori(0, NQ) as q:
                    pe.wait_ge(z["qd"], q + 1)
                    pe.wait_ge(z["st"], q + 1)
                    nact = sum(k == "G" for k, _ in JL)
                    ndve = NJ - nact

                    def before(n):
                        if n >= 2:
                            m = n - 2
                            if JL[m][0] == "G":
                                pe.wait_ge(z["ja"], q * nact + sum(k == "G" for k, _ in JL[:m + 1]))
                            else:
                                pe.wait_ge(z["jd"], q * ndve + sum(k != "G" for k, _ in JL[:m + 1]))

                    def small(n):
                        kind, x = JL[n]
                        before(n)
                        b = 6 + n % 2
                        if kind == "S":
                            if x < 2:
                                for c in range(2):
                                    for pr in range(2):
                                        a = STL + pr * LAT + (2 * x + c) * P
                                        last = tr(bank(b, col=c * 256 + pr * P, w=P), ar[:, a:a + P])
                            else:
                                for c in range(TC):
                                    a = STL + 2 * LAT + c * P
                                    last = tr(bank(b, col=c * P, w=P), ar[:, a:a + P])
                        elif kind == "G":
                            if x == 0:
                                pe.wait_ge(z["jd"], q * ndve + (3 if wc else 2))
                            for c in range(TL):
                                a, r = XN2 + (TC + c) * D + x * P, SEL + c * 256
                                last = mm(bank(b, w=256), ar[:, a:a + P], ar[:, r:r + 256], c == 0, c == TL - 1)
                            if wc:
                                for c in range(TC):
                                    a, r = XN2 + c * D + x * P, SEL + TL * 256 + c * P
                                    last = mm(bank(b, col=256, w=P), ar[:, a:a + P], ar[:, r:r + P], c == 0, c == TC - 1)
                        elif kind == "H":
                            for i in range(3 if wc else 2):
                                a = HID + i * D + x * P
                                last = tr(bank(b, col=i * P, w=P), ar[:, a:a + P])
                        else:
                            t, hf = x
                            if t >= TC:
                                for pr in range(2):
                                    a, r = STL + pr * LAT + (t - TC) * P, HID + pr * D + hf * 512
                                    last = mm(bank(b), ar[:, a:a + P], ar[:, r:r + 512], pr == 0, pr == 1)
                            else:
                                a, r = STL + 2 * LAT + t * P, HID + 2 * D + hf * 512
                                last = mm(bank(b), ar[:, a:a + P], ar[:, r:r + 512])
                        last.then_inc(z["jp"], 1)

                    def big(st):
                        m, hf, kh = stage_of(st)
                        b0 = 3 * (hf if m == 2 else m)
                        src = HIDT if m == 2 else XST
                        for pr in range(2):
                            for e in (2 * pr, 2 * pr + 1):
                                pe.wait_ge(s_w[st % 2 * QUAD + e], q * 96 + (96 + 384 * l + 16 * (st // 2 + 1)))
                            for k, e in ((k, 2 * pr + j) for k in range(4) for j in range(2)):
                                slot = st % 2 * QUAD + e
                                a = src + (kh * 4 + k) * 384 + e * CAP_L
                                r = RING + slot * SLOT + k * 512
                                last = mm(bank(b0 + e // 2, 64 * (e % 2), 64), ar[:, a:a + CAP_L], ar[:, r:r + 512],
                                          kh == 0 and k == 0, kh == 1 and k == 3)
                        if wc:
                            for k in range(4):
                                for e in range(QUAD):
                                    a = src + (kh * 4 + k) * 384 + 256 + e * CAP_C
                                    r = RING + (st % 2 * QUAD + e) * SLOT + k * 512
                                    last = mm(bank(b0 + 2, 32 * e, 32), ar[:, a:a + CAP_C], ar[:, r:r + 512],
                                              kh == 0 and k == 0, kh == 1 and k == 3)
                        last.then_inc(z["wused"], 1)

                    n = 0
                    while JL[n][0] in "SG":
                        small(n)
                        n += 1
                    pe.wait_ge(z["ja"], q * nact + nact)
                    for hf in range(2):
                        if hf:
                            pe.wait_ge(z["silu"], q * 2 + 1)
                        big(hf * 4)
                        big(hf * 4 + 1)
                        if hf:
                            pe.wait_ge(z["prod"], q * 2 + 1)
                            for _ in range(4):
                                small(n)
                                n += 1
                        big(hf * 4 + 2)
                        big(hf * 4 + 3)
                    nh = sum(k in "S" for k, _ in JL)
                    pe.wait_ge(z["silu"], q * 2 + 2)
                    pe.wait_ge(z["jd"], q * ndve + nh + 4)
                    big(8)
                    pe.wait_ge(z["prod"], q * 2 + 2)
                    for _ in range(4):
                        small(n)
                        n += 1
                    pe.wait_ge(z["jd"], q * ndve + nh + 8)
                    big(9)
                    big(10)
                    big(11)
                    half = (NJ - n) // 2
                    pe.wait_ge(z["y"], q * 2 + 1)
                    for _ in range(half):
                        small(n)
                        n += 1
                    pe.wait_ge(z["y"], q * 2 + 2)
                    for _ in range(half):
                        small(n)
                        n += 1
                pe.wait_ge(z["xready"], l + 1)
                pe.sem_inc(z["ffn_done"], 1)

        @block.scalar
        def _(act):
            def a_(o, i, f=ACT.Copy, **kw):
                return nc.scalar.activation(o, i, f, **kw)

            act.wait_ge(s_const, 16 * NCONST)
            a_(sc[:, :], sc[:, :], ACT.Silu).then_inc(s_silu, 1)
            act.wait_ge(s_lamx, 1)
            for l in range(L):
                a_(lam[:, l * 8 + 2:l * 8 + 4], lam[:, l * 8:l * 8 + 2], ACT.Exp).then_inc(s_lamx, 1)

            for l in range(L):
                z = Z[l]
                if l == 0:
                    act.wait_ge(s_x, 16 * 4)
                else:
                    act.wait_ge(Z[l - 1]["ffn_done"], l)
                act.wait_ge(s_mrow, 6)
                for t in range(TT):
                    if t:
                        act.wait_ge(z["sq"], t)
                    a_(ar[:, JUNK:JUNK + D], X[:, t * D:(t + 1) * D], ACT.Square, accum_out=ss[:, t:t + 1]).then_inc(z["sq"], 1)
                for n in range(TT * 2):
                    t, g = n // 2, n % 2
                    if n == 0:
                        act.wait_ge(s_mcol, 7)
                    act.wait_ge(z["ht"], n + 1)
                    s = 0 if t >= TC else 1
                    for c in range(4):
                        k = 4 * g + c
                        h = HT0 + k * NTOK + t * P
                        last = a_(ar[:, h:h + P], bank(n % 4, col=c * P, w=P), ACT.Identity,
                                  scale=eff[:, l * 32 + s * 8 + k:l * 32 + s * 8 + k + 1],
                                  bias=modcol[:, l * 96 + s * 8 + k:l * 96 + s * 8 + k + 1])
                    last.then_inc(z["htev"], 1)
                for tau in range(NSTEP + 4):
                    if tau < NSTEP and uses_act(*STEPS[tau]):
                        sec, t = STEPS[tau]
                        name = SECTIONS[sec][0]
                        b = tau % 3
                        noq = l == L - 1 and t < TC
                        act.wait_ge(z["proj"], tau + 1)
                        v = VV + t * 768
                        if name == "B":
                            if t:
                                act.wait_ge(z["bsq"], 2 * t if l == 0 else 2 * t - min(t, TC))
                            if not noq:
                                a_(ar[:, JUNK:JUNK + B_QR], bank(b, w=B_QR), ACT.Square, accum_out=ss[:, 6:7]).then_inc(z["bsq"], 1)
                            a_(ar[:, JUNK + 256:JUNK + 384], bank(b, col=B_QR, w=B_KVR), ACT.Square,
                               accum_out=ss[:, 7:8]).then_inc(z["bsq"], 1)
                            act.wait_ge(z["pdve"], t + 1)
                            act.sem_inc(z["pact"], 1)
                        elif name == "A":
                            last = a_(ar[:, v:v + P], bank(b, col=384, w=P))
                            if t < TC:
                                n = K_ORDER.index(tau)
                                act.wait_ge(z["kpe"], n - 1)
                                if not noq:
                                    a_(view(ar, 0, P, QN + t * QNW + QN_AT["A"], (64, 2), (128, 2), (1, 64)),
                                       bankv(b, 0, P, 0, (128, 2), (64, 2), (1, 64)))
                                last = a_(ar[:, KN + n % 2 * 384:KN + n % 2 * 384 + P], bank(b, col=256, w=P))
                            last.then_inc(z["pact"], 1)
                            if t < TC:
                                act.wait_ge(z["pact"], int(ACT_DONE[tau]))
                                act.wait_ge(z["kn"], n)
                                act.sem_inc(z["kn"], 1)
                        elif name == "C1":
                            n = K_ORDER.index(tau)
                            act.wait_ge(z["kpe"], n - 1)
                            if not noq:
                                a_(ar[:, QN + t * QNW + QN_AT["C1"]:QN + t * QNW + QN_AT["C1"] + 256], bank(b, w=256))
                            a_(ar[:, KN + n % 2 * 384:KN + n % 2 * 384 + 256], bank(b, col=256, w=256)).then_inc(z["pact"], 1)
                            act.wait_ge(z["pact"], int(ACT_DONE[tau]))
                            act.wait_ge(z["kn"], n)
                            act.sem_inc(z["kn"], 1)
                        elif name == "C2":
                            a_(ar[:, v + 384:v + 640], bank(b, w=256)).then_inc(z["pact"], 1)
                        else:
                            a_(ar[:, v + 640:v + 768], bank(b, col=384, w=P))
                            q0 = 256 if noq else 0
                            if t:
                                act.wait_ge(z["dsq"], 2 * t)
                            a_(ar[:, SQ + q0:SQ + 384], bank(b, col=q0, w=384 - q0), ACT.Square).then_inc(z["dsq"], 1)
                            act.wait_ge(z["dsq"], 2 * t + 1)
                            act.sem_inc(z["pact"], 1)
                    b = tau - 1
                    if 0 <= b < TT:
                        act.wait_ge(z["bt"], b + 1)
                        if b:
                            act.wait_ge(z["bs"], b)
                        if not (l == L - 1 and b < TC):
                            for j in range(2):
                                a_(ar[0:96, CQT + j * P:CQT + (j + 1) * P], bank(5, 0, 96, j * P, P), ACT.Identity,
                                   scale=bgcol[0:96, l * 3 + j:l * 3 + j + 1])
                        a_(ar[:, CKVT:CKVT + P], bank(5, col=256, w=P), ACT.Identity,
                           scale=bgcol[:, l * 3 + 2:l * 3 + 3]).then_inc(z["btev"], 1)
                    b = tau - 2
                    if 0 <= b < TT:
                        n = K_ORDER.index(b)
                        act.wait_ge(z["bs"], b + 1)
                        if n >= 2:
                            act.wait_ge(z["kpe"], n - 1)
                        a_(view(ar, 0, P, KN + n % 2 * 384, (96, 4), (1, 64)), bankv(7, 0, P, 0, (128, 4), (1, 64)))
                        a_(view(ar, 0, P, VV + b * 768 + 128, (64, 4), (1, 64)), bankv(7, 0, P, 64, (128, 4), (1, 64))).then_inc(z["bsa"], 1)
                    for i in k_jobs(tau - 1):
                        n = K_ORDER.index(i)
                        sec, t = STEPS[i]
                        name = SECTIONS[sec][0]
                        kb = 3 + n % 2
                        act.wait_ge(z["kpe"], n + 1)
                        if name == "B":
                            last = a_(view(ar, 0, 96, KT + NTOK + t * P, (NTOK, 4), (1, P)), bankv(kb, 0, 96, 0, (P, 4), (1, P)))
                        elif name == "C1":
                            last = a_(view(ar, 0, P, KT + 5 * NTOK + t * P, (NTOK, 2), (1, P)), bankv(kb, 0, P, 0, (P, 2), (1, P)))
                        else:
                            k0 = KT + (0 if name == "A" else 7) * NTOK + t * P
                            last = a_(ar[:, k0:k0 + P], bank(kb, w=P))
                        last.then_inc(z["kt"], 1)
                tiles = TILES[l]
                for s, v, pv, jobs in PLANS[l]:
                    if v is not None:
                        i, u = divmod(v, TURNS)
                        act.wait_ge(z["T"], v + 1)
                        if v >= 2:
                            act.wait_ge(z["O"], v - 1)
                        w = min(len(keys_of(tiles[i], LAST_SLOT[u])), 4) * P
                        a = PT + v % 2 * NTOK
                        a_(ar[:, a:a + w], psT[:, 0:w]).then_inc(z["PTa"], 1)
                    if s is not None:
                        i, slot = divmod(s, SLOTS)
                        par = i % 2 * SLOTS + slot
                        act.wait_ge(z["nb"], s + 1)
                        if s >= 4:
                            i4, s4 = divmod(s - 4, SLOTS)
                            u4 = next(u for u, x in enumerate(LAST_SLOT) if x >= s4)
                            act.wait_ge(z["T"], i4 * TURNS + u4 + 1)
                        n = len(keys_of(tiles[i], slot)) * P
                        a = PB + s % 4 * NTOK
                        if slot < 4:
                            a_(esk[:, i % 2 * 4 + slot:i % 2 * 4 + slot + 1], sink[:, l * 8 + slot:l * 8 + slot + 1], ACT.Exp,
                               bias=nb[:, par:par + 1])
                        a_(ar[:, a:a + n], psS[s % 2][:, 0:n], ACT.Exp, bias=nb[:, par:par + 1], scale=SCALE[slot],
                           accum_out=rs[:, par:par + 1]).then_inc(z["P"], 1)
                tl = TILES[l]
                for n, t in enumerate(tl):
                    act.wait_ge(z["me"], 7 * len(tl))
                    if n:
                        act.wait_ge(z["fxn_sq"], n)
                    a_(ar[:, PRB:PRB + D], X[:, t * D:(t + 1) * D], ACT.Square,
                       accum_out=ss[:, t:t + 1]).then_inc(z["fxn_sq"], 1)
                for n in range(4):
                    act.wait_ge(z["fht"], n + 1)
                    a_(gtb[:, n * 512:(n + 1) * 512], bank(n)).then_inc(z["fhtev"], 1)
                for n in range(len(tl) * 2):
                    t, g = tl[n // 2], n % 2
                    act.wait_ge(z["fht"], 4 + n + 1)
                    s = 0 if t >= TC else 1
                    for c in range(4):
                        k = 4 * g + c
                        h = HT2 + k * NTOK + t * P
                        last = a_(ar[:, h:h + P], bank(n % 4, col=c * P, w=P), ACT.Identity,
                                  scale=eff[:, l * 32 + 16 + s * 8 + k:l * 32 + 16 + s * 8 + k + 1],
                                  bias=modcol[:, l * 96 + 48 + s * 8 + k:l * 96 + 48 + s * 8 + k + 1])
                    last.then_inc(z["fhtev"], 1)
                act.wait_ge(z["pe_ex"], 2 * l + 1)
                c0 = tl[0] * NE
                a_(ar[:, PRB + c0:PRB + TT * NE], ar[:, PRB + c0:PRB + TT * NE], ACT.Exp).then_inc(z["pe_ex"], 1)
                wc = l == 0
                JL = jobs_of_quad(wc)
                NJ = len(JL)
                nS = 3 if wc else 2
                with act.Fori(0, NQ) as q:
                    for x in range(KD):
                        act.wait_ge(z["jp"], q * NJ + (nS + x + 1))
                        b = 6 + (nS + x) % 2
                        a = XST + x * 384
                        k = l * 32 + 16 + x
                        m = l * 96 + 48 + x
                        if wc:
                            a_(ar[:, a + 256:a + 384], bank(b, col=256, w=P), ACT.Identity, scale=eff[:, k + 8:k + 9],
                               bias=modcol[:, m + 8:m + 9])
                        a_(ar[:, a:a + 256], bank(b, w=256), ACT.Identity, scale=eff[:, k:k + 1],
                           bias=modcol[:, m:m + 1]).then_inc(z["ja"], 1)
                    for hf in range(2):
                        act.wait_ge(z["wused"], q * 12 + (4 + 4 * hf))
                        for i in range(3 if wc else 2):
                            a = HID + i * D + hf * 512
                            last = a_(ar[:, a:a + 512], bank(i), ACT.Silu)
                        last.then_inc(z["silu"], 1)
            for t in range(TL):
                act.wait_ge(Z[L - 1]["ffn_done"], L)
                if t:
                    act.wait_ge(s_fin0, t)
                a_(ar[:, HID:HID + D], X[:, (TC + t) * D:(TC + t + 1) * D], ACT.Square, accum_out=ss[:, t:t + 1]).then_inc(s_fin0, 1)

        @block.vector
        def _(dve):
            chain = [0]
            powers = [0]
            V = nc.vector

            def link(ins):
                chain[0] += 1
                ins.then_inc(s_dve, 1)
                dve.wait_ge(s_dve, chain[0])

            def rsqrt(sums, n, count):
                link(V.tensor_scalar(pw[:, 0:n], sums, 1.0 / count, EPS, ALU.mult, ALU.add))
                powers[0] += 1
                dve.sem_inc(s_pin, 1)
                dve.wait_ge(s_pout, powers[0])
                link(V.tensor_tensor(pwa[:, 0:n], pw[:, 0:n], pw[:, 8:8 + n], ALU.mult))
                link(V.scalar_tensor_tensor(pwa[:, 0:n], pwa[:, 0:n], -0.5, pw[:, 8:8 + n], ALU.mult, ALU.mult))
                link(V.scalar_tensor_tensor(pwr[:, 0:n], pwa[:, 0:n], 1.5, pw[:, 8:8 + n], ALU.add, ALU.mult))

            link(V.memset(pw[:, 0:16], 1.0))
            link(V.memset(pw[:, 16:24], -0.5))
            link(V.memset(scm[:, :], 0.0))
            dve.wait_ge(s_silu, 1)
            V.tensor_copy(view(scm, 0, P, 0, (1, 2), (32, KD)), view(sc, 0, P, 0, (KD, 2), (1, KD))).then_inc(s_scm, 1)
            for l in range(L):
                for j in range(2):
                    link(V.tensor_tensor(view(ar, 0, P, LAMP + l * 128 + 64 * j, (1, 32)), view(ar, 0, P, LAMP + l * 128 + 64 * j, (1, 32)),
                                         view(ar, 0, P, LAMP + l * 128 + 64 * j + 32, (1, 32)), ALU.mult))
                    link(V.reduce_sum(lam[:, l * 8 + j:l * 8 + j + 1], ar[:, LAMP + l * 128 + 64 * j:LAMP + l * 128 + 64 * j + 32], axis=AX.X))
            dve.sem_inc(s_lamx, 1)
            dve.wait_ge(s_lamx, 1 + L)
            for l in range(L):
                init = 0.8 - 0.6 * math.exp(-0.3 * l)
                link(V.tensor_tensor(lam[:, l * 8 + 4:l * 8 + 5], lam[:, l * 8 + 3:l * 8 + 4], lam[:, l * 8 + 2:l * 8 + 3], ALU.subtract))
                link(V.tensor_scalar(lam[:, l * 8 + 5:l * 8 + 6], lam[:, l * 8 + 4:l * 8 + 5], -init, None, ALU.add))
                link(V.tensor_scalar(gC[:, l * 64:l * 64 + 64], gC[:, l * 64:l * 64 + 64], 1 - init, None, ALU.mult))
                link(V.tensor_copy(view(sink, 0, P, l * 8, (2, 2), (1, 2)), view(sinkn, 0, P, l * 4, (1, 2), (2, 2))))
                link(V.tensor_scalar(sink[:, l * 8 + 4:l * 8 + 8], sink[:, l * 8:l * 8 + 4], -1.0, None, ALU.mult))

            dve.wait_ge(s_bm, 16 * 8)
            for n in range(6):
                dve.wait_ge(s_mused, 8 * (n + 1))
                V.tensor_tensor(modrow[:, n * 512:(n + 1) * 512], bank(n), ar[:, PX + n * 512:PX + (n + 1) * 512],
                                ALU.add).then_inc(s_mrow, 1)
            for n in range(6):
                l, r = n // 3, n % 3
                dve.wait_ge(s_mT, n + 1)
                for s in range(2):
                    last = V.tensor_copy(view(modcol, 0, P, l * 96 + 2 * r * 16 + s * 8, (16, 2), (4, 2), (1, 4)),
                                         bankv(6 + n % 2, 0, P, s, (64, 2), (32, 2), (P, 4)))
                last.then_inc(s_mcol, 1)
            dve.wait_ge(s_mcol, 6)
            for l in range(L):
                for f in range(2):
                    last = V.scalar_tensor_tensor(view(eff, 0, P, l * 32 + f * 16, (8, 2), (1, 8)),
                                                  view(modcol, 0, P, l * 96 + (1 + 3 * f) * 16, (8, 2), (1, 8)), 1.0,
                                                  view(gcol, 0, P, l * 16 + f * 8, (0, 2), (1, 8)), ALU.add, ALU.mult)
            last.then_inc(s_mcol, 1)

            def rot(src, srcw, half, heads, lt):
                c = lt * 48 + (0 if half == 32 else 32)
                w = TL * 48
                V.tensor_tensor(view(ar, 0, P, T1, (2 * half, heads), (half, 2), (1, half)),
                                src(0, (2 * half, heads), (half, 2), (1, half)),
                                view(rope, 0, P, c, (0, heads), (0, 2), (1, half)), ALU.mult)
                V.tensor_tensor(view(ar, 0, P, T2, (2 * half, heads), (1, half)), src(half, (2 * half, heads), (1, half)),
                                view(rope, 0, P, 2 * w + c, (0, heads), (1, half)), ALU.mult)
                link(V.tensor_tensor(view(ar, 0, P, T2 + half, (2 * half, heads), (1, half)), src(0, (2 * half, heads), (1, half)),
                                     view(rope, 0, P, w + c, (0, heads), (1, half)), ALU.mult))

            for l in range(L):
                z = Z[l]
                dve.wait_ge(z["sq"], TT)
                rsqrt(ss[:, 0:TT], TT, D)
                for t in range(TT):
                    V.tensor_scalar(ar[:, XN + t * D:XN + (t + 1) * D], X[:, t * D:(t + 1) * D], pwr[:, t:t + 1], None,
                                    ALU.mult).then_inc(z["xn"], 1)
                for n in range(4):
                    dve.wait_ge(z["gt"], n + 1)
                    V.tensor_copy(gtb[:, n * 512:(n + 1) * 512], bank(4 + n)).then_inc(z["gtev"], 1)
                dve.wait_ge(z["ht"], 2 * TT)
                for tau in range(NSTEP + 4):
                    if tau < NSTEP and uses_dve(*STEPS[tau]):
                        sec, t = STEPS[tau]
                        name = SECTIONS[sec][0]
                        b, lt = tau % 3, t - TC
                        noq = l == L - 1 and t < TC
                        dve.wait_ge(z["proj"], tau + 1)
                        if name == "A":
                            dve.wait_ge(z["pact"], int(ACT_DONE[tau]))

                        def src(col, *dims, b=b):
                            return bankv(b, 0, P, col, *dims)

                        if name == "B":
                            dve.wait_ge(z["bsq"], 2 * (t + 1) if l == 0 else 2 * (t + 1) - min(t + 1, TC))
                            if not noq:
                                link(V.tensor_scalar(ss[:, 8:9], ss[:, 6:7], B_KVR / B_QR, None, ALU.mult))
                            else:
                                link(V.tensor_copy(ss[:, 8:9], ss[:, 7:8]))
                            link(V.tensor_copy(ss[:, 9:10], ss[:, 7:8]))
                            rsqrt(ss[:, 8:10], 2, B_KVR)
                            if t:
                                dve.wait_ge(z["bt"], t)
                            if not noq:
                                link(V.tensor_scalar(ar[:, BN:BN + B_QR], bank(b, w=B_QR), pwr[:, 0:1], None, ALU.mult))
                            link(V.tensor_scalar(ar[:, BN + B_QR:BN + 320], bank(b, col=B_QR, w=B_KVR), pwr[:, 1:2], None, ALU.mult))
                            dve.sem_inc(z["bn"], 1)
                            kr = KR + t % 3 * 32
                            if t >= TC:
                                rot(lambda col, *dims: src(320 + col, *dims), 0, 16, 1, lt)
                                link(V.tensor_tensor(ar[:, kr:kr + 32], ar[:, T1:T1 + 32], ar[:, T2:T2 + 32], ALU.add))
                            else:
                                link(V.tensor_copy(ar[:, kr:kr + 32], bank(b, col=320, w=32)))
                            dve.sem_inc(z["pdve"], 1)
                        else:
                            heads, half = (16, 16) if name == "C1" else (6, 32)
                            nk = 256 if name == "C1" else 128
                            n = K_ORDER.index(tau)
                            kb = KN + n % 2 * 384
                            if name == "D":
                                q0 = 256 if noq else 0
                                hq = q0 // 64
                                dve.wait_ge(z["dsq"], 2 * t + 1)
                                if noq:
                                    link(V.memset(ss[:, 10:14], 64.0))
                                link(V.tensor_reduce(ss[:, 10 + hq:16], view(ar, 0, P, SQ + q0, (64, 6 - hq), (1, 64)), AX.X, ALU.add))
                                dve.sem_inc(z["dsq"], 1)
                                rsqrt(ss[:, 10:16], 6, HD)
                                link(V.tensor_tensor(ar[:, T0 + q0:T0 + 384], bank(b, col=q0, w=384 - q0),
                                                     gD[:, l * 384 + q0:l * 384 + 384], ALU.mult))
                                link(V.tensor_tensor(view(ar, 0, P, T0 + q0, (64, 6 - hq), (1, 64)), view(ar, 0, P, T0 + q0, (64, 6 - hq), (1, 64)),
                                                     view(pwr, 0, P, hq, (1, 6 - hq), (0, 64)), ALU.mult))

                                def src(col, *dims):
                                    return view(ar, 0, P, T0 + col, *dims)

                            if t >= TC:
                                rot(src, 0, half, heads, lt)
                                in0, in1 = (lambda c, *d: view(ar, 0, P, T1 + c, *d)), (lambda c, *d: view(ar, 0, P, T2 + c, *d))
                            if n >= 2:
                                dve.wait_ge(z["kpe"], n - 1)
                            qa = QN + t * QNW + QN_AT[name]
                            if name == "C1":
                                qv, iv = (view(ar, 0, P, qa, (1, 256)), (0, (1, 256)))
                            else:
                                qv, iv = (view(ar, 0, P, qa, (64, 2), (128, 2), (1, 64)), (0, (128, 2), (64, 2), (1, 64)))
                            if t >= TC:
                                link(V.tensor_tensor(qv, in0(*iv), in1(*iv), ALU.add))
                                link(V.tensor_tensor(ar[:, kb:kb + nk], in0(256, (1, nk)), in1(256, (1, nk)), ALU.add))
                            else:
                                if not noq:
                                    link(V.tensor_copy(qv, src(*iv)))
                                link(V.tensor_copy(ar[:, kb:kb + nk], src(256, (1, nk))))
                            dve.sem_inc(z["pdve"], 1)
                            if n:
                                dve.wait_ge(z["kn"], n)
                            dve.sem_inc(z["kn"], 1)
                    b = tau - 2
                    if 0 <= b < TT:
                        n = K_ORDER.index(b)
                        noq = l == L - 1 and b < TC
                        dve.wait_ge(z["bs"], b + 1)
                        qa = QN + b * QNW + QN_AT["B"] + 64
                        if not noq:
                            link(V.tensor_copy(view(ar, 0, P, qa - 64, (96, 4), (1, 64)), bankv(6, 0, P, 0, (96, 4), (1, 64))))
                        if b >= TC:
                            rot(lambda col, *dims: bankv(6, 0, P, 64 + col, (96, 4), *dims[1:]), 0, 16, 4, b - TC)
                            link(V.tensor_tensor(view(ar, 0, P, qa, (96, 4), (1, 32)), view(ar, 0, P, T1, (32, 4), (1, 32)),
                                                 view(ar, 0, P, T2, (32, 4), (1, 32)), ALU.add))
                        elif not noq:
                            link(V.tensor_copy(view(ar, 0, P, qa, (96, 4), (1, 32)), bankv(6, 0, P, 64, (96, 4), (1, 32))))
                        if n >= 2:
                            dve.wait_ge(z["kpe"], n - 1)
                        link(V.tensor_copy(view(ar, 0, P, KN + n % 2 * 384 + 64, (96, 4), (1, 32)),
                                           view(ar, 0, P, KR + b % 3 * 32, (0, 4), (1, 32))))
                        dve.sem_inc(z["bsd"], 1)
                        dve.wait_ge(z["bsa"], b + 1)
                        if n:
                            dve.wait_ge(z["kn"], n)
                        dve.sem_inc(z["kn"], 1)
                tiles, mj = TILES[l], 0
                dve.wait_ge(z["qz"], l + 1)

                def job(kind, i, r):
                    nonlocal mj
                    t = tiles[i]
                    dve.wait_ge(z["mj"], mj + 1)
                    qt = QT + i % 2 * SLOTS * P
                    if kind == "Q":
                        if r == 1:
                            last = V.tensor_copy(ar[0:96, qt + 4 * P:qt + 8 * P], bank(7, 0, 96, 0, 512))
                        else:
                            s0 = 0 if r == 0 else 16
                            for j in range(2):
                                last = V.tensor_copy(view(ar, 64 * j, 64, qt + (s0 + j) * P, (2 * P, 2), (1, P)),
                                                     bankv(7, 64 * j, 64, 0, (P, 2), (1, P)))
                            if r == 0:
                                for j in range(4):
                                    last = V.tensor_copy(view(ar, 32 * j, 32, qt + (8 + j) * P, (4 * P, 2), (1, P)),
                                                         bankv(7, 32 * j, 32, 256, (P, 2), (1, P)))
                        last.then_inc(z["me"], 1)
                    elif kind == "T":
                        a = QN + t * QNW + 4 * r * P
                        V.tensor_copy(ar[:, a:a + 512], bank(7)).then_inc(z["me"], 1)
                    else:
                        g = (0 if t >= TC else 1) * D + r * 512
                        link(V.tensor_tensor(bank(7), bank(7), gtb[:, g:g + 512], ALU.mult))
                        x = t * D + r * 512
                        V.tensor_tensor(X[:, x:x + 512], X[:, x:x + 512], bank(7), ALU.add).then_inc(z["me"], 1)
                    mj += 1

                for r in range(3):
                    job("Q", 0, r)
                for s, v, pv, jobs in PLANS[l]:
                    if v is not None and 8 <= v % TURNS < 12:
                        i, u = divmod(v, TURNS)
                        s1 = i * SLOTS + LAST_SLOT[u]
                        p1 = i % 2 * SLOTS + LAST_SLOT[u]
                        dve.wait_ge(z["P"], s1 + 1)
                        link(V.reciprocal(rr[:, p1:p1 + 1], rs[:, p1:p1 + 1]))
                        link(V.scalar_tensor_tensor(kk[:, 0:1], rr[:, p1:p1 + 1], lam[:, l * 8 + 5:l * 8 + 6], rs[:, p1 - 1:p1],
                                                    ALU.mult, ALU.mult))
                        n = len(keys_of(tiles[i], 8)) * P
                        a, b = PB + (s1 - 1) % 4 * NTOK, PB + s1 % 4 * NTOK
                        V.scalar_tensor_tensor(ar[:, a:a + n], ar[:, b:b + n], kk[:, 0:1], ar[:, a:a + n],
                                               ALU.mult, ALU.add).then_inc(z["mixed"], 1)
                    if s is not None:
                        i, slot = divmod(s, SLOTS)
                        par = i % 2 * SLOTS + slot
                        kt = keys_of(tiles[i], slot)
                        n = len(kt) * P
                        S = psS[s % 2]
                        dve.wait_ge(z["S"], s + 1)
                        if slot < 4 and tiles[i] >= TC:
                            b = tiles[i] - TC
                            if b > 0:
                                link(V.tensor_tensor(S[:, 256:384], S[:, 256:384], mask[:, 0:P], ALU.add))
                            if b < TL - 1:
                                link(V.tensor_tensor(S[:, n - P:n], S[:, n - P:n], mask[:, P:2 * P], ALU.add))
                        link(V.reduce_max(mx[:, par:par + 1], S[:, 0:n], axis=AX.X))
                        if slot < 4:
                            V.tensor_scalar(nb[:, par:par + 1], mx[:, par:par + 1], -SCALE[slot], sink[:, l * 8 + 4 + slot:l * 8 + 5 + slot],
                                            ALU.mult, ALU.min).then_inc(z["nb"], 1)
                        else:
                            V.tensor_scalar(nb[:, par:par + 1], mx[:, par:par + 1], -SCALE[slot], None, ALU.mult).then_inc(z["nb"], 1)
                    if v is not None:
                        i, u = divmod(v, TURNS)
                        dve.wait_ge(z["T"], v + 1)
                        if v >= 2:
                            dve.wait_ge(z["O"], v - 1)
                        w = len(keys_of(tiles[i], LAST_SLOT[u])) * P
                        a = PT + v % 2 * NTOK
                        if w > 512:
                            V.tensor_copy(ar[:, a + 512:a + w], psT[:, 512:w]).then_inc(z["PTd"], 1)
                        else:
                            dve.sem_inc(z["PTd"], 1)
                    if pv is not None and pv % 4 == 3:
                        i, u = divmod(pv, TURNS)
                        g = u // 4
                        p0 = i % 2 * SLOTS
                        dve.wait_ge(z["O"], pv + 1)
                        if g == 0 and i:
                            dve.wait_ge(z["mj"], jobs_through_values(PLANS[l], i - 1))
                        if g == 0:
                            link(V.tensor_tensor(rs[:, p0:p0 + 4], rs[:, p0:p0 + 4], esk[:, i % 2 * 4:i % 2 * 4 + 4], ALU.add))
                        if g == 2:
                            link(V.reciprocal(view(rr, 0, P, p0 + 8, (2, 4)), view(rs, 0, P, p0 + 8, (2, 4))))
                            rv = view(rr, 0, P, p0 + 8, (4, 2), (2, 2), (0, 64))
                        else:
                            r0 = p0 + (0, 4, 8, 16)[g]
                            link(V.reciprocal(rr[:, r0:r0 + 4], rs[:, r0:r0 + 4]))
                            rv = view(rr, 0, P, r0, (2, 2), (1, 2), (0, 64))
                        o = OS + OCOL[g]
                        ov = (view(ar, 0, P, o, (64, 2), (128, 2), (1, 64)) if g in (0, 3)
                              else view(ar, 0, P, o, (128, 2), (64, 2), (1, 64)))
                        ins = V.tensor_tensor(ov, bankv(6, 0, P, 0, (256, 2), (192, 2), (1, 64)), rv, ALU.mult)
                        if g == 2:
                            link(ins)
                            link(V.tensor_tensor(tmp[:, 0:256], ar[:, o:o + 256], ar[:, o:o + 256], ALU.mult))
                            link(V.tensor_reduce(ss[:, 8:12], view(ar, 0, P, TMP, (64, 4), (1, 64)), AX.X, ALU.add))
                            rsqrt(ss[:, 8:12], 4, HD)
                            link(V.tensor_tensor(view(ar, 0, P, o, (64, 4), (1, 64)), view(ar, 0, P, o, (64, 4), (1, 64)),
                                                 view(pwr, 0, P, 0, (1, 4), (0, 64)), ALU.mult))
                            ins = V.tensor_tensor(view(ar, 0, P, o, (64, 4), (1, 64)), view(ar, 0, P, o, (64, 4), (1, 64)),
                                                  view(gC, 0, P, l * 64, (0, 4), (1, 64)), ALU.mult)
                        ins.then_inc(z["Og"], 1)
                    for j in jobs:
                        job(*j)
                tl = TILES[l]
                t0 = tl[0]
                dve.wait_ge(z["fxn_sq"], len(tl))
                rsqrt(ss[:, t0:TT], len(tl), D)
                for n, t in enumerate(tl):
                    V.tensor_scalar(ar[:, XN2 + t * D:XN2 + (t + 1) * D], X[:, t * D:(t + 1) * D], pwr[:, n:n + 1], None,
                                    ALU.mult).then_inc(z["fxn"], 1)
                dve.wait_ge(z["lg"], l + 1)
                if l == 0:
                    V.tensor_copy(ar[0:NE, LGT:LGT + CTX], bank(1, 0, NE, 0, CTX))
                V.tensor_copy(ar[0:NE, LGT + CTX:LGT + NTOK], bank(0, 0, NE, 0, LAT)).then_inc(z["lgev"], 1)
                dve.wait_ge(z["lt"], l + 1)
                nt = len(tl)

                def pv3(a):
                    return view(ar, 0, P, a + t0 * NE, (NE, nt), (1, NE))

                def bc3(c):
                    return view(ar, 0, P, TMP + c, (1, nt), (0, NE))

                lt_ = bankv(2, 0, P, t0 * NE, (NE, nt), (1, NE))
                link(V.tensor_reduce(tmp[:, 0:nt], lt_, AX.X, ALU.max))
                link(V.tensor_tensor(pv3(PRB), lt_, bc3(0), ALU.subtract))
                dve.sem_inc(z["pe_ex"], 1)
                dve.wait_ge(z["pe_ex"], 2 * l + 2)
                link(V.tensor_reduce(tmp[:, 8:8 + nt], pv3(PRB), AX.X, ALU.add))
                link(V.reciprocal(tmp[:, 16:16 + nt], tmp[:, 8:8 + nt]))
                V.tensor_tensor(pv3(PRB), pv3(PRB), bc3(16), ALU.mult).then_inc(z["prb"], 1)
                link(V.memset(ar[0:48, AFF:AFF + LAT], -1.0))
                link(V.memset(ar[0:48, DUP:DUP + 2 * P], 0.0))
                dve.wait_ge(z["at"], l + 1)
                link(V.tensor_copy(ar[0:NE, AFF:AFF + LAT], bank(3, 0, NE, 0, LAT)))
                if l == 0:
                    link(V.tensor_copy(ar[32:48, AFF:AFF + CTX], bank(4, 0, NE, 0, CTX)))
                for r in range(CAP_L // 8):
                    v8 = ar[0:48, VAL + 8 * r:VAL + 8 * r + 8]
                    link(V.max(v8, ar[0:48, AFF:AFF + LAT]))
                    link(V.max_index(idx[0:48, 8 * r:8 * r + 8], v8, ar[0:48, AFF:AFF + LAT]))
                    if r < CAP_L // 8 - 1:
                        link(V.match_replace(ar[0:48, AFF:AFF + LAT], v8, ar[0:48, AFF:AFF + LAT], -2.0))
                for n in range(2):
                    o = DUP + n * P
                    srcs = [idx[0:NE, :], idx[32:48, :]] if n == 0 else [ar[0:NE, VAL:VAL + 64], ar[32:48, VAL:VAL + 64]]
                    for j in range(2):
                        link(V.tensor_copy(ar[0:NE, o + 64 * j:o + 64 * j + 64], srcs[0]))
                    if l == 0:
                        for j in range(4):
                            link(V.tensor_copy(ar[32:48, o + 32 * j:o + 32 * j + 32], srcs[1][:, 0:32]))
                    dve.sem_inc(z["dup"], 1)
                for n, dst in enumerate((LI, LG)):
                    dve.wait_ge(z["dupT"], 2 * l + n + 1)
                    for j in range(2):
                        link(V.tensor_copy(view(dst, 64 * j, 64, 0, (1, 8)), bankv(5 + n, 64 * j, 64, j, (2, 8))))
                    if l == 0:
                        for j in range(4):
                            link(V.tensor_copy(view(dst, 32 * j, 32, 8, (1, 4)), bankv(5 + n, 32 * j, 32, 32 + j, (4, 4))))
                dve.wait_ge(s_dve, chain[0])
                dve.sem_inc(z["qd"], 1)
                wc = l == 0
                JL = jobs_of_quad(wc)
                NJ = len(JL)
                with dve.Fori(0, NQ) as q:
                    for pr in range(2):
                        last = V.tensor_scalar(ar[:, STL + pr * LAT:STL + (pr + 1) * LAT], iota[:, :],
                                               LI[:, bass.ds(q * 2 + pr, 1)], None, ALU.is_equal)
                    if wc:
                        last = V.tensor_scalar(ar[:, STL + 2 * LAT:STL + 2 * LAT + CTX], iota[:, 0:CTX],
                                               LI[:, bass.ds(q + 8, 1)], None, ALU.is_equal)
                    last.then_inc(z["st"], 1)

                    def small(n):
                        kind, x = JL[n]
                        b = 6 + n % 2
                        dve.wait_ge(z["jp"], q * NJ + (n + 1))
                        if kind == "S":
                            if x < 2:
                                ins = V.tensor_copy(ar[:, SEL + x * 512:SEL + (x + 1) * 512], bank(b))
                            else:
                                ins = V.tensor_copy(ar[:, SEL + 1024:SEL + 1280], bank(b, w=256))
                        elif kind == "H":
                            w = 384 if wc else 256
                            ins = V.tensor_copy(ar[:, HIDT + x * 384:HIDT + x * 384 + w], bank(b, w=w))
                        else:
                            t, hf = x
                            a = t * D + hf * 512
                            ins = V.tensor_tensor(X[:, a:a + 512], X[:, a:a + 512], bank(b), ALU.add)
                        ins.then_inc(z["jd"], 1)

                    n = 0
                    while JL[n][0] == "S":
                        small(n)
                        n += 1
                    while JL[n][0] == "G":
                        n += 1
                    for hf in range(2):
                        dve.wait_ge(z["wused"], q * 12 + (6 + 4 * hf))
                        dve.wait_ge(z["silu"], q * 2 + (hf + 1))
                        for i in range(3 if wc else 2):
                            a = HID + i * D + hf * 512
                            last = V.tensor_tensor(ar[:, a:a + 512], ar[:, a:a + 512], bank(3 + i), ALU.mult)
                        last.then_inc(z["prod"], 1)
                        for _ in range(4):
                            small(n)
                            n += 1
                    for hf in range(2):
                        dve.wait_ge(z["wused"], q * 12 + (12 + 2 * hf))
                        for i in range(3 if wc else 2):
                            a = HID + i * D + hf * 512
                            g = (D if i == 2 else 0) + hf * 512
                            col = q + 8 if i == 2 else q * 2 + i
                            last = V.scalar_tensor_tensor(ar[:, a:a + 512], bank(3 * hf + i), LG[:, bass.ds(col, 1)],
                                                          gtb[:, g:g + 512], ALU.mult, ALU.mult)
                        last.then_inc(z["y"], 1)
                    while n < NJ:
                        small(n)
                        n += 1
                    ndve = sum(k != "G" for k, _ in JL)
                    dve.wait_ge(z["jd"], q * ndve + ndve)
                    dve.sem_inc(z["qd"], 1)
                dve.wait_ge(z["jd"], NQ * sum(k != "G" for k, _ in JL))
                dve.sem_inc(z["xready"], 1)
            dve.wait_ge(s_fin0, TL)
            rsqrt(ss[:, 0:TL], TL, D)
            dve.wait_ge(s_x, 16 * 5)
            for t in range(TL):
                V.scalar_tensor_tensor(ar[:, XN2 + t * D:XN2 + (t + 1) * D], X[:, (TC + t) * D:(TC + t + 1) * D],
                                       pwr[:, t:t + 1], gfin, ALU.mult, ALU.mult).then_inc(s_fin, 1)


INPUTS = ["x", "c", "ctx", "c_ctx", "w_mod", "b_mod", "g_attn", "g_ffn", "w_in", "a_sink", "b_q_norm", "b_w_uq", "b_kv_norm",
          "b_w_ukv", "c_lambda", "c_subln", "d_q_norm", "d_k_norm", "w_out", "w_router", "w_gate", "w_up", "w_down", "g_final"]


def shape_constants():
    col = np.arange(P)
    before = np.where(col[None, :] >= col[:, None], 0.0, NEG)
    after = np.where(col[None, :] <= col[:, None], 0.0, NEG)
    n = np.arange(LAT)
    tables = []
    for dim in (HD, B_ROPE):
        quarter = dim // 4
        inv = (np.float32(10000.0) ** (-np.arange(quarter, dtype=np.float32) / np.float32(quarter))).astype(np.float32)
        ang = np.concatenate([(n // GRID_W)[:, None].astype(np.float32) * inv, (n % GRID_W)[:, None].astype(np.float32) * inv], 1)
        tables.append(ang.astype(np.float64))
    ang = np.concatenate(tables, 1)
    rope = np.stack([np.cos(ang), np.sin(ang), -np.sin(ang)])
    rope = rope.reshape(3, TL, P, 48).transpose(2, 0, 1, 3).reshape(P, 3 * TL * 48)
    return {
        "ident": np.eye(P, dtype=np.float32),
        "iota": np.broadcast_to(np.arange(LAT, dtype=np.float32), (P, LAT)).copy(),
        "mask": np.concatenate([before, after], 1).astype(np.float32),
        "rope": rope.astype(np.float32),
    }


def kernel(**inputs):
    import numpy as _np
    import concourse.bacc as _bacc
    from concourse import mybir as _mybir
    from concourse.bass_utils import run_bass_kernel_spmd as _run

    nc = _bacc.Bacc("TRN2", target_bir_lowering=False, num_devices=1)
    given = {name: _np.ascontiguousarray(inputs[name]) for name in INPUTS}
    given.update(shape_constants())
    arrays, aps = {}, {}
    for name, a in given.items():
        arrays[f"in_{name}"] = a
        aps[name] = nc.dram_tensor(f"in_{name}", a.shape, _mybir.dt.from_np(a.dtype), kind="ExternalInput").ap()
    out = nc.dram_tensor("out_0", (1, LAT, D), _mybir.dt.float32, kind="ExternalOutput").ap()
    backbone_program(nc, aps, out)
    r = _run(nc, [arrays], core_ids=[0])
    return r.results[0]["out_0"]
```

```python
import math
from contextlib import ExitStack

import concourse.bass as bass
import numpy as np
from concourse import mybir

f32 = mybir.dt.float32
u32 = mybir.dt.uint32
ALU = mybir.AluOpType
ACT = mybir.ActivationFunctionType
AX = mybir.AxisListType

P = 128
D, L = 1024, 2
KD = D // P
CTX, LAT = 256, 512
TC, TL = CTX // P, LAT // P
TT = TC + TL
NTOK = CTX + LAT
EPS = 1e-6
NEG = -1e30
GRID_W = 64
HD = 64
B_NOPE, B_ROPE, B_QR, B_KVR = 64, 32, 192, 128
B_QK = B_NOPE + B_ROPE
C_QK = 32
IN_COLS = 2144
NE, FE = 16, 1024
CAP_L, CAP_C = 2 * LAT // NE, 2 * CTX // NE
QUAD = 4
NQ = NE // QUAD

SECTIONS = [("B", 512, B_QR, 352), ("A", 0, 256, 512), ("C2", 1376, 0, 256), ("C1", 864, 256, 512),
            ("D", 1632, 256, 512)]
STEPS = [(sec, t) for sec in range(len(SECTIONS)) for t in range(TT)]
NSTEP = len(STEPS)

SLOTS = 20
SCALE = [HD ** -0.5] * 4 + [B_QK ** -0.5] * 4 + [C_QK ** -0.5] * 8 + [HD ** -0.5] * 4
KTILE = [0] * 4 + [1, 2, 3, 4] + [5] * 4 + [6] * 4 + [7] * 4
LAST_SLOT = [0, 1, 2, 3, 4, 5, 6, 7, 9, 11, 13, 15, 16, 17, 18, 19]
TURNS = len(LAST_SLOT)
VCOL = [0] * 4 + [128, 128, 256, 256] + [384, 384, 512, 512] + [640] * 4
LAG = 3
OT_AT, OP_AT, QT_AT = (3,), (5, 8), (12, 14, 16)


def keys_of(t, slot):
    if t < TC:
        return list(range(TC))
    if slot < 4:
        b = t - TC
        return list(range(TC)) + [TC + j for j in range(max(b - 1, 0), min(b + 1, TL - 1) + 1)]
    return list(range(TT))


def runs_of(kt):
    runs = []
    for n, k in enumerate(kt):
        if runs and runs[-1][0] + runs[-1][2] == k * P and n % 4:
            runs[-1][2] += P
        else:
            runs.append([k * P, n * P, P])
    return runs


def attention_plan(tiles):
    n = len(tiles) * SLOTS
    ready = {i * SLOTS + s + LAG: i * TURNS + v for i in range(len(tiles)) for v, s in enumerate(LAST_SLOT)}
    plan, waiting = [], None
    for s in range(n + LAG + 2):
        v = ready.get(s)
        i, at = divmod(s, SLOTS)
        jobs = []
        if at in QT_AT and i + 1 < len(tiles):
            jobs.append(("Q", i + 1, QT_AT.index(at)))
        if i and s < n:
            if at in OT_AT:
                jobs.append(("T", i - 1, OT_AT.index(at)))
            if at in OP_AT:
                jobs.append(("O", i - 1, OP_AT.index(at)))
        mult = None
        if v is not None or s >= n:
            mult, waiting = waiting, v
        plan.append((s if s < n else None, v, mult, jobs, ready.get(s + 1)))
    last = len(tiles) - 1
    plan.append((None, None, None, [("T", last, 0), ("O", last, 0), ("O", last, 1)], None))
    return plan


def uses_act(sec, t):
    return not (SECTIONS[sec][0] == "C1" and t >= TC)


def uses_dve(sec, t):
    name = SECTIONS[sec][0]
    return name in ("B", "D") or (name in ("A", "C1") and t >= TC)


ACT_DONE = np.cumsum([uses_act(*s) for s in STEPS])
DVE_DONE = np.cumsum([uses_dve(*s) for s in STEPS])


def k_jobs(tau):
    out = []
    if 0 <= tau < NSTEP and SECTIONS[STEPS[tau][0]][0] in ("A", "C1", "D"):
        out.append(tau)
    if 0 <= tau - 2 < TT:
        out.append(tau - 2)
    return out


MOD_CHUNKS = [(l, r, k) for l in range(L) for r in range(3) for k in range(KD)]
MOD_AT = {(3 * g + i // 4, 2 * (i % 4) + 1): KD + g * KD + i for g in range(3 * L - 1) for i in range(KD)}
MOD_STEP = {n: at for at, n in MOD_AT.items()}
MOD_T_AT = {3 * g + 2: g + 1 for g in range(3 * L - 1)}
MOD_ADD_AT = {3 * g + 1: g + 1 for g in range(3 * L - 1)}
MOD_SLOTS = 3

K_ORDER = [j for tau in range(NSTEP + 3) for j in k_jobs(tau)]


def jobs_of_quad(with_ctx):
    tiles = list(range(TT)) if with_ctx else list(range(TC, TT))
    out = [("H", f) for f in range(KD)] + [("G", k) for k in range(KD)]
    return out + [("C", (t, h)) for h in range(2) for t in tiles]


def stage_of(st):
    return (0, 0, 1, 1, 0, 0, 1, 1, 2, 2, 2, 2)[st], (0, 0, 0, 0, 1, 1, 1, 1, 0, 0, 1, 1)[st], st % 2


def jobs_through_values(plan, i):
    n = 3
    for _, _, _, jobs, _ in plan:
        for j in jobs:
            n += 1
            if j == ("T", i, 0):
                return n


def backbone_program(nc, A, out):
    ctx = ExitStack()
    with ctx:
        def sb(name, cols, dt=f32, rows=P):
            return ctx.enter_context(nc.sbuf_tensor(name, [rows, cols], dt))

        def sem(name):
            return ctx.enter_context(nc.semaphore(name))

        def view(tensor, p0, n, col, *dims):
            w = tensor.shape[1]
            return bass.AP(tensor, p0 * w + col, [[w, n], *[list(d) for d in dims]])

        X = sb("X", TT * D)
        ident = sb("ident", P)
        iota = sb("iota", LAT)
        mask = sb("mask", 2 * P)
        modrow = sb("modrow", L * 3 * 512)
        modcol = sb("modcol", L * 96)
        eff = sb("eff", L * 32)
        gtb = sb("gtb", 2 * D)
        rope = sb("rope", 3 * TL * 48)
        gD = sb("gD", L * 384)
        gC = sb("gC", L * 64)
        gcol = sb("gcol", L * 16)
        bgcol = sb("bgcol", L * 3)
        sinkn = sb("sinkn", L * 4)
        sink = sb("sink", L * 8)
        lam = sb("lam", L * 8)
        wrt = sb("wrt", L * KD * NE)
        wuq = sb("wuq", 2 * 384)
        wukv = sb("wukv", 512)
        sc = sb("sc", 2 * KD)
        scm = sb("scm", KD * 32)
        ss = sb("ss", 16)
        pw = sb("pw", 24)
        mx = sb("mx", 2 * SLOTS)
        nb = sb("nb", 2 * SLOTS)
        rs = sb("rs", 2 * SLOTS)
        rr = sb("rr", 2 * SLOTS)
        esk = sb("esk", 2 * 4)
        kk = sb("kk", 8)
        LI = sb("LI", 16)
        LG = sb("LG", 16)
        AR = 36864
        ar = sb("arena", AR)

        LAMP = 22528
        M_RING = 6144
        FIN, FJ = 4096, 2048
        XN, HT0, WIN, PX = 0, 17664, 23808, 32000
        JUNK, T1, T2, T0 = PX, PX + 1024, PX + 1408, PX + 1792
        T1, T2, T0 = PX + 1024, PX + 1536, PX + 2048
        KN = PX + 2560
        BN = PX + 3328
        KR = PX + 3648
        CQT, CKVT = PX + 3744, PX + 4000
        SQ = PX + 4128
        KT, VV, QN = 0, 6144, 10752
        QNW = 1152
        MS1, MS2 = QN + 640, 5 * NTOK
        QN_AT = {"A": 0, "B": 256, "C1": 640, "D": 896}
        QT, WOUT, PB, OS = 17664, 23808, 32000, 22784
        PT = (32000 + 3072, 32000 + 3840, OS + 256)
        RING, SLOT = 0, 2048
        SW = (384, 256)
        RSTAGES = (2, 3)

        def places(l):
            at, p = RSTAGES[l] * QUAD * SLOT, {}
            for name, cols in (("XST", KD * SW[l]), ("HID", SW[l] // P * D), ("HIDT", KD * SW[l]), ("XG", SW[l] // P * D),
                               ("STL", 2 * LAT + (CTX if l == 0 else 0))):
                p[name] = at
                at += cols
            assert at <= 36864
            at = RSTAGES[l] * QUAD * SLOT
            n = NTOK if l == 0 else LAT
            for name, cols in (("XN2", n * KD), ("HT2", n * KD), ("AFF", LAT), ("VAL", 64), ("DUP", 2 * P), ("LGT", NTOK),
                               ("PRB", TT * NE)):
                p[name] = at
                at += cols
            assert at <= TMP
            p["n"], p["t0"] = n, (0 if l == 0 else TC)
            return p

        idx = sb("idx", 64, u32)
        LIU = sb("LIU", 12, u32)
        pwa, pwr = sb("pwa", 8), sb("pwr", 8)
        TMP = 36608
        tmp = ar[:, TMP:TMP + 256]

        psS = [ctx.enter_context(nc.psum_tensor(f"psS{i}", [P, 1024], f32)) for i in range(2)]
        psT = ctx.enter_context(nc.psum_tensor("psT", [P, 1024], f32))
        psO = ctx.enter_context(nc.psum_tensor("psO", [P, 512], f32))
        psM = ctx.enter_context(nc.psum_tensor("psM", [P, 512], f32))
        BANKS = [(psS[0], 0), (psS[0], 512), (psS[1], 0), (psS[1], 512), (psT, 0), (psT, 512), (psO, 0), (psM, 0)]

        def bank(b, p0=0, n=P, col=0, w=512):
            t, c = BANKS[b]
            return t[p0:p0 + n, c + col:c + col + w]

        def bankv(b, p0, n, col, *dims):
            t, c = BANKS[b]
            return view(t, p0, n, c + col, *dims)

        s_const, s_x, s_bm = sem("consts_loaded"), sem("tokens_loaded"), sem("bias_loaded")
        s_bm0 = sem("bias_cleared")
        s_mused, s_scm, s_mrow, s_mT, s_mcol = (sem(n) for n in (
            "mod_slots_used", "silu_ready", "mod_row_ready", "mod_transposed", "mod_columns_ready"))
        s_silu = sem("silu_done")
        s_dve = sem("dve_chain")
        s_pin, s_pout = sem("pow_base_ready"), sem("pow_done")
        s_eff = sem("gains_ready")
        s_lamx = sem("lambda_exponents")
        s_fin0 = sem("final_squares")
        s_out = sem("out_stored")
        s_fin = sem("final_ready")

        s_xd = sem("rows_stored")

        def sems(l, names):
            return {n: sem(f"{n}_{l}") for n in names.split()}

        Z = [sems(l, "sq xn ht htev htevd gt gtev win0 win1 proj pact pdve dsq bsq bn bt btev bs bsa bsd kn kpe kt "
                     "S nb P Cn mixed T PTa PTd O Og mj me fxn_sq fxn fht fhtev wused st jp ja jd silu prod y qd xg want gt0") for l in range(L)]
        once = {n: sem(n) for n in "wb wo qz lg lgev lt pe_ex prb at dup dupT ffn_done xready".split()}
        for z in Z:
            z.update(once)
        s_w = [sem(f"ring_slot{i}") for i in range(12)]

        def slot_filled(l, q, st, e):
            n = RSTAGES[l]
            base = 96 + 384 * l if st % n < 2 else 0
            return s_w[st % n * QUAD + e], q * (16 * 12 // n) + (base + 16 * (st // n + 1))

        block = ctx.enter_context(nc.Block())
        PLANS = [attention_plan(list(range(TT))), attention_plan(list(range(TC, TT)))]
        TILES = [list(range(TT)), list(range(TC, TT))]

        NCONST = 7 + 12 * L
        rows = nc.dram_tensor("normed_rows", (NTOK, D), f32).ap()
        FP = [places(l) for l in range(L)]
        gfin = ar[:, XN:XN + D]

        @block.sync
        def _(sp):
            def load(dst, src, s, columns=False):
                sp.dma_start(dst, src, allow_slow_non_contiguous=columns).then_inc(s, 16)

            load(X[:, 0:TC * D].rearrange("p (t d) -> p t d", t=TC), A["ctx"][0].rearrange("(t p) d -> p t d", p=P), s_x)
            load(X[:, TC * D:].rearrange("p (t d) -> p t d", t=TL), A["x"][0].rearrange("(t p) d -> p t d", p=P), s_x)
            load(sc[:, 0:KD], A["c"].rearrange("b (k p) -> p (b k)", p=P), s_const, True)
            load(sc[:, KD:2 * KD], A["c_ctx"].rearrange("(k p) -> p k", p=P), s_const, True)
            load(ident[:, :], A["ident"], s_const)
            load(iota[:, :], A["iota"], s_const)
            load(mask[:, :], A["mask"], s_const)
            load(rope[:, :], A["rope"], s_const)
            load(sinkn[:, :], A["a_sink"].rearrange("l h -> (l h)").partition_broadcast(P), s_const)
            for l in range(L):
                for h in range(4):
                    load(gD[:, l * 384 + h * 64:l * 384 + h * 64 + 64], A["d_q_norm"][l, :].partition_broadcast(P), s_const)
                for h in range(2):
                    load(gD[:, l * 384 + 256 + h * 64:l * 384 + 320 + h * 64], A["d_k_norm"][l, :].partition_broadcast(P), s_const)
                load(gC[:, l * 64:l * 64 + 64], A["c_subln"][l, :].partition_broadcast(P), s_const)
                load(gcol[:, l * 16:l * 16 + 8], A["g_attn"][l, :].rearrange("(k p) -> p k", p=P), s_const, True)
                load(gcol[:, l * 16 + 8:l * 16 + 16], A["g_ffn"][l, :].rearrange("(k p) -> p k", p=P), s_const, True)
                load(bgcol[0:96, l * 3:l * 3 + 2], A["b_q_norm"][l, :].rearrange("(k p) -> p k", p=96), s_const, True)
                load(bgcol[:, l * 3 + 2:l * 3 + 3], A["b_kv_norm"][l, :].rearrange("(p k) -> p k", k=1), s_const, True)
                load(ar[:, LAMP + l * 128:LAMP + l * 128 + 128], A["c_lambda"][l].rearrange("a b -> (a b)").partition_broadcast(P), s_const)

            def mod_chunk(n):
                l, r, k = MOD_CHUNKS[n]
                w = A["w_mod"][l, k * P:(k + 1) * P, r * 2048:(r + 1) * 2048]
                if n < KD:
                    load(ar[:, M_RING + n * SLOT:M_RING + (n + 1) * SLOT], w, s_w[n])
                    return
                i = (n - KD) % MOD_SLOTS
                if n - KD >= MOD_SLOTS:
                    sp.wait_ge(s_mused, n - MOD_SLOTS + 1)
                elif i == 0:
                    sp.wait_ge(s_mused, 1)
                else:
                    sp.wait_ge(s_mused, KD) if i == 1 else sp.wait_ge(Z[0]["ht"], 2 * TT)
                if i == 0:
                    load(gtb[:, :], w, s_w[n % 8])
                elif i == 1:
                    load(view(ar, 0, P, MS1, (QNW, 4), (1, 512)), w.rearrange("p (j n) -> p j n", j=4), s_w[n % 8])
                else:
                    load(ar[:, MS2:MS2 + SLOT], w, s_w[n % 8])

            for n in range(KD):
                mod_chunk(n)
            sp.wait_ge(s_bm0, 1)
            for j in range(4):
                for s in range(2):
                    load(view(modrow, 32 * j + s, 1, 0, (1536, L), (512, 3), (1, 512)),
                         A["b_mod"].rearrange("l (r j n) -> j l r n", r=3, j=4)[j:j + 1], s_bm)
            mod_next = [KD]
            for l in range(L):
                z = Z[l]
                if l:
                    sp.wait_ge(Z[l - 1]["ffn_done"], l)
                load(wuq[0:96, :].rearrange("p (k n) -> p k n", k=2), A["b_w_uq"][l].rearrange("(k p) n -> p k n", p=96), z["wb"])
                load(wukv[:, :], A["b_w_ukv"][l], z["wb"])
                for sec, (_, c0, _, nc_) in enumerate(SECTIONS):
                    while l == 0 and mod_next[0] < len(MOD_CHUNKS):
                        n = mod_next[0]
                        if sec < 2 or (n - MOD_SLOTS >= KD and MOD_STEP[n - MOD_SLOTS][0] >= (sec - 1) * TT):
                            break
                        mod_chunk(n)
                        mod_next[0] += 1
                    if sec >= 2:
                        sp.wait_ge(z["proj"], (sec - 1) * TT)
                    at = WIN + sec % 2 * 4096
                    load(ar[:, at:at + KD * nc_].rearrange("p (k n) -> p k n", k=KD),
                         A["w_in"][l, :, c0:c0 + nc_].rearrange("(k p) n -> p k n", p=P), z[f"win{sec % 2}"])
                if l == 0:
                    assert mod_next[0] == len(MOD_CHUNKS)
                    for k in range(L):
                        load(wrt[:, k * P:(k + 1) * P].rearrange("p (k e) -> p k e", k=KD),
                             A["w_router"][k].rearrange("(k p) e -> p k e", p=P), s_x)
                sp.wait_ge(z["proj"], NSTEP)
                for k, w in ((0, A["w_out"][l, 0:256, :]), (6, A["w_out"][l, 768:1024, :])):
                    for b in range(2):
                        load(view(ar, 64 * b, 64, WOUT + k * D, (D, 2), (1, D)),
                             w[128 * b:128 * b + 128, :].rearrange("(a p) n -> p a n", p=64), z["wo"])
                load(ar[:, WOUT + 2 * D:WOUT + 6 * D].rearrange("p (k n) -> p k n", k=4),
                     A["w_out"][l, 256:768, :].rearrange("(k p) n -> p k n", p=P), z["wo"])
                with sp.Fori(0, NQ) as q:
                    for st in range(12):
                        m, hf, kh = stage_of(st)
                        w = A[("w_gate", "w_up", "w_down")[m]][l]
                        sp.wait_ge(z["wused"], q * 12 + (st + 1))
                        for e in range(QUAD):
                            slot = st % RSTAGES[l] * QUAD + e
                            load(ar[:, RING + slot * SLOT:RING + (slot + 1) * SLOT].rearrange("p (k n) -> p k n", k=4),
                                 w[bass.ds(q * QUAD + e, 1), kh * 512:(kh + 1) * 512, hf * 512:(hf + 1) * 512]
                                 .rearrange("e (k p) n -> p (e k) n", p=P), s_w[slot])
            sp.wait_ge(Z[L - 1]["ffn_done"], L)
            F = FP[L - 1]
            load(gfin, A["g_final"].partition_broadcast(P), s_x)
            for t in range(TL):
                sp.wait_ge(s_fin, t + 1)
                load(out[0, t * P:(t + 1) * P, :], ar[:, FIN + t * D:FIN + (t + 1) * D], s_out)
            sp.wait_ge(s_out, 16 * TL)

        PBANKS = (2, 3)
        POWS = [1 + 2 * TT + len(TILES[l]) + 1 for l in range(L)]

        @block.gpsimd
        def _(pool):
            nc.gpsimd.memset(modrow[:, :], 0.0).then_inc(s_bm0, 1)
            done = 0

            def powers(n):
                nonlocal done
                base = done
                with pool.Fori(0, n) as i:
                    pool.wait_ge(s_pin, i + (base + 1))
                    nc.gpsimd.tensor_tensor(pw[:, 8:16], pw[:, 0:8], pw[:, 16:24], ALU.pow).then_inc(s_pout, 1)
                done += n

            for l in range(L):
                z = Z[l]
                powers(1 + 2 * TT)
                pool.wait_ge(z["proj"], NSTEP)
                nc.gpsimd.memset(ar[:, QT:QT + 2 * SLOTS * P], 0.0).then_inc(z["qz"], 1)
                powers(len(TILES[l]) + 1)
                nx, F = SW[l] // P, FP[l]
                pool.wait_ge(s_xd, 16 * (l * TT + len(TILES[l])))
                for q in range(NQ):
                    pool.wait_ge(z["want"], q + 1)
                    for i in range(nx):
                        c = 8 + q if i == 2 else 2 * q + i
                        nc.gpsimd.indirect_dma_start(
                            out=ar[:, F["XG"] + i * D:F["XG"] + (i + 1) * D], out_offset=None, in_=rows,
                            in_offset=bass.IndirectOffsetOnAxis(ap=LIU[:, c:c + 1], axis=0),
                            bounds_check=NTOK - 1).then_inc(z["xg"], 16)
            powers(1)

        @block.tensor
        def _(pe):
            def mm(o, lhsT, rhs, start=True, stop=True):
                return nc.tensor.matmul(o, lhsT, rhs, start=start, stop=stop)

            def tr(o, in_, n=P):
                return nc.tensor.transpose(o, in_, ident[0:n, 0:n])

            pe.wait_ge(s_scm, 1)

            def mod_mult(n):
                pe.wait_ge(s_w[n % 8], 16 * (n // 8 + 1))
                k = n % 8
                if k == 0 and n:
                    pe.wait_ge(s_mcol, n // 8)
                for j in range(4):
                    if n < KD:
                        rhs = ar[:, M_RING + n * SLOT + j * 512:M_RING + n * SLOT + (j + 1) * 512]
                    else:
                        i = (n - KD) % MOD_SLOTS
                        t, a = ((gtb, j * 512), (ar, MS1 + j * QNW), (ar, MS2 + j * 512))[i]
                        rhs = t[:, a:a + 512]
                    last = mm(bank(2, 32 * j, 32), scm[:, k * 32:(k + 1) * 32], rhs, k == 0, k == 7)
                last.then_inc(s_mused, 1)

            def mod_transpose(g):
                pe.wait_ge(s_mrow, g + 1)
                for t in range(4):
                    last = tr(bank(2, col=t * P, w=P), modrow[:, g * 512 + t * P:g * 512 + (t + 1) * P])
                last.then_inc(s_mT, 1)

            for n in range(KD):
                mod_mult(n)

            for l in range(L):
                z = Z[l]
                def gates(sec, sent, banks):
                    for n in range(4):
                        s, jj = n // 2, n % 2
                        j = 2 * (sec % 2) + jj
                        mm(bank(banks[n]), view(ident, 0, P, 32 * j + s, (0, P)),
                           modrow[:, l * 1536 + sec // 2 * 512:l * 1536 + sec // 2 * 512 + 512]).then_inc(z[sent], 1)

                for n in range(TT * 2):
                    t, g = n // 2, n % 2
                    if l == 0 and n == 4:
                        mod_transpose(0)
                    pe.wait_ge(z["xn"], t + 1)
                    if n >= 4:
                        pe.wait_ge(z["htev" if g == 0 else "htevd"], t - 1)
                    for c in range(4):
                        a = XN + t * D + (4 * g + c) * P
                        last = tr(bank(4 + n % 4, col=c * P, w=P), ar[:, a:a + P])
                    last.then_inc(z["ht"], 1)
                pe.wait_ge(z["htev"], TT)
                pe.wait_ge(z["htevd"], TT)
                NB = PBANKS[l]
                for tau in range(NSTEP + 4):
                    if tau < NSTEP:
                        sec, t = STEPS[tau]
                        _, _, nq, ncol = SECTIONS[sec]
                        skip = nq if (l == L - 1 and t < TC) else 0
                        if t == 0:
                            pe.wait_ge(z[f"win{sec % 2}"], 16 * (sec // 2 + 1))
                        if tau >= NB:
                            if ACT_DONE[tau - NB]:
                                pe.wait_ge(z["pact"], int(ACT_DONE[tau - NB]))
                            if DVE_DONE[tau - NB]:
                                pe.wait_ge(z["pdve"], int(DVE_DONE[tau - NB]))
                        for k in range(KD):
                            a = WIN + sec % 2 * 4096 + k * ncol
                            h = HT0 + k * NTOK + t * P
                            if l == 0 and (tau, k) in MOD_AT:
                                mod_mult(MOD_AT[tau, k])
                            if l == 0 and k == 4 and tau in MOD_T_AT:
                                mod_transpose(MOD_T_AT[tau])
                            last = mm(bank(tau % NB, col=skip, w=ncol - skip), ar[:, h:h + P], ar[:, a + skip:a + ncol],
                                      k == 0, k == KD - 1)
                        last.then_inc(z["proj"], 1)
                    b = tau - 1
                    if 0 <= b < TT:
                        pe.wait_ge(z["bn"], b + 1)
                        if b:
                            pe.wait_ge(z["btev"], b)
                        noq = l == L - 1 and b < TC
                        if not noq:
                            for j in range(2):
                                tr(bank(5, 0, 96, j * P, P), ar[:, BN + 96 * j:BN + 96 * (j + 1)])
                        tr(bank(5, col=256, w=P), ar[:, BN + 192:BN + 320]).then_inc(z["bt"], 1)
                    b = tau - 2
                    if 0 <= b < TT:
                        pe.wait_ge(z["btev"], b + 1)
                        if b:
                            pe.wait_ge(z["bsa"], b)
                            pe.wait_ge(z["bsd"], b)
                        else:
                            pe.wait_ge(z["wb"], 32 * (l + 1))
                        noq = l == L - 1 and b < TC
                        if not noq:
                            for j in range(2):
                                mm(bank(6, w=384), ar[0:96, CQT + j * P:CQT + (j + 1) * P], wuq[0:96, j * 384:(j + 1) * 384],
                                   j == 0, j == 1)
                        mm(bank(7), ar[:, CKVT:CKVT + P], wukv[:, :]).then_inc(z["bs"], 1)
                    for i in k_jobs(tau - 1):
                        n = K_ORDER.index(i)
                        name = SECTIONS[STEPS[i][0]][0]
                        pe.wait_ge(z["kn"], n + 1)
                        if n >= 2:
                            pe.wait_ge(z["kt"], n - 1)
                        kb = KN + n % 2 * 384
                        if name == "B":
                            for h in range(4):
                                last = tr(bank(3 + n % 2, 0, 96, h * P, P), ar[:, kb + h * 96:kb + (h + 1) * 96])
                        else:
                            for h in range(2 if name == "C1" else 1):
                                last = tr(bank(3 + n % 2, col=h * P, w=P), ar[:, kb + h * P:kb + (h + 1) * P])
                        last.then_inc(z["kpe"], 1)
                tiles, mj = TILES[l], 0

                def job(kind, i, r):
                    nonlocal mj
                    t = tiles[i]
                    if mj:
                        pe.wait_ge(z["me"], mj)
                    else:
                        pe.wait_ge(z["bsd"], TT)
                        pe.wait_ge(z["bsa"], TT)
                    qn = QN + t * QNW
                    if kind == "Q":
                        blocks = [[("A", 0, P), ("A", P, P), ("C1", 0, P), ("C1", P, P)],
                                  [("B", 96 * h, 96) for h in range(4)], [("D", 0, P), ("D", P, P)]][r]
                        for c, (name, a, w) in enumerate(blocks):
                            a += qn + QN_AT[name]
                            last = tr(bank(7, 0, w, c * P, P), ar[:, a:a + w])
                    elif kind == "T":
                        pe.wait_ge(z["Cn"], i + 1)
                        for c in range(2):
                            a = OS + c * P
                            last = tr(bank(7, col=c * P, w=P), ar[:, a:a + P])
                    else:
                        if i == 0 and r == 0:
                            pe.wait_ge(z["wo"], 80 * (l + 1))
                        pe.wait_ge(z["Og"], 4 * (i + 1))
                        for k in range(KD):
                            a = WOUT + k * D + r * 512
                            last = mm(bank(7), ar[:, qn + k * P:qn + (k + 1) * P], ar[:, a:a + 512], k == 0, k == KD - 1)
                    last.then_inc(z["mj"], 1)
                    mj += 1

                pe.wait_ge(z["kt"], len(K_ORDER))
                pe.wait_ge(z["pact"], int(ACT_DONE[-1]))
                pe.wait_ge(z["pdve"], int(DVE_DONE[-1]))
                for r in range(3):
                    job("Q", 0, r)
                gates(2, "gt", (4, 5, 6, 3))
                for s, v, pv, jobs, ahead in PLANS[l]:
                    if s is not None:
                        i, slot = divmod(s, SLOTS)
                        if s == 1:
                            pe.wait_ge(z["gtev"], 4)
                        if slot == 0:
                            pe.wait_ge(z["me"], 3 if i == 0 else 6 * i)
                        if s >= 2:
                            pe.wait_ge(z["P"], s - 1)
                        rows = 96 if 4 <= slot < 8 else P
                        qa = QT + i % 2 * SLOTS * P + slot * P
                        for k0, c0, n in runs_of(keys_of(tiles[i], slot)):
                            a = KT + KTILE[slot] * NTOK + k0
                            last = mm(psS[s % 2][:, c0:c0 + n], ar[0:rows, qa:qa + P], ar[0:rows, a:a + n])
                        last.then_inc(z["S"], 1)
                    if v is not None:
                        i, u = divmod(v, TURNS)
                        s0 = i * SLOTS + LAST_SLOT[u]
                        pe.wait_ge(z["mixed"], v + 1)
                        if 8 <= u < 12:
                            s0 -= 1
                        if v:
                            pe.wait_ge(z["PTa"], v)
                            pe.wait_ge(z["PTd"], v)
                        for n, _ in enumerate(keys_of(tiles[i], LAST_SLOT[u])):
                            a = PB + s0 % 4 * NTOK + n * P
                            last = tr(psT[:, n * P:(n + 1) * P], ar[:, a:a + P])
                        last.then_inc(z["T"], 1)
                    if pv is not None:
                        i, u = divmod(pv, TURNS)
                        pe.wait_ge(z["PTa"], pv + 1)
                        pe.wait_ge(z["PTd"], pv + 1)
                        kt = keys_of(tiles[i], LAST_SLOT[u])
                        if pv >= 4 and (u % 4 == 0 if 8 <= u < 12 else u % 4 == 1):
                            pe.wait_ge(z["Og"], i * 4 + u // 4)
                        if 8 <= u < 12:
                            for n, k in enumerate(kt):
                                a, b = PT[pv % 3] + n * P, VV + k * 768 + VCOL[u]
                                last = mm(psO[:, u % 4 * P:(u % 4 + 1) * P], ar[:, a:a + P], ar[:, b:b + P], n == 0, n == len(kt) - 1)
                            last.then_inc(z["O"], 1)
                        elif u % 2:
                            for n, k in enumerate(kt):
                                for h in range(2):
                                    a, b = PT[(pv - 1 + h) % 3] + n * P, VV + k * 768 + VCOL[u] + 64 * h
                                    last = mm(psO[64 * h:64 * h + 64, u % 4 // 2 * P:(u % 4 // 2 + 1) * P], ar[:, b:b + 64],
                                              ar[:, a:a + P], n == 0, n == len(kt) - 1)
                            last.then_inc(z["O"], 2)
                    for j in jobs:
                        job(*j)
                pe.wait_ge(z["me"], mj)
                pe.sem_inc(z["wused"], RSTAGES[l])

                F = FP[l]
                gates(5, "fht", (0, 1, 2, 3))
                pe.wait_ge(z["fhtev"], 4)
                tl = TILES[l]
                for n in range(len(tl) * 2):
                    t, g = tl[n // 2], n % 2
                    pe.wait_ge(z["fxn"], n // 2 + 1)
                    if n >= 4:
                        pe.wait_ge(z["fhtev"], n + 1)
                    for c in range(4):
                        a = F["XN2"] + (t - F["t0"]) * D + (4 * g + c) * P
                        last = tr(bank(n % 4, col=c * P, w=P), ar[:, a:a + P])
                    last.then_inc(z["fht"], 1)
                pe.wait_ge(z["fhtev"], 4 + 2 * len(tl))
                if l == 0:
                    pe.wait_ge(s_x, 16 * 4)
                streams = [0, 1] if l == 0 else [0]
                for s in streams:
                    c0, n = ((CTX, LAT), (0, CTX))[s]
                    c0 -= F["t0"] * P
                    for k in range(KD):
                        last = mm(bank(s, 0, NE, 0, n), wrt[:, l * P + k * NE:l * P + (k + 1) * NE],
                                  ar[:, F["HT2"] + k * F["n"] + c0:F["HT2"] + k * F["n"] + c0 + n], k == 0, k == KD - 1)
                last.then_inc(z["lg"], 1)
                pe.wait_ge(z["lgev"], l + 1)
                for t in tl:
                    last = tr(bank(2, col=t * NE, w=NE), ar[0:NE, F["LGT"] + t * P:F["LGT"] + (t + 1) * P], NE)
                last.then_inc(z["lt"], 1)
                pe.wait_ge(z["prb"], l + 1)
                for t in tl:
                    o = bank(3, 0, NE, (t - TC) * P, P) if t >= TC else bank(4, 0, NE, t * P, P)
                    last = tr(o, ar[:, F["PRB"] + t * NE:F["PRB"] + (t + 1) * NE])
                last.then_inc(z["at"], 1)
                for n in range(2):
                    pe.wait_ge(z["dup"], 2 * l + n + 1)
                    tr(bank(5 + n, 0, P, 0, 48), ar[0:48, F["DUP"] + n * P:F["DUP"] + n * P + P], 48).then_inc(z["dupT"], 1)

                wc = l == 0
                JL = jobs_of_quad(wc)
                NJ = len(JL)
                W = SW[l]
                NX = W // P
                nact, ndve = KD, NJ - KD

                def read(q, n):
                    if JL[n][0] == "G":
                        pe.wait_ge(z["ja"], q * nact + (n - KD + 1 + KD))
                    else:
                        pe.wait_ge(z["jd"], q * ndve + sum(k != "G" for k, _ in JL[:n + 1]))

                def small(q, n):
                    kind, x = JL[n]
                    if n >= 2:
                        read(q, n - 2)
                    b = 6 + n % 2
                    if kind == "G":
                        for i in range(NX):
                            a = F["XG"] + i * D + x * P
                            last = tr(bank(b, col=i * P, w=P), ar[:, a:a + P])
                    elif kind == "H":
                        for i in range(NX):
                            a = F["HID"] + i * D + x * P
                            last = tr(bank(b, col=i * P, w=P), ar[:, a:a + P])
                    else:
                        t, hf = x
                        if t >= TC:
                            for pr in range(2):
                                a, r = F["STL"] + pr * LAT + (t - TC) * P, F["HID"] + pr * D + hf * 512
                                last = mm(bank(b), ar[:, a:a + P], ar[:, r:r + 512], pr == 0, pr == 1)
                        else:
                            a, r = F["STL"] + 2 * LAT + t * P, F["HID"] + 2 * D + hf * 512
                            last = mm(bank(b), ar[:, a:a + P], ar[:, r:r + 512])
                    last.then_inc(z["jp"], 1)

                def big(q, st):
                    m, hf, kh = stage_of(st)
                    b0 = 3 * (hf if m == 2 else m)
                    src = F["HIDT"] if m == 2 else F["XST"]
                    for pr in range(2):
                        for e in (2 * pr, 2 * pr + 1):
                            pe.wait_ge(*slot_filled(l, q, st, e))
                        for k, e in ((k, 2 * pr + j) for k in range(4) for j in range(2)):
                            a = src + (kh * 4 + k) * W + e * CAP_L
                            r = RING + (st % RSTAGES[l] * QUAD + e) * SLOT + k * 512
                            last = mm(bank(b0 + e // 2, 64 * (e % 2), 64), ar[:, a:a + CAP_L], ar[:, r:r + 512],
                                      kh == 0 and k == 0, kh == 1 and k == 3)
                    if wc:
                        for k in range(4):
                            for e in range(QUAD):
                                a = src + (kh * 4 + k) * W + 256 + e * CAP_C
                                r = RING + (st % RSTAGES[l] * QUAD + e) * SLOT + k * 512
                                last = mm(bank(b0 + 2, 32 * e, 32), ar[:, a:a + CAP_C], ar[:, r:r + 512],
                                          kh == 0 and k == 0, kh == 1 and k == 3)
                    last.then_inc(z["wused"], 1)

                pe.wait_ge(z["xg"], 16 * NX)
                for n in range(KD):
                    if n >= 2:
                        pe.wait_ge(z["ja"], n - 1)
                    for i in range(NX):
                        a = F["XG"] + i * D + n * P
                        last = tr(bank(n % 2, col=i * P, w=P), ar[:, a:a + P])
                    last.then_inc(z["gt0"], 1)
                pe.wait_ge(z["ja"], KD)
                pe.sem_inc(z["want"], 1)

                def quad(q, final):
                    pe.wait_ge(z["ja"], q * nact + nact)
                    pe.wait_ge(z["qd"], q + 1)
                    big(q, 0)
                    big(q, 1)
                    big(q, 2)
                    big(q, 3)
                    pe.wait_ge(z["silu"], q * 2 + 1)
                    big(q, 4)
                    big(q, 5)
                    pe.wait_ge(z["prod"], q * 2 + 1)
                    for n in range(4):
                        small(q, n)
                    big(q, 6)
                    big(q, 7)
                    pe.wait_ge(z["silu"], q * 2 + 2)
                    pe.wait_ge(z["jd"], q * ndve + 4)
                    big(q, 8)
                    pe.wait_ge(z["prod"], q * 2 + 2)
                    for n in range(4, 8):
                        small(q, n)
                    pe.wait_ge(z["jd"], q * ndve + 8)
                    big(q, 9)
                    if not final:
                        pe.wait_ge(z["xg"], q * (16 * NX) + 32 * NX)
                        for n in range(8, 16):
                            small(q, n)
                        read(q, 15)
                        pe.sem_inc(z["want"], 1)
                    big(q, 10)
                    big(q, 11)
                    half = (NJ - 16) // 2
                    pe.wait_ge(z["st"], q + 1)
                    for n in range(16, NJ):
                        if (n - 16) % half == 0:
                            pe.wait_ge(z["y"], q * 2 + ((n - 16) // half + 1))
                        if final and n < 18:
                            b = 6 + n % 2
                            small_c(q, n)
                        else:
                            small(q, n)

                def small_c(q, n):
                    t, hf = JL[n][1]
                    b = 6 + n % 2
                    if t >= TC:
                        for pr in range(2):
                            a, r = F["STL"] + pr * LAT + (t - TC) * P, F["HID"] + pr * D + hf * 512
                            last = mm(bank(b), ar[:, a:a + P], ar[:, r:r + 512], pr == 0, pr == 1)
                    else:
                        a, r = F["STL"] + 2 * LAT + t * P, F["HID"] + 2 * D + hf * 512
                        last = mm(bank(b), ar[:, a:a + P], ar[:, r:r + 512])
                    last.then_inc(z["jp"], 1)

                with pe.Fori(0, NQ - 1) as q:
                    quad(q, False)
                quad(NQ - 1, True)
                pe.wait_ge(z["xready"], l + 1)
                pe.sem_inc(z["ffn_done"], 1)

        @block.scalar
        def _(act):
            def a_(o, i, f=ACT.Copy, **kw):
                return nc.scalar.activation(o, i, f, **kw)

            act.wait_ge(s_const, 16 * NCONST)
            a_(sc[:, :], sc[:, :], ACT.Silu).then_inc(s_silu, 1)
            act.wait_ge(s_lamx, 1)
            for l in range(L):
                a_(lam[:, l * 8 + 2:l * 8 + 4], lam[:, l * 8:l * 8 + 2], ACT.Exp).then_inc(s_lamx, 1)

            for l in range(L):
                z = Z[l]
                if l == 0:
                    act.wait_ge(s_x, 16 * 2)
                else:
                    act.wait_ge(Z[l - 1]["ffn_done"], l)
                for t in range(TT):
                    if t:
                        act.wait_ge(z["sq"], t)
                    a_(ar[:, JUNK:JUNK + D], X[:, t * D:(t + 1) * D], ACT.Square, accum_out=ss[:, t:t + 1]).then_inc(z["sq"], 1)
                for t in range(TT):
                    if t == 0:
                        act.wait_ge(s_eff, 1 + l)
                    act.wait_ge(z["ht"], 2 * t + 1)
                    s = 0 if t >= TC else 1
                    for k in range(4):
                        h = HT0 + k * NTOK + t * P
                        last = a_(ar[:, h:h + P], bank(4 + 2 * (t % 2), col=k * P, w=P), ACT.Identity,
                                  scale=eff[:, l * 32 + s * 8 + k:l * 32 + s * 8 + k + 1],
                                  bias=modcol[:, l * 96 + s * 8 + k:l * 96 + s * 8 + k + 1])
                    last.then_inc(z["htev"], 1)
                for tau in range(NSTEP + 4):
                    if tau < NSTEP and uses_act(*STEPS[tau]):
                        sec, t = STEPS[tau]
                        name = SECTIONS[sec][0]
                        b = tau % PBANKS[l]
                        noq = l == L - 1 and t < TC
                        act.wait_ge(z["proj"], tau + 1)
                        v = VV + t * 768
                        if name == "B":
                            if t:
                                act.wait_ge(z["bsq"], 2 * t if l == 0 else 2 * t - min(t, TC))
                            if not noq:
                                a_(ar[:, JUNK:JUNK + B_QR], bank(b, w=B_QR), ACT.Square, accum_out=ss[:, 6:7]).then_inc(z["bsq"], 1)
                            a_(ar[:, JUNK + 256:JUNK + 384], bank(b, col=B_QR, w=B_KVR), ACT.Square,
                               accum_out=ss[:, 7:8]).then_inc(z["bsq"], 1)
                            act.wait_ge(z["pdve"], t + 1)
                            act.sem_inc(z["pact"], 1)
                        elif name == "A":
                            last = a_(ar[:, v:v + P], bank(b, col=384, w=P))
                            if t < TC:
                                n = K_ORDER.index(tau)
                                act.wait_ge(z["kpe"], n - 1)
                                if not noq:
                                    a_(view(ar, 0, P, QN + t * QNW + QN_AT["A"], (64, 2), (128, 2), (1, 64)),
                                       bankv(b, 0, P, 0, (128, 2), (64, 2), (1, 64)))
                                last = a_(ar[:, KN + n % 2 * 384:KN + n % 2 * 384 + P], bank(b, col=256, w=P))
                            last.then_inc(z["pact"], 1)
                            if t < TC:
                                act.wait_ge(z["pact"], int(ACT_DONE[tau]))
                                act.wait_ge(z["kn"], n)
                                act.sem_inc(z["kn"], 1)
                        elif name == "C1":
                            n = K_ORDER.index(tau)
                            act.wait_ge(z["kpe"], n - 1)
                            if not noq:
                                a_(ar[:, QN + t * QNW + QN_AT["C1"]:QN + t * QNW + QN_AT["C1"] + 256], bank(b, w=256))
                            a_(ar[:, KN + n % 2 * 384:KN + n % 2 * 384 + 256], bank(b, col=256, w=256)).then_inc(z["pact"], 1)
                            act.wait_ge(z["pact"], int(ACT_DONE[tau]))
                            act.wait_ge(z["kn"], n)
                            act.sem_inc(z["kn"], 1)
                        elif name == "C2":
                            a_(ar[:, v + 384:v + 640], bank(b, w=256)).then_inc(z["pact"], 1)
                        else:
                            a_(ar[:, v + 640:v + 768], bank(b, col=384, w=P))
                            q0 = 256 if noq else 0
                            if t:
                                act.wait_ge(z["dsq"], 2 * t)
                            a_(ar[:, SQ + q0:SQ + 384], bank(b, col=q0, w=384 - q0), ACT.Square).then_inc(z["dsq"], 1)
                            act.wait_ge(z["dsq"], 2 * t + 1)
                            act.sem_inc(z["pact"], 1)
                    b = tau - 1
                    if 0 <= b < TT:
                        act.wait_ge(z["bt"], b + 1)
                        if b:
                            act.wait_ge(z["bs"], b)
                        if not (l == L - 1 and b < TC):
                            for j in range(2):
                                a_(ar[0:96, CQT + j * P:CQT + (j + 1) * P], bank(5, 0, 96, j * P, P), ACT.Identity,
                                   scale=bgcol[0:96, l * 3 + j:l * 3 + j + 1])
                        a_(ar[:, CKVT:CKVT + P], bank(5, col=256, w=P), ACT.Identity,
                           scale=bgcol[:, l * 3 + 2:l * 3 + 3]).then_inc(z["btev"], 1)
                    b = tau - 2
                    if 0 <= b < TT:
                        n = K_ORDER.index(b)
                        act.wait_ge(z["bs"], b + 1)
                        if n >= 2:
                            act.wait_ge(z["kpe"], n - 1)
                        a_(view(ar, 0, P, KN + n % 2 * 384, (96, 4), (1, 64)), bankv(7, 0, P, 0, (128, 4), (1, 64)))
                        a_(view(ar, 0, P, VV + b * 768 + 128, (64, 4), (1, 64)), bankv(7, 0, P, 64, (128, 4), (1, 64))).then_inc(z["bsa"], 1)
                    for i in k_jobs(tau - 1):
                        n = K_ORDER.index(i)
                        sec, t = STEPS[i]
                        name = SECTIONS[sec][0]
                        kb = 3 + n % 2
                        act.wait_ge(z["kpe"], n + 1)
                        if name == "B":
                            last = a_(view(ar, 0, 96, KT + NTOK + t * P, (NTOK, 4), (1, P)), bankv(kb, 0, 96, 0, (P, 4), (1, P)))
                        elif name == "C1":
                            last = a_(view(ar, 0, P, KT + 5 * NTOK + t * P, (NTOK, 2), (1, P)), bankv(kb, 0, P, 0, (P, 2), (1, P)))
                        else:
                            k0 = KT + (0 if name == "A" else 7) * NTOK + t * P
                            last = a_(ar[:, k0:k0 + P], bank(kb, w=P))
                        last.then_inc(z["kt"], 1)
                tiles = TILES[l]
                mj = 0

                def job(kind, i, r):
                    nonlocal mj
                    t = tiles[i]
                    mj += 1
                    if kind == "O":
                        return
                    act.wait_ge(z["mj"], mj)
                    qt = QT + i % 2 * SLOTS * P
                    if kind == "T":
                        a = QN + t * QNW + 4 * P
                        last = a_(ar[:, a:a + 256], bank(7, w=256))
                    elif r == 1:
                        last = a_(ar[0:96, qt + 4 * P:qt + 8 * P], bank(7, 0, 96, 0, 512))
                    else:
                        s0 = 0 if r == 0 else 16
                        for j in range(2):
                            last = a_(view(ar, 64 * j, 64, qt + (s0 + j) * P, (2 * P, 2), (1, P)),
                                      bankv(7, 64 * j, 64, 0, (P, 2), (1, P)))
                        if r == 0:
                            for j in range(4):
                                last = a_(view(ar, 32 * j, 32, qt + (8 + j) * P, (4 * P, 2), (1, P)),
                                          bankv(7, 32 * j, 32, 256, (P, 2), (1, P)))
                    last.then_inc(z["me"], 1)

                act.wait_ge(z["qz"], l + 1)
                for r in range(3):
                    job("Q", 0, r)
                for n, b in enumerate((4, 5, 6, 3)):
                    act.wait_ge(z["gt"], n + 1)
                    a_(gtb[:, n * 512:(n + 1) * 512], bank(b)).then_inc(z["gtev"], 1)
                for s, v, pv, jobs, ahead in PLANS[l]:
                    if v is not None:
                        i, u = divmod(v, TURNS)
                        act.wait_ge(z["T"], v + 1)
                        if v >= 3:
                            act.wait_ge(z["O"], v - 2)
                        w = min(len(keys_of(tiles[i], LAST_SLOT[u])), 4) * P
                        a = PT[v % 3]
                        a_(ar[:, a:a + w], psT[:, 0:w]).then_inc(z["PTa"], 1)
                    if s is not None:
                        i, slot = divmod(s, SLOTS)
                        par = i % 2 * SLOTS + slot
                        act.wait_ge(z["nb"], s + 1)
                        if s >= 4:
                            i4, s4 = divmod(s - 4, SLOTS)
                            u4 = next(u for u, x in enumerate(LAST_SLOT) if x >= s4)
                            act.wait_ge(z["T"], i4 * TURNS + u4 + 1)
                        n = len(keys_of(tiles[i], slot)) * P
                        a = PB + s % 4 * NTOK
                        if slot < 4:
                            a_(esk[:, i % 2 * 4 + slot:i % 2 * 4 + slot + 1], sink[:, l * 8 + slot:l * 8 + slot + 1], ACT.Exp,
                               bias=nb[:, par:par + 1])
                        a_(ar[:, a:a + n], psS[s % 2][:, 0:n], ACT.Exp, bias=nb[:, par:par + 1], scale=SCALE[slot],
                           accum_out=rs[:, par:par + 1]).then_inc(z["P"], 1)
                    for j in jobs:
                        job(*j)
                tl = TILES[l]
                F, W = FP[l], SW[l]
                for n, t in enumerate(tl):
                    act.wait_ge(z["me"], 6 * len(tl))
                    if n:
                        act.wait_ge(z["fxn_sq"], n)
                    a_(ar[:, F["HT2"]:F["HT2"] + D], X[:, t * D:(t + 1) * D], ACT.Square,
                       accum_out=ss[:, t:t + 1]).then_inc(z["fxn_sq"], 1)
                for n in range(4):
                    act.wait_ge(z["fht"], n + 1)
                    a_(gtb[:, n * 512:(n + 1) * 512], bank(n)).then_inc(z["fhtev"], 1)
                for n in range(len(tl) * 2):
                    t, g = tl[n // 2], n % 2
                    act.wait_ge(z["fht"], 4 + n + 1)
                    s = 0 if t >= TC else 1
                    if g == 0:
                        x = F["XN2"] + (t - F["t0"]) * D
                        act.dma_start(rows[t * P:(t + 1) * P, :], ar[:, x:x + D]).then_inc(s_xd, 16)
                    for c in range(4):
                        k = 4 * g + c
                        h = F["HT2"] + k * F["n"] + (t - F["t0"]) * P
                        last = a_(ar[:, h:h + P], bank(n % 4, col=c * P, w=P), ACT.Identity,
                                  scale=eff[:, l * 32 + 16 + s * 8 + k:l * 32 + 16 + s * 8 + k + 1],
                                  bias=modcol[:, l * 96 + 48 + s * 8 + k:l * 96 + 48 + s * 8 + k + 1])
                    last.then_inc(z["fhtev"], 1)
                act.wait_ge(z["pe_ex"], 2 * l + 1)
                c0 = tl[0] * NE
                a_(ar[:, F["PRB"] + c0:F["PRB"] + TT * NE], ar[:, F["PRB"] + c0:F["PRB"] + TT * NE], ACT.Exp).then_inc(z["pe_ex"], 1)
                wc = l == 0
                NJ = len(jobs_of_quad(wc))
                R = RSTAGES[l]

                def modulated(x, b):
                    a = F["XST"] + x * W
                    k = l * 32 + 16 + x
                    m = l * 96 + 48 + x
                    if wc:
                        a_(ar[:, a + 256:a + 384], bank(b, col=256, w=P), ACT.Identity, scale=eff[:, k + 8:k + 9],
                           bias=modcol[:, m + 8:m + 9])
                    a_(ar[:, a:a + 256], bank(b, w=256), ACT.Identity, scale=eff[:, k:k + 1],
                       bias=modcol[:, m:m + 1]).then_inc(z["ja"], 1)

                def gated(q, hf):
                    act.wait_ge(z["wused"], q * 12 + (R + 2 + 4 * hf))
                    for i in range(W // P):
                        a = F["HID"] + i * D + hf * 512
                        last = a_(ar[:, a:a + 512], bank(i), ACT.Silu)
                    last.then_inc(z["silu"], 1)

                for x in range(KD):
                    act.wait_ge(z["gt0"], x + 1)
                    modulated(x, x % 2)
                with act.Fori(0, NQ - 1) as q:
                    gated(q, 0)
                    gated(q, 1)
                    for x in range(KD):
                        act.wait_ge(z["jp"], q * NJ + (KD + x + 1))
                        modulated(x, 6 + x % 2)
                gated(NQ - 1, 0)
                gated(NQ - 1, 1)
            for t in range(TL):
                act.wait_ge(Z[L - 1]["ffn_done"], L)
                if t:
                    act.wait_ge(s_fin0, t)
                a_(ar[:, FJ:FJ + D], X[:, (TC + t) * D:(TC + t + 1) * D], ACT.Square, accum_out=ss[:, t:t + 1]).then_inc(s_fin0, 1)

        @block.vector
        def _(dve):
            chain = [0]
            powers = [0]
            V = nc.vector

            def link(ins):
                chain[0] += 1
                ins.then_inc(s_dve, 1)
                dve.wait_ge(s_dve, chain[0])

            def rsqrt_begin(sums, n, count):
                link(V.tensor_scalar(pw[:, 0:n], sums, 1.0 / count, EPS, ALU.mult, ALU.add))
                powers[0] += 1
                dve.sem_inc(s_pin, 1)

            def rsqrt_end(n):
                dve.wait_ge(s_pout, powers[0])
                link(V.tensor_tensor(pwa[:, 0:n], pw[:, 0:n], pw[:, 8:8 + n], ALU.mult))
                link(V.scalar_tensor_tensor(pwa[:, 0:n], pwa[:, 0:n], -0.5, pw[:, 8:8 + n], ALU.mult, ALU.mult))
                link(V.scalar_tensor_tensor(pwr[:, 0:n], pwa[:, 0:n], 1.5, pw[:, 8:8 + n], ALU.add, ALU.mult))

            def rsqrt(sums, n, count):
                rsqrt_begin(sums, n, count)
                rsqrt_end(n)

            link(V.memset(pw[:, 0:16], 1.0))
            link(V.memset(pw[:, 16:24], -0.5))
            link(V.memset(scm[:, :], 0.0))
            dve.wait_ge(s_silu, 1)
            V.tensor_copy(view(scm, 0, P, 0, (1, 2), (32, KD)), view(sc, 0, P, 0, (KD, 2), (1, KD))).then_inc(s_scm, 1)
            for l in range(L):
                for j in range(2):
                    link(V.tensor_tensor(view(ar, 0, P, LAMP + l * 128 + 64 * j, (1, 32)), view(ar, 0, P, LAMP + l * 128 + 64 * j, (1, 32)),
                                         view(ar, 0, P, LAMP + l * 128 + 64 * j + 32, (1, 32)), ALU.mult))
                    link(V.reduce_sum(lam[:, l * 8 + j:l * 8 + j + 1], ar[:, LAMP + l * 128 + 64 * j:LAMP + l * 128 + 64 * j + 32], axis=AX.X))
            dve.sem_inc(s_lamx, 1)
            dve.wait_ge(s_lamx, 1 + L)
            for l in range(L):
                init = 0.8 - 0.6 * math.exp(-0.3 * l)
                link(V.tensor_tensor(lam[:, l * 8 + 4:l * 8 + 5], lam[:, l * 8 + 3:l * 8 + 4], lam[:, l * 8 + 2:l * 8 + 3], ALU.subtract))
                link(V.tensor_scalar(lam[:, l * 8 + 5:l * 8 + 6], lam[:, l * 8 + 4:l * 8 + 5], -init, None, ALU.add))
                link(V.tensor_scalar(gC[:, l * 64:l * 64 + 64], gC[:, l * 64:l * 64 + 64], 1 - init, None, ALU.mult))
                link(V.tensor_copy(view(sink, 0, P, l * 8, (2, 2), (1, 2)), view(sinkn, 0, P, l * 4, (1, 2), (2, 2))))
                link(V.tensor_scalar(sink[:, l * 8 + 4:l * 8 + 8], sink[:, l * 8:l * 8 + 4], -1.0, None, ALU.mult))

            def mod_rows(g):
                dve.wait_ge(s_bm, 16 * 8)
                dve.wait_ge(s_mused, KD * (g + 1))
                V.tensor_tensor(modrow[:, g * 512:(g + 1) * 512], modrow[:, g * 512:(g + 1) * 512], bank(2),
                                ALU.add).then_inc(s_mrow, 1)

            def mod_columns(g):
                l, r = divmod(g, 3)
                dve.wait_ge(s_mT, g + 1)
                for s in range(2):
                    last = V.tensor_copy(view(modcol, 0, P, l * 96 + 2 * r * 16 + s * 8, (16, 2), (4, 2), (1, 4)),
                                         bankv(2, 0, P, s, (64, 2), (32, 2), (P, 4)))
                last.then_inc(s_mcol, 1)
                if r != 1:
                    f = r // 2
                    dve.wait_ge(s_mcol, g + 1)
                    link(V.scalar_tensor_tensor(view(eff, 0, P, l * 32 + f * 16, (8, 2), (1, 8)),
                                                view(modcol, 0, P, l * 96 + (1 + 3 * f) * 16, (8, 2), (1, 8)), 1.0,
                                                view(gcol, 0, P, l * 16 + f * 8, (0, 2), (1, 8)), ALU.add, ALU.mult))
                    if f == 0:
                        dve.sem_inc(s_eff, 1)

            def rot(src, srcw, half, heads, lt):
                c = lt * 48 + (0 if half == 32 else 32)
                w = TL * 48
                V.tensor_tensor(view(ar, 0, P, T1, (2 * half, heads), (half, 2), (1, half)),
                                src(0, (2 * half, heads), (half, 2), (1, half)),
                                view(rope, 0, P, c, (0, heads), (0, 2), (1, half)), ALU.mult)
                V.tensor_tensor(view(ar, 0, P, T2, (2 * half, heads), (1, half)), src(half, (2 * half, heads), (1, half)),
                                view(rope, 0, P, 2 * w + c, (0, heads), (1, half)), ALU.mult)
                link(V.tensor_tensor(view(ar, 0, P, T2 + half, (2 * half, heads), (1, half)), src(0, (2 * half, heads), (1, half)),
                                     view(rope, 0, P, w + c, (0, heads), (1, half)), ALU.mult))

            for l in range(L):
                z = Z[l]
                dve.wait_ge(z["sq"], TT)
                rsqrt(ss[:, 0:TT], TT, D)
                for t in range(TT):
                    V.tensor_scalar(ar[:, XN + t * D:XN + (t + 1) * D], X[:, t * D:(t + 1) * D], pwr[:, t:t + 1], None,
                                    ALU.mult).then_inc(z["xn"], 1)
                if l == 0:
                    mod_rows(0)
                    mod_columns(0)
                for t in range(TT):
                    dve.wait_ge(z["ht"], 2 * t + 2)
                    s = 0 if t >= TC else 1
                    for k in range(4, 8):
                        h = HT0 + k * NTOK + t * P
                        last = V.tensor_scalar(ar[:, h:h + P], bank(5 + 2 * (t % 2), col=(k - 4) * P, w=P),
                                               eff[:, l * 32 + s * 8 + k:l * 32 + s * 8 + k + 1],
                                               modcol[:, l * 96 + s * 8 + k:l * 96 + s * 8 + k + 1], ALU.mult, ALU.add)
                    last.then_inc(z["htevd"], 1)
                dve.wait_ge(z["ht"], 2 * TT)
                for tau in range(NSTEP + 4):
                    if l == 0 and tau in MOD_ADD_AT:
                        mod_rows(MOD_ADD_AT[tau])
                    if l == 0 and tau in MOD_T_AT:
                        mod_columns(MOD_T_AT[tau])
                    if tau < NSTEP and uses_dve(*STEPS[tau]):
                        sec, t = STEPS[tau]
                        name = SECTIONS[sec][0]
                        b, lt = tau % PBANKS[l], t - TC
                        noq = l == L - 1 and t < TC
                        dve.wait_ge(z["proj"], tau + 1)
                        if name == "A":
                            dve.wait_ge(z["pact"], int(ACT_DONE[tau]))

                        def src(col, *dims, b=b):
                            return bankv(b, 0, P, col, *dims)

                        if name == "B":
                            dve.wait_ge(z["bsq"], 2 * (t + 1) if l == 0 else 2 * (t + 1) - min(t + 1, TC))
                            if not noq:
                                link(V.tensor_scalar(ss[:, 8:9], ss[:, 6:7], B_KVR / B_QR, None, ALU.mult))
                            else:
                                link(V.tensor_copy(ss[:, 8:9], ss[:, 7:8]))
                            link(V.tensor_copy(ss[:, 9:10], ss[:, 7:8]))
                            rsqrt(ss[:, 8:10], 2, B_KVR)
                            if t:
                                dve.wait_ge(z["bt"], t)
                            if not noq:
                                link(V.tensor_scalar(ar[:, BN:BN + B_QR], bank(b, w=B_QR), pwr[:, 0:1], None, ALU.mult))
                            link(V.tensor_scalar(ar[:, BN + B_QR:BN + 320], bank(b, col=B_QR, w=B_KVR), pwr[:, 1:2], None, ALU.mult))
                            dve.sem_inc(z["bn"], 1)
                            kr = KR + t % 3 * 32
                            if t >= TC:
                                rot(lambda col, *dims: src(320 + col, *dims), 0, 16, 1, lt)
                                link(V.tensor_tensor(ar[:, kr:kr + 32], ar[:, T1:T1 + 32], ar[:, T2:T2 + 32], ALU.add))
                            else:
                                link(V.tensor_copy(ar[:, kr:kr + 32], bank(b, col=320, w=32)))
                            dve.sem_inc(z["pdve"], 1)
                        else:
                            heads, half = (16, 16) if name == "C1" else (6, 32)
                            nk = 256 if name == "C1" else 128
                            n = K_ORDER.index(tau)
                            kb = KN + n % 2 * 384
                            if name == "D":
                                q0 = 256 if noq else 0
                                hq = q0 // 64
                                dve.wait_ge(z["dsq"], 2 * t + 1)
                                if noq:
                                    link(V.memset(ss[:, 10:14], 64.0))
                                link(V.tensor_reduce(ss[:, 10 + hq:16], view(ar, 0, P, SQ + q0, (64, 6 - hq), (1, 64)), AX.X, ALU.add))
                                dve.sem_inc(z["dsq"], 1)
                                rsqrt(ss[:, 10:16], 6, HD)
                                link(V.tensor_tensor(ar[:, T0 + q0:T0 + 384], bank(b, col=q0, w=384 - q0),
                                                     gD[:, l * 384 + q0:l * 384 + 384], ALU.mult))
                                link(V.tensor_tensor(view(ar, 0, P, T0 + q0, (64, 6 - hq), (1, 64)), view(ar, 0, P, T0 + q0, (64, 6 - hq), (1, 64)),
                                                     view(pwr, 0, P, hq, (1, 6 - hq), (0, 64)), ALU.mult))

                                def src(col, *dims):
                                    return view(ar, 0, P, T0 + col, *dims)

                            if t >= TC:
                                rot(src, 0, half, heads, lt)
                                in0, in1 = (lambda c, *d: view(ar, 0, P, T1 + c, *d)), (lambda c, *d: view(ar, 0, P, T2 + c, *d))
                            if n >= 2:
                                dve.wait_ge(z["kpe"], n - 1)
                            qa = QN + t * QNW + QN_AT[name]
                            if name == "C1":
                                qv, iv = (view(ar, 0, P, qa, (1, 256)), (0, (1, 256)))
                            else:
                                qv, iv = (view(ar, 0, P, qa, (64, 2), (128, 2), (1, 64)), (0, (128, 2), (64, 2), (1, 64)))
                            if t >= TC:
                                link(V.tensor_tensor(qv, in0(*iv), in1(*iv), ALU.add))
                                link(V.tensor_tensor(ar[:, kb:kb + nk], in0(256, (1, nk)), in1(256, (1, nk)), ALU.add))
                            else:
                                if not noq:
                                    link(V.tensor_copy(qv, src(*iv)))
                                link(V.tensor_copy(ar[:, kb:kb + nk], src(256, (1, nk))))
                            dve.sem_inc(z["pdve"], 1)
                            if n:
                                dve.wait_ge(z["kn"], n)
                            dve.sem_inc(z["kn"], 1)
                    b = tau - 2
                    if 0 <= b < TT:
                        n = K_ORDER.index(b)
                        noq = l == L - 1 and b < TC
                        dve.wait_ge(z["bs"], b + 1)
                        qa = QN + b * QNW + QN_AT["B"] + 64
                        if not noq:
                            link(V.tensor_copy(view(ar, 0, P, qa - 64, (96, 4), (1, 64)), bankv(6, 0, P, 0, (96, 4), (1, 64))))
                        if b >= TC:
                            rot(lambda col, *dims: bankv(6, 0, P, 64 + col, (96, 4), *dims[1:]), 0, 16, 4, b - TC)
                            link(V.tensor_tensor(view(ar, 0, P, qa, (96, 4), (1, 32)), view(ar, 0, P, T1, (32, 4), (1, 32)),
                                                 view(ar, 0, P, T2, (32, 4), (1, 32)), ALU.add))
                        elif not noq:
                            link(V.tensor_copy(view(ar, 0, P, qa, (96, 4), (1, 32)), bankv(6, 0, P, 64, (96, 4), (1, 32))))
                        if n >= 2:
                            dve.wait_ge(z["kpe"], n - 1)
                        link(V.tensor_copy(view(ar, 0, P, KN + n % 2 * 384 + 64, (96, 4), (1, 32)),
                                           view(ar, 0, P, KR + b % 3 * 32, (0, 4), (1, 32))))
                        dve.sem_inc(z["bsd"], 1)
                        dve.wait_ge(z["bsa"], b + 1)
                        if n:
                            dve.wait_ge(z["kn"], n)
                        dve.sem_inc(z["kn"], 1)
                tiles, mj = TILES[l], 0

                def job(kind, i, r):
                    nonlocal mj
                    t = tiles[i]
                    mj += 1
                    if kind == "O":
                        dve.wait_ge(z["mj"], mj)
                        g = (0 if t >= TC else 1) * D + r * 512
                        link(V.tensor_tensor(bank(7), bank(7), gtb[:, g:g + 512], ALU.mult))
                        x = t * D + r * 512
                        V.tensor_tensor(X[:, x:x + 512], X[:, x:x + 512], bank(7), ALU.add).then_inc(z["me"], 1)

                for r in range(3):
                    job("Q", 0, r)
                for s, v, pv, jobs, ahead in PLANS[l]:
                    if ahead is not None:
                        i, u = divmod(ahead, TURNS)
                        s1 = i * SLOTS + LAST_SLOT[u]
                        p1 = i % 2 * SLOTS + LAST_SLOT[u]
                        n = len(keys_of(tiles[i], LAST_SLOT[u])) * P
                        b = PB + s1 % 4 * NTOK
                        dve.wait_ge(z["P"], s1 + 1)
                        if u < 4:
                            link(V.tensor_tensor(rs[:, p1:p1 + 1], rs[:, p1:p1 + 1], esk[:, i % 2 * 4 + u:i % 2 * 4 + u + 1], ALU.add))
                        link(V.reciprocal(rr[:, p1:p1 + 1], rs[:, p1:p1 + 1]))
                        if 8 <= u < 12:
                            link(V.scalar_tensor_tensor(kk[:, 0:1], rr[:, p1:p1 + 1], lam[:, l * 8 + 5:l * 8 + 6], rs[:, p1 - 1:p1],
                                                        ALU.mult, ALU.mult))
                            a = PB + (s1 - 1) % 4 * NTOK
                            V.scalar_tensor_tensor(ar[:, a:a + n], ar[:, b:b + n], kk[:, 0:1], ar[:, a:a + n],
                                                   ALU.mult, ALU.add).then_inc(z["mixed"], 1)
                        else:
                            V.tensor_scalar(ar[:, b:b + n], ar[:, b:b + n], rr[:, p1:p1 + 1], None, ALU.mult).then_inc(z["mixed"], 1)
                    if s is not None:
                        i, slot = divmod(s, SLOTS)
                        par = i % 2 * SLOTS + slot
                        kt = keys_of(tiles[i], slot)
                        n = len(kt) * P
                        S = psS[s % 2]
                        dve.wait_ge(z["S"], s + 1)
                        if slot < 4 and tiles[i] >= TC:
                            b = tiles[i] - TC
                            if 0 < b < TL - 1:
                                link(V.tensor_tensor(view(S, 0, P, 256, (256, 2), (1, P)), view(S, 0, P, 256, (256, 2), (1, P)),
                                                     view(mask, 0, P, 0, (P, 2), (1, P)), ALU.add))
                            elif b > 0:
                                link(V.tensor_tensor(S[:, 256:384], S[:, 256:384], mask[:, 0:P], ALU.add))
                            else:
                                link(V.tensor_tensor(S[:, n - P:n], S[:, n - P:n], mask[:, P:2 * P], ALU.add))
                        link(V.reduce_max(mx[:, par:par + 1], S[:, 0:n], axis=AX.X))
                        if slot < 4:
                            V.tensor_scalar(nb[:, par:par + 1], mx[:, par:par + 1], -SCALE[slot], sink[:, l * 8 + 4 + slot:l * 8 + 5 + slot],
                                            ALU.mult, ALU.min).then_inc(z["nb"], 1)
                        else:
                            V.tensor_scalar(nb[:, par:par + 1], mx[:, par:par + 1], -SCALE[slot], None, ALU.mult).then_inc(z["nb"], 1)
                    if v is not None:
                        i, u = divmod(v, TURNS)
                        dve.wait_ge(z["T"], v + 1)
                        if v >= 3:
                            dve.wait_ge(z["O"], v - 2)
                        w = len(keys_of(tiles[i], LAST_SLOT[u])) * P
                        a = PT[v % 3]
                        if w > 512:
                            V.tensor_copy(ar[:, a + 512:a + w], psT[:, 512:w]).then_inc(z["PTd"], 1)
                        else:
                            dve.sem_inc(z["PTd"], 1)
                    if pv is not None and pv % 4 == 3:
                        i, u = divmod(pv, TURNS)
                        g = u // 4
                        p0 = i % 2 * SLOTS
                        dve.wait_ge(z["O"], pv + 1)
                        if g == 2:
                            if i:
                                dve.wait_ge(z["mj"], jobs_through_values(PLANS[l], i - 1))
                            link(V.reciprocal(view(rr, 0, P, p0 + 8, (2, 4)), view(rs, 0, P, p0 + 8, (2, 4))))
                            V.tensor_tensor(view(ar, 0, P, OS, (128, 2), (64, 2), (1, 64)),
                                            bankv(6, 0, P, 0, (256, 2), (192, 2), (1, 64)),
                                            view(rr, 0, P, p0 + 8, (4, 2), (2, 2), (0, 64)), ALU.mult).then_inc(z["Og"], 1)
                        else:
                            o = QN + tiles[i] * QNW + 2 * g * P
                            V.tensor_copy(ar[:, o:o + 256], bank(6, w=256)).then_inc(z["Og"], 1)
                        if g == 2:
                            dve.wait_ge(z["Og"], 4 * i + 3)
                            link(V.tensor_tensor(tmp[:, 0:256], ar[:, OS:OS + 256], ar[:, OS:OS + 256], ALU.mult))
                            link(V.tensor_reduce(ss[:, 8:12], view(ar, 0, P, TMP, (64, 4), (1, 64)), AX.X, ALU.add))
                            rsqrt_begin(ss[:, 8:12], 4, HD)
                    if pv is not None and pv % TURNS == 12:
                        o = OS
                        rsqrt_end(4)
                        link(V.tensor_tensor(view(ar, 0, P, o, (64, 4), (1, 64)), view(ar, 0, P, o, (64, 4), (1, 64)),
                                             view(pwr, 0, P, 0, (1, 4), (0, 64)), ALU.mult))
                        link(V.tensor_tensor(view(ar, 0, P, o, (64, 4), (1, 64)), view(ar, 0, P, o, (64, 4), (1, 64)),
                                             view(gC, 0, P, l * 64, (0, 4), (1, 64)), ALU.mult))
                        dve.sem_inc(z["Cn"], 1)
                    for j in jobs:
                        job(*j)
                tl = TILES[l]
                t0 = tl[0]
                F = FP[l]
                PRB, AFF, VAL, DUP, LGT = (F[n] for n in ("PRB", "AFF", "VAL", "DUP", "LGT"))
                dve.wait_ge(z["fxn_sq"], len(tl))
                rsqrt(ss[:, t0:TT], len(tl), D)
                for n, t in enumerate(tl):
                    V.tensor_scalar(ar[:, F["XN2"] + (t - t0) * D:F["XN2"] + (t - t0 + 1) * D], X[:, t * D:(t + 1) * D], pwr[:, n:n + 1], None,
                                    ALU.mult).then_inc(z["fxn"], 1)
                dve.wait_ge(z["lg"], l + 1)
                if l == 0:
                    V.tensor_copy(ar[0:NE, LGT:LGT + CTX], bank(1, 0, NE, 0, CTX))
                V.tensor_copy(ar[0:NE, LGT + CTX:LGT + NTOK], bank(0, 0, NE, 0, LAT)).then_inc(z["lgev"], 1)
                dve.wait_ge(z["lt"], l + 1)
                nt = len(tl)

                def pv3(a):
                    return view(ar, 0, P, a + t0 * NE, (NE, nt), (1, NE))

                def bc3(c):
                    return view(ar, 0, P, TMP + c, (1, nt), (0, NE))

                lt_ = bankv(2, 0, P, t0 * NE, (NE, nt), (1, NE))
                link(V.tensor_reduce(tmp[:, 0:nt], lt_, AX.X, ALU.max))
                link(V.tensor_tensor(pv3(PRB), lt_, bc3(0), ALU.subtract))
                dve.sem_inc(z["pe_ex"], 1)
                dve.wait_ge(z["pe_ex"], 2 * l + 2)
                link(V.tensor_reduce(tmp[:, 8:8 + nt], pv3(PRB), AX.X, ALU.add))
                link(V.reciprocal(tmp[:, 16:16 + nt], tmp[:, 8:8 + nt]))
                V.tensor_tensor(pv3(PRB), pv3(PRB), bc3(16), ALU.mult).then_inc(z["prb"], 1)
                link(V.memset(ar[0:48, AFF:AFF + LAT], -1.0))
                link(V.memset(ar[0:48, DUP:DUP + 2 * P], 0.0))
                dve.wait_ge(z["at"], l + 1)
                link(V.tensor_copy(ar[0:NE, AFF:AFF + LAT], bank(3, 0, NE, 0, LAT)))
                if l == 0:
                    link(V.tensor_copy(ar[32:48, AFF:AFF + CTX], bank(4, 0, NE, 0, CTX)))
                for r in range(CAP_L // 8):
                    v8 = ar[0:48, VAL + 8 * r:VAL + 8 * r + 8]
                    link(V.max(v8, ar[0:48, AFF:AFF + LAT]))
                    link(V.max_index(idx[0:48, 8 * r:8 * r + 8], v8, ar[0:48, AFF:AFF + LAT]))
                    if r < CAP_L // 8 - 1:
                        link(V.match_replace(ar[0:48, AFF:AFF + LAT], v8, ar[0:48, AFF:AFF + LAT], -2.0))
                for n in range(2):
                    o = DUP + n * P
                    srcs = [idx[0:NE, :], idx[32:48, :]] if n == 0 else [ar[0:NE, VAL:VAL + 64], ar[32:48, VAL:VAL + 64]]
                    for j in range(2):
                        link(V.tensor_copy(ar[0:NE, o + 64 * j:o + 64 * j + 64], srcs[0]))
                    if l == 0:
                        for j in range(4):
                            link(V.tensor_copy(ar[32:48, o + 32 * j:o + 32 * j + 32], srcs[1][:, 0:32]))
                    dve.sem_inc(z["dup"], 1)
                for n, dst in enumerate((LI, LG)):
                    dve.wait_ge(z["dupT"], 2 * l + n + 1)
                    for j in range(2):
                        link(V.tensor_copy(view(dst, 64 * j, 64, 0, (1, 8)), bankv(5 + n, 64 * j, 64, j, (2, 8))))
                    if l == 0:
                        for j in range(4):
                            link(V.tensor_copy(view(dst, 32 * j, 32, 8, (1, 4)), bankv(5 + n, 32 * j, 32, 32 + j, (4, 4))))
                link(V.tensor_scalar(LIU[:, 0:8], LI[:, 0:8], float(CTX), None, ALU.add))
                if l == 0:
                    link(V.tensor_copy(LIU[:, 8:12], LI[:, 8:12]))
                dve.sem_inc(z["want"], 1)
                dve.sem_inc(z["qd"], 1)
                wc = l == 0
                JL = jobs_of_quad(wc)
                NJ = len(JL)
                NX = SW[l] // P
                R = RSTAGES[l]
                ndve = NJ - KD
                STL, HID, HIDT = F["STL"], F["HID"], F["HIDT"]

                def selection(pairs, quads):
                    for pr in range(2):
                        last = V.tensor_scalar(ar[:, STL + pr * LAT:STL + (pr + 1) * LAT], iota[:, :], pairs(pr), None, ALU.is_equal)
                    if wc:
                        last = V.tensor_scalar(ar[:, STL + 2 * LAT:STL + 2 * LAT + CTX], iota[:, 0:CTX], quads, None, ALU.is_equal)
                    last.then_inc(z["st"], 1)

                def quad(q, final, col):
                    def small(n):
                        kind, x = JL[n]
                        b = 6 + n % 2
                        dve.wait_ge(z["jp"], q * NJ + (n + 1 - (KD if final and n >= 16 else 0)))
                        if kind == "H":
                            ins = V.tensor_copy(ar[:, HIDT + x * SW[l]:HIDT + (x + 1) * SW[l]], bank(b, w=SW[l]))
                        else:
                            t, hf = x
                            a = t * D + hf * 512
                            ins = V.tensor_tensor(X[:, a:a + 512], X[:, a:a + 512], bank(b), ALU.add)
                        ins.then_inc(z["jd"], 1)

                    for hf in range(2):
                        dve.wait_ge(z["wused"], q * 12 + (R + 4 + 4 * hf))
                        dve.wait_ge(z["silu"], q * 2 + (hf + 1))
                        for i in range(NX):
                            a = HID + i * D + hf * 512
                            last = V.tensor_tensor(ar[:, a:a + 512], ar[:, a:a + 512], bank(3 + i), ALU.mult)
                        last.then_inc(z["prod"], 1)
                        for n in range(4):
                            small(4 * hf + n)
                    selection(lambda pr: col(LI, q * 2 + pr), col(LI, q + 8))
                    for hf in range(2):
                        dve.wait_ge(z["wused"], q * 12 + (R + 10 + 2 * hf))
                        for i in range(NX):
                            a = HID + i * D + hf * 512
                            g = (D if i == 2 else 0) + hf * 512
                            last = V.scalar_tensor_tensor(ar[:, a:a + 512], bank(3 * hf + i), col(LG, q + 8 if i == 2 else q * 2 + i),
                                                          gtb[:, g:g + 512], ALU.mult, ALU.mult)
                        last.then_inc(z["y"], 1)
                    for n in range(16, NJ):
                        small(n)
                    dve.wait_ge(z["jd"], q * ndve + ndve)
                    dve.sem_inc(z["qd"], 1)

                with dve.Fori(0, NQ - 1) as q:
                    quad(q, False, lambda t, c: t[:, bass.ds(c, 1)])
                quad(NQ - 1, True, lambda t, c: t[:, c:c + 1])
                dve.sem_inc(z["xready"], 1)
            dve.wait_ge(s_fin0, TL)
            rsqrt(ss[:, 0:TL], TL, D)
            dve.wait_ge(s_x, 16 * 5)
            for t in range(TL):
                V.scalar_tensor_tensor(ar[:, FIN + t * D:FIN + (t + 1) * D], X[:, (TC + t) * D:(TC + t + 1) * D],
                                       pwr[:, t:t + 1], gfin, ALU.mult, ALU.mult).then_inc(s_fin, 1)


INPUTS = ["x", "c", "ctx", "c_ctx", "w_mod", "b_mod", "g_attn", "g_ffn", "w_in", "a_sink", "b_q_norm", "b_w_uq", "b_kv_norm",
          "b_w_ukv", "c_lambda", "c_subln", "d_q_norm", "d_k_norm", "w_out", "w_router", "w_gate", "w_up", "w_down", "g_final"]


def shape_constants():
    col = np.arange(P)
    before = np.where(col[None, :] >= col[:, None], 0.0, NEG)
    after = np.where(col[None, :] <= col[:, None], 0.0, NEG)
    n = np.arange(LAT)
    tables = []
    for dim in (HD, B_ROPE):
        quarter = dim // 4
        inv = (np.float32(10000.0) ** (-np.arange(quarter, dtype=np.float32) / np.float32(quarter))).astype(np.float32)
        ang = np.concatenate([(n // GRID_W)[:, None].astype(np.float32) * inv, (n % GRID_W)[:, None].astype(np.float32) * inv], 1)
        tables.append(ang.astype(np.float64))
    ang = np.concatenate(tables, 1)
    rope = np.stack([np.cos(ang), np.sin(ang), -np.sin(ang)])
    rope = rope.reshape(3, TL, P, 48).transpose(2, 0, 1, 3).reshape(P, 3 * TL * 48)
    return {
        "ident": np.eye(P, dtype=np.float32),
        "iota": np.broadcast_to(np.arange(LAT, dtype=np.float32), (P, LAT)).copy(),
        "mask": np.concatenate([before, after], 1).astype(np.float32),
        "rope": rope.astype(np.float32),
    }


def kernel(**inputs):
    import numpy as _np
    import concourse.bacc as _bacc
    from concourse import mybir as _mybir
    from concourse.bass_utils import run_bass_kernel_spmd as _run

    nc = _bacc.Bacc("TRN2", target_bir_lowering=False, num_devices=1)
    given = {name: _np.ascontiguousarray(inputs[name]) for name in INPUTS}
    given.update(shape_constants())
    arrays, aps = {}, {}
    for name, a in given.items():
        arrays[f"in_{name}"] = a
        aps[name] = nc.dram_tensor(f"in_{name}", a.shape, _mybir.dt.from_np(a.dtype), kind="ExternalInput").ap()
    out = nc.dram_tensor("out_0", (1, LAT, D), _mybir.dt.float32, kind="ExternalOutput").ap()
    backbone_program(nc, aps, out)
    r = _run(nc, [arrays], core_ids=[0])
    return r.results[0]["out_0"]
```

```python
import math
from contextlib import ExitStack

import concourse.bass as bass
import numpy as np
from concourse import mybir

f32 = mybir.dt.float32
f32r = mybir.dt.float32r
u32 = mybir.dt.uint32
ALU = mybir.AluOpType
ACT = mybir.ActivationFunctionType
AX = mybir.AxisListType

P = 128
D, L = 1024, 2
KD = D // P
CTX, LAT = 256, 512
TC, TL = CTX // P, LAT // P
TT = TC + TL
NTOK = CTX + LAT
EPS = 1e-6
NEG = -1e30
GRID_W = 64
HD = 64
B_NOPE, B_ROPE, B_QR, B_KVR = 64, 32, 192, 128
B_QK = B_NOPE + B_ROPE
C_QK = 32
IN_COLS = 2144
NE, FE = 16, 1024
CAP_L, CAP_C = 2 * LAT // NE, 2 * CTX // NE
QUAD = 4
NQ = NE // QUAD

SECTIONS = [("B", 512, B_QR, 352), ("A", 0, 256, 512), ("C2", 1376, 0, 256), ("D", 1632, 256, 512),
            ("C1", 864, 256, 512)]
STEPS = [(sec, t) for sec in range(len(SECTIONS)) for t in range(TT)]
NSTEP = len(STEPS)

SLOTS = 20
SCALE = [HD ** -0.5] * 4 + [B_QK ** -0.5] * 4 + [C_QK ** -0.5] * 8 + [HD ** -0.5] * 4
KTILE = [0] * 4 + [1, 2, 3, 4] + [5] * 4 + [6] * 4 + [7] * 4
LAST_SLOT = [0, 1, 2, 3, 4, 5, 6, 7, 9, 11, 13, 15, 16, 17, 18, 19]
TURNS = len(LAST_SLOT)
VCOL = [0] * 4 + [128, 128, 256, 256] + [384, 384, 512, 512] + [640] * 4
LAG = 3
OT_AT, OP_AT, QT_AT = (3,), (5, 8), (12, 14, 16)


def keys_of(t, slot):
    if t < TC:
        return list(range(TC))
    if slot < 4:
        b = t - TC
        return list(range(TC)) + [TC + j for j in range(max(b - 1, 0), min(b + 1, TL - 1) + 1)]
    return list(range(TT))


def runs_of(kt):
    runs = []
    for n, k in enumerate(kt):
        if runs and runs[-1][0] + runs[-1][2] == k * P and n % 4:
            runs[-1][2] += P
        else:
            runs.append([k * P, n * P, P])
    return runs


def attention_plan(tiles):
    n = len(tiles) * SLOTS
    ready = {i * SLOTS + s + LAG: i * TURNS + v for i in range(len(tiles)) for v, s in enumerate(LAST_SLOT)}
    plan, waiting = [], None
    for s in range(n + LAG + 2):
        v = ready.get(s)
        i, at = divmod(s, SLOTS)
        jobs = []
        if at in QT_AT and i + 1 < len(tiles):
            jobs.append(("Q", i + 1, QT_AT.index(at)))
        if i and s < n:
            if at in OT_AT:
                jobs.append(("T", i - 1, OT_AT.index(at)))
            if at in OP_AT:
                jobs.append(("O", i - 1, OP_AT.index(at)))
        mult = None
        if v is not None or s >= n:
            mult, waiting = waiting, v
        plan.append((s if s < n else None, v, mult, jobs, ready.get(s + 1)))
    last = len(tiles) - 1
    plan.append((None, None, None, [("T", last, 0), ("O", last, 0), ("O", last, 1)], None))
    return plan


def uses_act(sec, t):
    return not (SECTIONS[sec][0] == "C1" and t >= TC)


def uses_dve(sec, t):
    name = SECTIONS[sec][0]
    return name in ("B", "D") or (name in ("A", "C1") and t >= TC)


ACT_DONE = np.cumsum([uses_act(*s) for s in STEPS])
DVE_DONE = np.cumsum([uses_dve(*s) for s in STEPS])


def k_jobs(tau):
    out = []
    if 0 <= tau < NSTEP and SECTIONS[STEPS[tau][0]][0] in ("A", "C1", "D"):
        out.append(tau)
    if 0 <= tau - 2 < TT:
        out.append(tau - 2)
    return out


MOD_CHUNKS = [(l, r, k) for l in range(L) for r in range(3) for k in range(KD)]
MOD_AT = {(1 + 3 * g + i // 4, 2 * (i % 4) + 1): KD + g * KD + i for g in range(3 * L - 1) for i in range(KD)}
MOD_STEP = {n: at for at, n in MOD_AT.items()}
MOD_T_AT = {1 + 3 * g + 2: g + 1 for g in range(3 * L - 1)}
MOD_ADD_AT = {1 + 3 * g + 1: g + 1 for g in range(3 * L - 1)}
MOD_SLOTS = 3

K_ORDER = [j for tau in range(NSTEP + 3) for j in k_jobs(tau)]


def jobs_of_quad(with_ctx):
    tiles = list(range(TT)) if with_ctx else list(range(TC, TT))
    out = [("H", f) for f in range(KD)] + [("G", k) for k in range(KD)]
    return out + [("C", (t, h)) for h in range(2) for t in tiles]


COMBINE_BANKS = (6, 7, 0, 1, 2)


def stage_of(st):
    return (0, 0, 1, 1, 0, 0, 1, 1, 2, 2, 2, 2)[st], (0, 0, 0, 0, 1, 1, 1, 1, 0, 0, 1, 1)[st], st % 2


def jobs_through_values(plan, i):
    n = 3
    for _, _, _, jobs, _ in plan:
        for j in jobs:
            n += 1
            if j == ("T", i, 0):
                return n


def backbone_program(nc, A, out):
    ctx = ExitStack()
    with ctx:
        def sb(name, cols, dt=f32, rows=P):
            return ctx.enter_context(nc.sbuf_tensor(name, [rows, cols], dt))

        def sem(name):
            return ctx.enter_context(nc.semaphore(name))

        def view(tensor, p0, n, col, *dims):
            w = tensor.shape[1]
            return bass.AP(tensor, p0 * w + col, [[w, n], *[list(d) for d in dims]])

        X = sb("X", TT * D)
        ident = sb("ident", P)
        iota = sb("iota", LAT)
        mask = sb("mask", 2 * P)
        modrow = sb("modrow", L * 3 * 512)
        modcol = sb("modcol", L * 96)
        eff = sb("eff", L * 32)
        gtb = sb("gtb", 2 * D)
        rope = sb("rope", 3 * TL * 48)
        gD = sb("gD", L * 384)
        gC = sb("gC", L * 64)
        gcol = sb("gcol", L * 16)
        bgcol = sb("bgcol", L * 3)
        sinkn = sb("sinkn", L * 4)
        sink = sb("sink", L * 8)
        lam = sb("lam", L * 8)
        wrt = sb("wrt", L * KD * NE + NE)
        wuq = sb("wuq", 2 * 384)
        wukv = sb("wukv", 512)
        sc = sb("sc", 2 * KD)
        scm = sb("scm", KD * 32)
        ss = sb("ss", 16)
        pw = sb("pw", 24)
        mx = sb("mx", 2 * SLOTS)
        nb = sb("nb", 2 * SLOTS)
        rs = sb("rs", 2 * SLOTS)
        rr = sb("rr", 2 * SLOTS)
        esk = sb("esk", 2 * 4)
        kk = sb("kk", 8)
        LI = sb("LI", 16)
        LG = sb("LG", 16)
        AR = 36864
        arena_at = nc.sbuf_base
        ar = sb("arena", AR)
        assert nc.sbuf_base == arena_at + 4 * AR

        LAMP = 22528
        M_RING = 6144
        FIN = 4096
        XN, HT0, WIN, PX = 0, 17664, 23808, 32000
        JUNK, T1, T2, T0 = PX, PX + 1024, PX + 1536, PX + 2048
        KN = PX + 2560
        BN = PX + 3328
        KR = PX + 3648
        CQT, CKVT = PX + 3744, PX + 4000
        SQ = PX + 4128
        KT, VV, QN = 0, 6144, 10752
        QNW = 1152
        MS1, MS2 = QN + 640, 5 * NTOK
        QN_AT = {"A": 0, "B": 256, "C1": 640, "D": 896}
        QT, WOUT, PB, OS = 17664, 23808, 32000, 22784
        PT = (32000 + 3072, 32000 + 3840, OS + 256)
        RING, SLOT = 0, 2048
        SW = (384, 256)
        RSTAGES = (2, 3)

        def places(l):
            at, p = RSTAGES[l] * QUAD * SLOT, {}
            for name, cols in (("XST", KD * SW[l]), ("HID", SW[l] // P * D), ("HIDT", KD * SW[l]), ("XG", SW[l] // P * D),
                               ("STL", 2 * LAT + (CTX if l == 0 else 0))):
                p[name] = at
                at += cols
            if l == 0:
                p["YH"], p["YL"] = at, at + SW[l] // P * D
                at += 2 * (SW[l] // P * D)
            assert at <= TMP
            at = RSTAGES[l] * QUAD * SLOT
            n = NTOK if l == 0 else LAT
            for name, cols in (("XN2", n * KD), ("HT2", n * KD), ("AFF", LAT), ("VAL", 64), ("DUP", 2 * P), ("LGT", NTOK),
                               ("PRB", TT * NE), ("LG4", TT * NE)):
                p[name] = at
                at += cols
            assert at <= TMP
            p["n"], p["t0"] = n, (0 if l == 0 else TC)
            return p

        idx = sb("idx", 64, u32)
        LIU = sb("LIU", 12, u32)
        pwa, pwr = sb("pwa", 8), sb("pwr", 8)
        TMP = 36608
        tmp = ar[:, TMP:TMP + 256]

        psS = [ctx.enter_context(nc.psum_tensor(f"psS{i}", [P, 1024], f32)) for i in range(2)]
        psT = ctx.enter_context(nc.psum_tensor("psT", [P, 1024], f32))
        psO = ctx.enter_context(nc.psum_tensor("psO", [P, 512], f32))
        psM = ctx.enter_context(nc.psum_tensor("psM", [P, 512], f32))
        BANKS = [(psS[0], 0), (psS[0], 512), (psS[1], 0), (psS[1], 512), (psT, 0), (psT, 512), (psO, 0), (psM, 0)]

        def bank(b, p0=0, n=P, col=0, w=512):
            t, c = BANKS[b]
            return t[p0:p0 + n, c + col:c + col + w]

        def bankv(b, p0, n, col, *dims):
            t, c = BANKS[b]
            return view(t, p0, n, c + col, *dims)

        s_const, s_x, s_bm = sem("consts_loaded"), sem("tokens_loaded"), sem("bias_loaded")
        s_bm0 = sem("bias_cleared")
        s_mused, s_scm, s_mrow, s_mT, s_mcol = (sem(n) for n in (
            "mod_slots_used", "silu_ready", "mod_row_ready", "mod_transposed", "mod_columns_ready"))
        s_silu = sem("silu_done")
        s_dve = sem("dve_chain")
        s_pin, s_pout = sem("pow_base_ready"), sem("pow_done")
        s_eff = sem("gains_ready")
        s_lamx = sem("lambda_exponents")
        s_fin0 = sem("final_squares")
        s_out = sem("out_stored")
        s_fin = sem("final_ready")

        s_xd = sem("rows_stored")
        yf, yh = sem("outputs_ready"), sem("outputs_rounded")

        def sems(l, names):
            return {n: sem(f"{n}_{l}") for n in names.split()}

        Z = [sems(l, "sq xn ht htev htevd gt gtev win0 win1 proj pact pdve dsq bsq bn bt btev bs bsa bsd kn kpe kt "
                     "S nb P Cn mixed T PTa PTd O Og mj me fxn_sq fxn fht fhtev fhtevd wused st jp ja jg jd silu prod y qd xg want gt0") for l in range(L)]
        once = {n: sem(n) for n in "wb wo qz lg lgev lt pe_ex prb at dup dupT ffn_done xready".split()}
        for z in Z:
            z.update(once)
        s_w = [sem(f"ring_slot{i}") for i in range(12)]

        def slot_filled(l, q, st, e):
            n = RSTAGES[l]
            base = 96 + 384 * l if st % n < 2 else 0
            return s_w[st % n * QUAD + e], q * (16 * 12 // n) + (base + 16 * (st // n + 1))

        block = ctx.enter_context(nc.Block())
        PLANS = [attention_plan(list(range(TT))), attention_plan(list(range(TC, TT)))]
        TILES = [list(range(TT)), list(range(TC, TT))]

        NCONST = 7 + 12 * L
        rows = nc.dram_tensor("normed_rows", (NTOK, D), f32).ap()
        FP = [places(l) for l in range(L)]
        stl_r, yh_r, yl_r = (nc.alloc_sbuf_tensor_at(name, [P, cols], f32r, offset=arena_at + 4 * FP[0][at])
                             for name, cols, at in (("selection_r", 2 * LAT + CTX, "STL"), ("output_high", 3 * D, "YH"),
                                                    ("output_low", 3 * D, "YL")))
        gfin = ar[:, XN:XN + D]

        @block.sync
        def _(sp):
            def load(dst, src, s, columns=False):
                sp.dma_start(dst, src, allow_slow_non_contiguous=columns).then_inc(s, 16)

            load(X[:, 0:TC * D].rearrange("p (t d) -> p t d", t=TC), A["ctx"][0].rearrange("(t p) d -> p t d", p=P), s_x)
            load(X[:, TC * D:].rearrange("p (t d) -> p t d", t=TL), A["x"][0].rearrange("(t p) d -> p t d", p=P), s_x)
            load(sc[:, 0:KD], A["c"].rearrange("b (k p) -> p (b k)", p=P), s_const, True)
            load(sc[:, KD:2 * KD], A["c_ctx"].rearrange("(k p) -> p k", p=P), s_const, True)
            load(ident[:, :], A["ident"], s_const)
            load(iota[:, :], A["iota"], s_const)
            load(mask[:, :], A["mask"], s_const)
            load(rope[:, :], A["rope"], s_const)
            load(sinkn[:, :], A["a_sink"].rearrange("l h -> (l h)").partition_broadcast(P), s_const)
            for l in range(L):
                for h in range(4):
                    load(gD[:, l * 384 + h * 64:l * 384 + h * 64 + 64], A["d_q_norm"][l, :].partition_broadcast(P), s_const)
                for h in range(2):
                    load(gD[:, l * 384 + 256 + h * 64:l * 384 + 320 + h * 64], A["d_k_norm"][l, :].partition_broadcast(P), s_const)
                load(gC[:, l * 64:l * 64 + 64], A["c_subln"][l, :].partition_broadcast(P), s_const)
                load(gcol[:, l * 16:l * 16 + 8], A["g_attn"][l, :].rearrange("(k p) -> p k", p=P), s_const, True)
                load(gcol[:, l * 16 + 8:l * 16 + 16], A["g_ffn"][l, :].rearrange("(k p) -> p k", p=P), s_const, True)
                load(bgcol[0:96, l * 3:l * 3 + 2], A["b_q_norm"][l, :].rearrange("(k p) -> p k", p=96), s_const, True)
                load(bgcol[:, l * 3 + 2:l * 3 + 3], A["b_kv_norm"][l, :].rearrange("(p k) -> p k", k=1), s_const, True)
                load(ar[:, LAMP + l * 128:LAMP + l * 128 + 128], A["c_lambda"][l].rearrange("a b -> (a b)").partition_broadcast(P), s_const)

            def mod_chunk(n):
                l, r, k = MOD_CHUNKS[n]
                w = A["w_mod"][l, k * P:(k + 1) * P, r * 2048:(r + 1) * 2048]
                if n < KD:
                    load(ar[:, M_RING + n * SLOT:M_RING + (n + 1) * SLOT], w, s_w[n])
                    return
                i = (n - KD) % MOD_SLOTS
                if n - KD >= MOD_SLOTS:
                    sp.wait_ge(s_mused, n - MOD_SLOTS + 1)
                elif i == 0:
                    sp.wait_ge(s_mused, 1)
                else:
                    sp.wait_ge(s_mused, KD) if i == 1 else sp.wait_ge(Z[0]["ht"], 2 * TT)
                if i == 0:
                    load(gtb[:, :], w, s_w[n % 8])
                elif i == 1:
                    load(view(ar, 0, P, MS1, (QNW, 4), (1, 512)), w.rearrange("p (j n) -> p j n", j=4), s_w[n % 8])
                else:
                    load(ar[:, MS2:MS2 + SLOT], w, s_w[n % 8])

            for n in range(KD):
                mod_chunk(n)
            sp.wait_ge(s_bm0, 1)
            for j in range(4):
                for s in range(2):
                    load(view(modrow, 32 * j + s, 1, 0, (1536, L), (512, 3), (1, 512)),
                         A["b_mod"].rearrange("l (r j n) -> j l r n", r=3, j=4)[j:j + 1], s_bm)
            mod_next = [KD]
            for l in range(L):
                z = Z[l]
                if l:
                    sp.wait_ge(Z[l - 1]["ffn_done"], l)
                load(wuq[0:96, :].rearrange("p (k n) -> p k n", k=2), A["b_w_uq"][l].rearrange("(k p) n -> p k n", p=96), z["wb"])
                load(wukv[:, :], A["b_w_ukv"][l], z["wb"])
                for sec, (_, c0, _, nc_) in enumerate(SECTIONS):
                    while l == 0 and mod_next[0] < len(MOD_CHUNKS):
                        n = mod_next[0]
                        if sec < 2 or (n - MOD_SLOTS >= KD and MOD_STEP[n - MOD_SLOTS][0] >= (sec - 1) * TT):
                            break
                        mod_chunk(n)
                        mod_next[0] += 1
                    if sec >= 2:
                        sp.wait_ge(z["proj"], (sec - 1) * TT)
                    at = WIN + sec % 2 * 4096
                    load(ar[:, at:at + KD * nc_].rearrange("p (k n) -> p k n", k=KD),
                         A["w_in"][l, :, c0:c0 + nc_].rearrange("(k p) n -> p k n", p=P), z[f"win{sec % 2}"])
                if l == 0:
                    assert mod_next[0] == len(MOD_CHUNKS)
                    for k in range(L):
                        load(wrt[:, k * P:(k + 1) * P].rearrange("p (k e) -> p k e", k=KD),
                             A["w_router"][k].rearrange("(k p) e -> p k e", p=P), s_x)
                sp.wait_ge(z["proj"], NSTEP)
                for k, w in ((0, A["w_out"][l, 0:256, :]), (6, A["w_out"][l, 768:1024, :])):
                    for b in range(2):
                        load(view(ar, 64 * b, 64, WOUT + k * D, (D, 2), (1, D)),
                             w[128 * b:128 * b + 128, :].rearrange("(a p) n -> p a n", p=64), z["wo"])
                load(ar[:, WOUT + 2 * D:WOUT + 6 * D].rearrange("p (k n) -> p k n", k=4),
                     A["w_out"][l, 256:768, :].rearrange("(k p) n -> p k n", p=P), z["wo"])
                with sp.Fori(0, NQ) as q:
                    for st in range(12):
                        m, hf, kh = stage_of(st)
                        w = A[("w_gate", "w_up", "w_down")[m]][l]
                        sp.wait_ge(z["wused"], q * 12 + (st + 1))
                        for e in range(QUAD):
                            slot = st % RSTAGES[l] * QUAD + e
                            load(ar[:, RING + slot * SLOT:RING + (slot + 1) * SLOT].rearrange("p (k n) -> p k n", k=4),
                                 w[bass.ds(q * QUAD + e, 1), kh * 512:(kh + 1) * 512, hf * 512:(hf + 1) * 512]
                                 .rearrange("e (k p) n -> p (e k) n", p=P), s_w[slot])
            sp.wait_ge(Z[L - 1]["ffn_done"], L)
            load(gfin, A["g_final"].partition_broadcast(P), s_x)
            for t in range(TL):
                sp.wait_ge(s_fin, t + 1)
                load(out[0, t * P:(t + 1) * P, :], ar[:, FIN + t * D:FIN + (t + 1) * D], s_out)
            sp.wait_ge(s_out, 16 * TL)

        PBANKS = (2, 3)
        POWS = [1 + 2 * TT + len(TILES[l]) + 1 for l in range(L)]

        @block.gpsimd
        def _(pool):
            nc.gpsimd.memset(wrt[:, L * KD * NE:], 0.0)
            nc.gpsimd.memset(modrow[:, :], 0.0).then_inc(s_bm0, 1)
            done = 0

            def powers(n):
                nonlocal done
                base = done
                with pool.Fori(0, n) as i:
                    pool.wait_ge(s_pin, i + (base + 1))
                    nc.gpsimd.tensor_tensor(pw[:, 8:16], pw[:, 0:8], pw[:, 16:24], ALU.pow).then_inc(s_pout, 1)
                done += n

            for l in range(L):
                z = Z[l]
                powers(1 + 2 * TT)
                pool.wait_ge(z["proj"], NSTEP)
                for i in range(2):
                    nc.gpsimd.memset(ar[:, QT + i * SLOTS * P:QT + i * SLOTS * P + 4 * P], 0.0)
                    nc.gpsimd.memset(ar[:, QT + i * SLOTS * P + 8 * P:QT + (i + 1) * SLOTS * P], 0.0).then_inc(z["qz"], 1)
                powers(len(TILES[l]) + 1)
                nx, F = SW[l] // P, FP[l]
                pool.wait_ge(s_xd, 16 * (l * TT + len(TILES[l])))
                for q in range(NQ):
                    pool.wait_ge(z["want"], q + 1)
                    for i in range(nx):
                        c = 8 + q if i == 2 else 2 * q + i
                        nc.gpsimd.indirect_dma_start(
                            out=ar[:, F["XG"] + i * D:F["XG"] + (i + 1) * D], out_offset=None, in_=rows,
                            in_offset=bass.IndirectOffsetOnAxis(ap=LIU[:, c:c + 1], axis=0),
                            bounds_check=NTOK - 1).then_inc(z["xg"], 16)
            powers(1)

        @block.tensor
        def _(pe):
            def mm(o, lhsT, rhs, start=True, stop=True):
                return nc.tensor.matmul(o, lhsT, rhs, start=start, stop=stop)

            def tr(o, in_, n=P):
                return nc.tensor.transpose(o, in_, ident[0:n, 0:n])

            pe.wait_ge(s_scm, 1)

            def mod_mult(n):
                pe.wait_ge(s_w[n % 8], 16 * (n // 8 + 1))
                k = n % 8
                if k == 0 and n:
                    pe.wait_ge(s_mcol, n // 8)
                for j in range(4):
                    if n < KD:
                        rhs = ar[:, M_RING + n * SLOT + j * 512:M_RING + n * SLOT + (j + 1) * 512]
                    else:
                        i = (n - KD) % MOD_SLOTS
                        t, a = ((gtb, j * 512), (ar, MS1 + j * QNW), (ar, MS2 + j * 512))[i]
                        rhs = t[:, a:a + 512]
                    last = mm(bank(2, 32 * j, 32), scm[:, k * 32:(k + 1) * 32], rhs, k == 0, k == 7)
                last.then_inc(s_mused, 1)

            def mod_transpose(g):
                pe.wait_ge(s_mrow, g + 1)
                for t in range(4):
                    last = tr(bank(2, col=t * P, w=P), modrow[:, g * 512 + t * P:g * 512 + (t + 1) * P])
                last.then_inc(s_mT, 1)

            for n in range(KD):
                mod_mult(n)

            for l in range(L):
                z = Z[l]
                def gates(sec, sent, banks, which=range(4)):
                    for n in which:
                        s, jj = n // 2, n % 2
                        j = 2 * (sec % 2) + jj
                        mm(bank(banks[n]), view(ident, 0, P, 32 * j + s, (0, P)),
                           modrow[:, l * 1536 + sec // 2 * 512:l * 1536 + sec // 2 * 512 + 512]).then_inc(z[sent], 1)

                for n in range(TT * 2):
                    t, g = n // 2, n % 2
                    if l == 0 and n == 4:
                        mod_transpose(0)
                    pe.wait_ge(z["xn"], t + 1)
                    if n >= 4:
                        pe.wait_ge(z["htev" if g == 0 else "htevd"], t - 1)
                    for c in range(4):
                        a = XN + t * D + (4 * g + c) * P
                        last = tr(bank(4 + n % 4, col=c * P, w=P), ar[:, a:a + P])
                    last.then_inc(z["ht"], 1)
                tiles, mj = TILES[l], 0

                def job(kind, i, r):
                    nonlocal mj
                    t = tiles[i]
                    first = kind == "Q" and i == 0
                    b = 7 - r if first else 7
                    if not first:
                        pe.wait_ge(z["me"], mj)
                    qn = QN + t * QNW
                    if kind == "Q":
                        blocks = [[("A", 0, P), ("A", P, P), ("C1", 0, P), ("C1", P, P)],
                                  [("B", 96 * h, 96) for h in range(4)], [("D", 0, P), ("D", P, P)]][r]
                        for c, (name, a, w) in enumerate(blocks):
                            a += qn + QN_AT[name]
                            last = tr(bank(b, 0, w, c * P, P), ar[:, a:a + w])
                    elif kind == "T":
                        pe.wait_ge(z["Cn"], i + 1)
                        for c in range(2):
                            a = OS + c * P
                            last = tr(bank(b, col=c * P, w=P), ar[:, a:a + P])
                    else:
                        if i == 0 and r == 0:
                            pe.wait_ge(z["wo"], 80 * (l + 1))
                        pe.wait_ge(z["Og"], 4 * (i + 1))
                        for k in range(KD):
                            a = WOUT + k * D + r * 512
                            last = mm(bank(b), ar[:, qn + k * P:qn + (k + 1) * P], ar[:, a:a + 512], k == 0, k == KD - 1)
                    last.then_inc(z["mj"], 1)
                    mj += 1

                pe.wait_ge(z["htev"], TT)
                pe.wait_ge(z["htevd"], TT)
                NB = PBANKS[l]
                for tau in range(NSTEP + 4):
                    if tau < NSTEP:
                        sec, t = STEPS[tau]
                        _, _, nq, ncol = SECTIONS[sec]
                        skip = nq if (l == L - 1 and t < TC) else 0
                        if t == 0:
                            pe.wait_ge(z[f"win{sec % 2}"], 16 * (sec // 2 + 1))
                        if tau >= NB:
                            if ACT_DONE[tau - NB]:
                                pe.wait_ge(z["pact"], int(ACT_DONE[tau - NB]))
                            if DVE_DONE[tau - NB]:
                                pe.wait_ge(z["pdve"], int(DVE_DONE[tau - NB]))
                        for k in range(KD):
                            a = WIN + sec % 2 * 4096 + k * ncol
                            h = HT0 + k * NTOK + t * P
                            if l == 0 and (tau, k) in MOD_AT:
                                mod_mult(MOD_AT[tau, k])
                            if l == 0 and k == 4 and tau in MOD_T_AT:
                                mod_transpose(MOD_T_AT[tau])
                            last = mm(bank(tau % NB, col=skip, w=ncol - skip), ar[:, h:h + P], ar[:, a + skip:a + ncol],
                                      k == 0, k == KD - 1)
                        last.then_inc(z["proj"], 1)
                    b = tau - 1
                    if 0 <= b < TT:
                        pe.wait_ge(z["bn"], b + 1)
                        if b:
                            pe.wait_ge(z["btev"], b)
                        noq = l == L - 1 and b < TC
                        if not noq:
                            for j in range(2):
                                tr(bank(5, 0, 96, j * P, P), ar[:, BN + 96 * j:BN + 96 * (j + 1)])
                        tr(bank(5, col=256, w=P), ar[:, BN + 192:BN + 320]).then_inc(z["bt"], 1)
                    b = tau - 2
                    if 0 <= b < TT:
                        pe.wait_ge(z["btev"], b + 1)
                        if b:
                            pe.wait_ge(z["bsa"], b)
                            pe.wait_ge(z["bsd"], b)
                        else:
                            pe.wait_ge(z["wb"], 32 * (l + 1))
                        noq = l == L - 1 and b < TC
                        if not noq:
                            for j in range(2):
                                mm(bank(6, w=384), ar[0:96, CQT + j * P:CQT + (j + 1) * P], wuq[0:96, j * 384:(j + 1) * 384],
                                   j == 0, j == 1)
                        mm(bank(7), ar[:, CKVT:CKVT + P], wukv[:, :]).then_inc(z["bs"], 1)
                    if tau == NSTEP:
                        pe.wait_ge(z["pact"], int(ACT_DONE[NSTEP - TT - 1]))
                        pe.wait_ge(z["pdve"], int(DVE_DONE[NSTEP - TT - 1]))
                        pe.wait_ge(z["bsd"], TT)
                        pe.wait_ge(z["bsa"], TT)
                        job("Q", 0, 1)
                        job("Q", 0, 2)
                    for i in k_jobs(tau - 1):
                        n = K_ORDER.index(i)
                        name = SECTIONS[STEPS[i][0]][0]
                        pe.wait_ge(z["kn"], n + 1)
                        if n >= 2:
                            pe.wait_ge(z["kt"], n - 1)
                        kb = KN + n % 2 * 384
                        if name == "B":
                            for h in range(4):
                                last = tr(bank(3 + n % 2, 0, 96, h * P, P), ar[:, kb + h * 96:kb + (h + 1) * 96])
                        else:
                            for h in range(2 if name == "C1" else 1):
                                last = tr(bank(3 + n % 2, col=h * P, w=P), ar[:, kb + h * P:kb + (h + 1) * P])
                        last.then_inc(z["kpe"], 1)
                pe.wait_ge(z["pact"], int(ACT_DONE[-1]))
                pe.wait_ge(z["pdve"], int(DVE_DONE[-1]))
                job("Q", 0, 0)
                pe.wait_ge(z["kt"], len(K_ORDER))
                for s, v, pv, jobs, ahead in PLANS[l]:
                    if s is not None:
                        i, slot = divmod(s, SLOTS)
                        if slot == 0:
                            pe.wait_ge(z["me"], 3 if i == 0 else 6 * i)
                        if s >= 2:
                            pe.wait_ge(z["P"], s - 1)
                        rows = 96 if 4 <= slot < 8 else P
                        qa = QT + i % 2 * SLOTS * P + slot * P
                        for k0, c0, n in runs_of(keys_of(tiles[i], slot)):
                            a = KT + KTILE[slot] * NTOK + k0
                            last = mm(psS[s % 2][:, c0:c0 + n], ar[0:rows, qa:qa + P], ar[0:rows, a:a + n])
                        last.then_inc(z["S"], 1)
                        if s == 0:
                            gates(2, "gt", (4, 5, 6, 4), range(3))
                        elif s == 1:
                            pe.wait_ge(z["gtev"], 1)
                            gates(2, "gt", (4, 5, 6, 4), range(3, 4))
                        elif s == 2:
                            pe.wait_ge(z["gtev"], 4)
                    if v is not None:
                        i, u = divmod(v, TURNS)
                        s0 = i * SLOTS + LAST_SLOT[u]
                        pe.wait_ge(z["mixed"], v + 1)
                        if 8 <= u < 12:
                            s0 -= 1
                        if v:
                            pe.wait_ge(z["PTa"], v)
                            pe.wait_ge(z["PTd"], v)
                        for n, _ in enumerate(keys_of(tiles[i], LAST_SLOT[u])):
                            a = PB + s0 % 4 * NTOK + n * P
                            last = tr(psT[:, n * P:(n + 1) * P], ar[:, a:a + P])
                        last.then_inc(z["T"], 1)
                    if pv is not None:
                        i, u = divmod(pv, TURNS)
                        pe.wait_ge(z["PTa"], pv + 1)
                        pe.wait_ge(z["PTd"], pv + 1)
                        kt = keys_of(tiles[i], LAST_SLOT[u])
                        if pv >= 4 and (u % 4 == 0 if 8 <= u < 12 else u % 4 == 1):
                            pe.wait_ge(z["Og"], i * 4 + u // 4)
                        if 8 <= u < 12:
                            for n, k in enumerate(kt):
                                a, b = PT[pv % 3] + n * P, VV + k * 768 + VCOL[u]
                                last = mm(psO[:, u % 4 * P:(u % 4 + 1) * P], ar[:, a:a + P], ar[:, b:b + P], n == 0, n == len(kt) - 1)
                            last.then_inc(z["O"], 1)
                        elif u % 2:
                            for n, k in enumerate(kt):
                                for h in range(2):
                                    a, b = PT[(pv - 1 + h) % 3] + n * P, VV + k * 768 + VCOL[u] + 64 * h
                                    last = mm(psO[64 * h:64 * h + 64, u % 4 // 2 * P:(u % 4 // 2 + 1) * P], ar[:, b:b + 64],
                                              ar[:, a:a + P], n == 0, n == len(kt) - 1)
                            last.then_inc(z["O"], 2)
                    for j in jobs:
                        job(*j)
                pe.wait_ge(z["me"], mj)
                pe.sem_inc(z["wused"], 2)

                F = FP[l]
                gates(5, "fht", (0, 1, 2, 3))
                pe.wait_ge(z["fhtev"], 4)
                tl = TILES[l]
                for n in range(len(tl) * 2):
                    t, g = tl[n // 2], n % 2
                    pe.wait_ge(z["fxn"], n // 2 + 1)
                    if 4 <= n < 8:
                        pe.wait_ge(z["fhtev"], n - 3)
                    elif n >= 8 and g == 0:
                        pe.wait_ge(z["fhtev"], n // 2 + 1)
                    elif n >= 8:
                        pe.wait_ge(z["fhtevd"], n // 2 - 3)
                    for c in range(4):
                        a = F["XN2"] + (t - F["t0"]) * D + (4 * g + c) * P
                        last = tr(bank((4 + n) % 8, col=c * P, w=P), ar[:, a:a + P])
                    last.then_inc(z["fht"], 1)
                pe.wait_ge(z["fhtev"], 4 + len(tl))
                pe.wait_ge(z["fhtevd"], len(tl))
                if l == 0:
                    pe.wait_ge(s_x, 16 * 4)
                streams = [0, 1] if l == 0 else [0]
                for s in streams:
                    c0, n = ((CTX, LAT), (0, CTX))[s]
                    c0 -= F["t0"] * P
                    for k in range(KD):
                        last = mm(bank(s, 32 * (k % 4), 32, 0, n), wrt[:, l * P + k * NE:l * P + k * NE + 32],
                                  ar[:, F["HT2"] + k * F["n"] + c0:F["HT2"] + k * F["n"] + c0 + n], k < 4, k >= 4)
                last.then_inc(z["lg"], 1)
                pe.wait_ge(z["lgev"], l + 1)
                for t in tl:
                    last = tr(bank(2 + t // 4, col=t % 4 * P, w=P), ar[:, F["LGT"] + t * P:F["LGT"] + (t + 1) * P])
                last.then_inc(z["lt"], 1)
                pe.wait_ge(z["prb"], l + 1)
                for t in tl:
                    o = bank(0, 0, NE, (t - TC) * P, P) if t >= TC else bank(1, 0, NE, t * P, P)
                    last = tr(o, ar[:, F["PRB"] + t * NE:F["PRB"] + (t + 1) * NE])
                last.then_inc(z["at"], 1)
                for n in range(2):
                    pe.wait_ge(z["dup"], 2 * l + n + 1)
                    tr(bank(5 + n, 0, P, 0, 48), ar[0:48, F["DUP"] + n * P:F["DUP"] + n * P + P], 48).then_inc(z["dupT"], 1)

                wc = l == 0
                JL = jobs_of_quad(wc)
                NJ = len(JL)
                W = SW[l]
                NX = W // P
                nact, ndve = KD, NJ - KD

                def read(q, n):
                    if JL[n][0] == "G":
                        pe.wait_ge(z["ja"], q * nact + (n - KD + 1 + KD // 2))
                    else:
                        pe.wait_ge(z["jd"], q * ndve + sum(k != "G" for k, _ in JL[:n + 1]))

                def small(q, n):
                    kind, x = JL[n]
                    if kind == "C":
                        nb_ = len(COMBINE_BANKS)
                        b = COMBINE_BANKS[(n - 16) % nb_]
                        if n - 16 >= nb_:
                            read(q, n - nb_)
                    else:
                        b = 6 + n % 2
                        if n >= 2:
                            read(q, n - 2)
                    if kind == "G":
                        for i in range(NX):
                            a = F["XG"] + i * D + x * P
                            last = tr(bank(b, col=i * P, w=P), ar[:, a:a + P])
                    elif kind == "H":
                        for i in range(NX):
                            a = F["HID"] + i * D + x * P
                            last = tr(bank(b, col=i * P, w=P), ar[:, a:a + P])
                    else:
                        t, hf = x
                        if t >= TC:
                            blocks = [(pr * LAT + (t - TC) * P, pr * D + hf * 512) for pr in range(2)]
                        else:
                            blocks = [(2 * LAT + t * P, 2 * D + hf * 512)]
                        for a, r in blocks:
                            if wc:
                                mm(bank(b), stl_r[:, a:a + P], yh_r[:, r:r + 512], a == blocks[0][0], False)
                                last = mm(bank(b), stl_r[:, a:a + P], yl_r[:, r:r + 512], False, a == blocks[-1][0])
                            else:
                                a, r = a + F["STL"], r + F["HID"]
                                last = mm(bank(b), ar[:, a:a + P], ar[:, r:r + 512], a == F["STL"] + blocks[0][0],
                                          a == F["STL"] + blocks[-1][0])
                    last.then_inc(z["jp"], 1)

                def big(q, st):
                    m, hf, kh = stage_of(st)
                    b0 = 3 * (hf if m == 2 else m)
                    src = F["HIDT"] if m == 2 else F["XST"]
                    for pr in range(2):
                        for e in (2 * pr, 2 * pr + 1):
                            pe.wait_ge(*slot_filled(l, q, st, e))
                        for k, e in ((k, 2 * pr + j) for k in range(4) for j in range(2)):
                            a = src + (kh * 4 + k) * W + e * CAP_L
                            r = RING + (st % RSTAGES[l] * QUAD + e) * SLOT + k * 512
                            last = mm(bank(b0 + e // 2, 64 * (e % 2), 64), ar[:, a:a + CAP_L], ar[:, r:r + 512],
                                      kh == 0 and k == 0, kh == 1 and k == 3)
                    if wc:
                        for k in range(4):
                            for e in range(QUAD):
                                a = src + (kh * 4 + k) * W + 256 + e * CAP_C
                                r = RING + (st % RSTAGES[l] * QUAD + e) * SLOT + k * 512
                                last = mm(bank(b0 + 2, 32 * e, 32), ar[:, a:a + CAP_C], ar[:, r:r + 512],
                                          kh == 0 and k == 0, kh == 1 and k == 3)
                    last.then_inc(z["wused"], 1)

                pe.wait_ge(z["xg"], 16 * NX)
                if RSTAGES[l] > 2:
                    pe.sem_inc(z["wused"], RSTAGES[l] - 2)
                for n in range(KD):
                    if n >= 4:
                        pe.wait_ge(z[("ja", "jg")[n % 2]], n // 2 - 1)
                    for i in range(NX):
                        a = F["XG"] + i * D + n * P
                        last = tr(bank(n % 4, col=i * P, w=P), ar[:, a:a + P])
                    last.then_inc(z["gt0"], 1)
                pe.wait_ge(z["ja"], KD // 2)
                pe.wait_ge(z["jg"], KD // 2)
                pe.sem_inc(z["want"], 1)

                def quad(q, final):
                    pe.wait_ge(z["ja"], q * nact + KD // 2)
                    pe.wait_ge(z["qd"], q + 1)
                    big(q, 0)
                    big(q, 1)
                    big(q, 2)
                    big(q, 3)
                    pe.wait_ge(z["silu"], q * 2 + 1)
                    big(q, 4)
                    big(q, 5)
                    pe.wait_ge(z["prod"], q * 2 + 1)
                    for n in range(4):
                        small(q, n)
                    big(q, 6)
                    big(q, 7)
                    pe.wait_ge(z["silu"], q * 2 + 2)
                    pe.wait_ge(z["jd"], q * ndve + 4)
                    big(q, 8)
                    pe.wait_ge(z["prod"], q * 2 + 2)
                    for n in range(4, 8):
                        small(q, n)
                    pe.wait_ge(z["jd"], q * ndve + 8)
                    big(q, 9)
                    if not final:
                        pe.wait_ge(z["xg"], q * (16 * NX) + 32 * NX)
                        for n in range(8, 16):
                            small(q, n)
                        read(q, 15)
                        pe.sem_inc(z["want"], 1)
                    big(q, 10)
                    big(q, 11)
                    half = (NJ - 16) // 2
                    pe.wait_ge(z["st"], q + 1)
                    for n in range(16, NJ):
                        if (n - 16) % half == 0:
                            pe.wait_ge(z["y"], q * 2 + ((n - 16) // half + 1))
                        small(q, n)

                with pe.Fori(0, NQ - 1) as q:
                    quad(q, False)
                quad(NQ - 1, True)
                pe.wait_ge(z["xready"], l + 1)
                pe.sem_inc(z["ffn_done"], 1)

        @block.scalar
        def _(act):
            def a_(o, i, f=ACT.Copy, **kw):
                return nc.scalar.activation(o, i, f, **kw)

            act.wait_ge(s_const, 16 * NCONST)
            a_(sc[:, :], sc[:, :], ACT.Silu).then_inc(s_silu, 1)
            act.wait_ge(s_lamx, 1)
            for l in range(L):
                a_(lam[:, l * 8 + 2:l * 8 + 4], lam[:, l * 8:l * 8 + 2], ACT.Exp).then_inc(s_lamx, 1)

            for l in range(L):
                z = Z[l]
                if l == 0:
                    act.wait_ge(s_x, 16 * 2)
                    for t in range(TT):
                        if t:
                            act.wait_ge(z["sq"], t)
                        a_(ar[:, JUNK:JUNK + D], X[:, t * D:(t + 1) * D], ACT.Square, accum_out=ss[:, t:t + 1]).then_inc(z["sq"], 1)
                tiles = TILES[l]
                mj = 0

                def job(kind, i, r):
                    nonlocal mj
                    t = tiles[i]
                    mj += 1
                    if kind == "O":
                        return
                    if kind == "Q" and i < 2 and r != 1:
                        act.wait_ge(z["qz"], 2 * l + i + 1)
                    act.wait_ge(z["mj"], mj)
                    b = 7 - r if kind == "Q" and i == 0 else 7
                    qt = QT + i % 2 * SLOTS * P
                    if kind == "T":
                        a = QN + t * QNW + 4 * P
                        last = a_(ar[:, a:a + 256], bank(b, w=256))
                    elif r == 1:
                        last = a_(ar[0:96, qt + 4 * P:qt + 8 * P], bank(b, 0, 96, 0, 512))
                    else:
                        s0 = 0 if r == 0 else 16
                        for j in range(2):
                            last = a_(view(ar, 64 * j, 64, qt + (s0 + j) * P, (2 * P, 2), (1, P)),
                                      bankv(b, 64 * j, 64, 0, (P, 2), (1, P)))
                        if r == 0:
                            for j in range(4):
                                last = a_(view(ar, 32 * j, 32, qt + (8 + j) * P, (4 * P, 2), (1, P)),
                                          bankv(b, 32 * j, 32, 256, (P, 2), (1, P)))
                    last.then_inc(z["me"], 1)

                for t in range(TT):
                    if t == 0:
                        act.wait_ge(s_eff, 1 + l)
                    act.wait_ge(z["ht"], 2 * t + 1)
                    s = 0 if t >= TC else 1
                    for k in range(4):
                        h = HT0 + k * NTOK + t * P
                        last = a_(ar[:, h:h + P], bank(4 + 2 * (t % 2), col=k * P, w=P), ACT.Identity,
                                  scale=eff[:, l * 32 + s * 8 + k:l * 32 + s * 8 + k + 1],
                                  bias=modcol[:, l * 96 + s * 8 + k:l * 96 + s * 8 + k + 1])
                    last.then_inc(z["htev"], 1)
                for tau in range(NSTEP + 4):
                    if tau < NSTEP and uses_act(*STEPS[tau]):
                        sec, t = STEPS[tau]
                        name = SECTIONS[sec][0]
                        b = tau % PBANKS[l]
                        noq = l == L - 1 and t < TC
                        act.wait_ge(z["proj"], tau + 1)
                        v = VV + t * 768
                        if name == "B":
                            if t:
                                act.wait_ge(z["bsq"], 2 * t if l == 0 else 2 * t - min(t, TC))
                            if not noq:
                                a_(ar[:, JUNK:JUNK + B_QR], bank(b, w=B_QR), ACT.Square, accum_out=ss[:, 6:7]).then_inc(z["bsq"], 1)
                            a_(ar[:, JUNK + 256:JUNK + 384], bank(b, col=B_QR, w=B_KVR), ACT.Square,
                               accum_out=ss[:, 7:8]).then_inc(z["bsq"], 1)
                            act.wait_ge(z["pdve"], t + 1)
                            act.sem_inc(z["pact"], 1)
                        elif name == "A":
                            last = a_(ar[:, v:v + P], bank(b, col=384, w=P))
                            if t < TC:
                                n = K_ORDER.index(tau)
                                act.wait_ge(z["kpe"], n - 1)
                                if not noq:
                                    a_(view(ar, 0, P, QN + t * QNW + QN_AT["A"], (64, 2), (128, 2), (1, 64)),
                                       bankv(b, 0, P, 0, (128, 2), (64, 2), (1, 64)))
                                last = a_(ar[:, KN + n % 2 * 384:KN + n % 2 * 384 + P], bank(b, col=256, w=P))
                            last.then_inc(z["pact"], 1)
                            if t < TC:
                                act.wait_ge(z["pact"], int(ACT_DONE[tau]))
                                act.wait_ge(z["kn"], n)
                                act.sem_inc(z["kn"], 1)
                        elif name == "C1":
                            n = K_ORDER.index(tau)
                            act.wait_ge(z["kpe"], n - 1)
                            if not noq:
                                a_(ar[:, QN + t * QNW + QN_AT["C1"]:QN + t * QNW + QN_AT["C1"] + 256], bank(b, w=256))
                            a_(ar[:, KN + n % 2 * 384:KN + n % 2 * 384 + 256], bank(b, col=256, w=256)).then_inc(z["pact"], 1)
                            act.wait_ge(z["pact"], int(ACT_DONE[tau]))
                            act.wait_ge(z["kn"], n)
                            act.sem_inc(z["kn"], 1)
                        elif name == "C2":
                            a_(ar[:, v + 384:v + 640], bank(b, w=256)).then_inc(z["pact"], 1)
                        else:
                            a_(ar[:, v + 640:v + 768], bank(b, col=384, w=P))
                            q0 = 256 if noq else 0
                            if t:
                                act.wait_ge(z["dsq"], 2 * t)
                            a_(ar[:, SQ + q0:SQ + 384], bank(b, col=q0, w=384 - q0), ACT.Square).then_inc(z["dsq"], 1)
                            act.wait_ge(z["dsq"], 2 * t + 1)
                            act.sem_inc(z["pact"], 1)
                    b = tau - 1
                    if 0 <= b < TT:
                        act.wait_ge(z["bt"], b + 1)
                        if b:
                            act.wait_ge(z["bs"], b)
                        if not (l == L - 1 and b < TC):
                            for j in range(2):
                                a_(ar[0:96, CQT + j * P:CQT + (j + 1) * P], bank(5, 0, 96, j * P, P), ACT.Identity,
                                   scale=bgcol[0:96, l * 3 + j:l * 3 + j + 1])
                        a_(ar[:, CKVT:CKVT + P], bank(5, col=256, w=P), ACT.Identity,
                           scale=bgcol[:, l * 3 + 2:l * 3 + 3]).then_inc(z["btev"], 1)
                    b = tau - 2
                    if 0 <= b < TT:
                        n = K_ORDER.index(b)
                        act.wait_ge(z["bs"], b + 1)
                        if n >= 2:
                            act.wait_ge(z["kpe"], n - 1)
                        a_(view(ar, 0, P, KN + n % 2 * 384, (96, 4), (1, 64)), bankv(7, 0, P, 0, (128, 4), (1, 64)))
                        a_(view(ar, 0, P, VV + b * 768 + 128, (64, 4), (1, 64)), bankv(7, 0, P, 64, (128, 4), (1, 64))).then_inc(z["bsa"], 1)
                    if tau == NSTEP:
                        job("Q", 0, 1)
                        job("Q", 0, 2)
                    for i in k_jobs(tau - 1):
                        n = K_ORDER.index(i)
                        sec, t = STEPS[i]
                        name = SECTIONS[sec][0]
                        kb = 3 + n % 2
                        act.wait_ge(z["kpe"], n + 1)
                        if name == "B":
                            last = a_(view(ar, 0, 96, KT + NTOK + t * P, (NTOK, 4), (1, P)), bankv(kb, 0, 96, 0, (P, 4), (1, P)))
                        elif name == "C1":
                            last = a_(view(ar, 0, P, KT + 5 * NTOK + t * P, (NTOK, 2), (1, P)), bankv(kb, 0, P, 0, (P, 2), (1, P)))
                        else:
                            k0 = KT + (0 if name == "A" else 7) * NTOK + t * P
                            last = a_(ar[:, k0:k0 + P], bank(kb, w=P))
                        last.then_inc(z["kt"], 1)
                job("Q", 0, 0)
                def squares(i):
                    act.wait_ge(z["me"], 6 * (i + 1))
                    t = tiles[i]
                    a = QN + t * QNW if i < len(tiles) - 1 else WOUT + 6 * D
                    a_(ar[:, a:a + D], X[:, t * D:(t + 1) * D], ACT.Square, accum_out=ss[:, t:t + 1]).then_inc(z["fxn_sq"], 1)

                for s, v, pv, jobs, ahead in PLANS[l]:
                    if v is not None:
                        i, u = divmod(v, TURNS)
                        act.wait_ge(z["T"], v + 1)
                        if v >= 3:
                            act.wait_ge(z["O"], v - 2)
                        w = min(len(keys_of(tiles[i], LAST_SLOT[u])), 4) * P
                        a = PT[v % 3]
                        a_(ar[:, a:a + w], psT[:, 0:w]).then_inc(z["PTa"], 1)
                    if s is not None:
                        i, slot = divmod(s, SLOTS)
                        par = i % 2 * SLOTS + slot
                        act.wait_ge(z["nb"], s + 1)
                        if s >= 4:
                            i4, s4 = divmod(s - 4, SLOTS)
                            u4 = next(u for u, x in enumerate(LAST_SLOT) if x >= s4)
                            act.wait_ge(z["T"], i4 * TURNS + u4 + 1)
                        n = len(keys_of(tiles[i], slot)) * P
                        a = PB + s % 4 * NTOK
                        if slot < 4:
                            a_(esk[:, i % 2 * 4 + slot:i % 2 * 4 + slot + 1], sink[:, l * 8 + slot:l * 8 + slot + 1], ACT.Exp,
                               bias=nb[:, par:par + 1])
                        a_(ar[:, a:a + n], psS[s % 2][:, 0:n], ACT.Exp, bias=nb[:, par:par + 1], scale=SCALE[slot],
                           accum_out=rs[:, par:par + 1]).then_inc(z["P"], 1)
                        if slot == 10 and i:
                            squares(i - 1)
                        for g in {0: (0, 1, 2), 1: (3,)}.get(s, ()):
                            act.wait_ge(z["gt"], g + 1)
                            a_(gtb[:, g * 512:(g + 1) * 512], bank((4, 5, 6, 4)[g])).then_inc(z["gtev"], 1)
                    for j in jobs:
                        job(*j)
                tl = TILES[l]
                F, W = FP[l], SW[l]
                squares(len(tl) - 1)
                for n in range(4):
                    act.wait_ge(z["fht"], n + 1)
                    a_(gtb[:, n * 512:(n + 1) * 512], bank(n)).then_inc(z["fhtev"], 1)
                for n, t in enumerate(tl):
                    act.wait_ge(z["fht"], 4 + 2 * n + 1)
                    s = 0 if t >= TC else 1
                    x = F["XN2"] + (t - F["t0"]) * D
                    act.dma_start(rows[t * P:(t + 1) * P, :], ar[:, x:x + D]).then_inc(s_xd, 16)
                    for k in range(4):
                        h = F["HT2"] + k * F["n"] + (t - F["t0"]) * P
                        last = a_(ar[:, h:h + P], bank((4 + 2 * n) % 8, col=k * P, w=P), ACT.Identity,
                                  scale=eff[:, l * 32 + 16 + s * 8 + k:l * 32 + 16 + s * 8 + k + 1],
                                  bias=modcol[:, l * 96 + 48 + s * 8 + k:l * 96 + 48 + s * 8 + k + 1])
                    last.then_inc(z["fhtev"], 1)
                act.wait_ge(z["pe_ex"], 2 * l + 1)
                c0 = tl[0] * NE
                a_(ar[:, F["PRB"] + c0:F["PRB"] + TT * NE], ar[:, F["PRB"] + c0:F["PRB"] + TT * NE], ACT.Exp).then_inc(z["pe_ex"], 1)
                wc = l == 0
                NJ = len(jobs_of_quad(wc))
                R = RSTAGES[l]

                def modulated(x, b):
                    a = F["XST"] + x * W
                    k = l * 32 + 16 + x
                    m = l * 96 + 48 + x
                    if wc:
                        a_(ar[:, a + 256:a + 384], bank(b, col=256, w=P), ACT.Identity, scale=eff[:, k + 8:k + 9],
                           bias=modcol[:, m + 8:m + 9])
                    a_(ar[:, a:a + 256], bank(b, w=256), ACT.Identity, scale=eff[:, k:k + 1],
                       bias=modcol[:, m:m + 1]).then_inc(z["ja"], 1)

                def gated(q, hf):
                    act.wait_ge(z["wused"], q * 12 + (R + 2 + 4 * hf))
                    for i in range(W // P):
                        a = F["HID"] + i * D + hf * 512
                        last = a_(ar[:, a:a + 512], bank(i), ACT.Silu)
                    last.then_inc(z["silu"], 1)

                def rounded(q):
                    for n in range(2 * W // P if wc else 0):
                        a = n % (W // P) * D + n // (W // P) * 512
                        act.wait_ge(yf, q * (2 * W // P) + (n + 1))
                        a_(yh_r[:, a:a + 512], ar[:, F["HID"] + a:F["HID"] + a + 512]).then_inc(yh, 1)

                for x in range(0, KD, 2):
                    act.wait_ge(z["gt0"], x + 1)
                    modulated(x, x % 4)
                with act.Fori(0, NQ - 1) as q:
                    gated(q, 0)
                    gated(q, 1)
                    for x in range(KD):
                        act.wait_ge(z["jp"], q * NJ + (KD + x + 1))
                        modulated(x, 6 + x % 2)
                    rounded(q)
                gated(NQ - 1, 0)
                gated(NQ - 1, 1)
                rounded(NQ - 1)
                done = Z[l + 1]["sq"] if l < L - 1 else s_fin0
                for n, t in enumerate(tl):
                    nd = NJ - KD
                    act.wait_ge(z["jd"], (NQ - 1) * nd + KD + len(tl) + n + 1)
                    if n:
                        act.wait_ge(done, n)
                    c = t if l < L - 1 else n
                    a_(ar[:, F["HIDT"]:F["HIDT"] + D], X[:, t * D:(t + 1) * D], ACT.Square,
                       accum_out=ss[:, c:c + 1]).then_inc(done, 1)

        @block.vector
        def _(dve):
            chain = [0]
            powers = [0]
            V = nc.vector

            def link(ins):
                chain[0] += 1
                ins.then_inc(s_dve, 1)
                dve.wait_ge(s_dve, chain[0])

            def rsqrt_begin(sums, n, count):
                link(V.tensor_scalar(pw[:, 0:n], sums, 1.0 / count, EPS, ALU.mult, ALU.add))
                powers[0] += 1
                dve.sem_inc(s_pin, 1)

            def rsqrt_end(n):
                dve.wait_ge(s_pout, powers[0])
                link(V.tensor_tensor(pwa[:, 0:n], pw[:, 0:n], pw[:, 8:8 + n], ALU.mult))
                link(V.scalar_tensor_tensor(pwa[:, 0:n], pwa[:, 0:n], -0.5, pw[:, 8:8 + n], ALU.mult, ALU.mult))
                link(V.scalar_tensor_tensor(pwr[:, 0:n], pwa[:, 0:n], 1.5, pw[:, 8:8 + n], ALU.add, ALU.mult))

            def rsqrt(sums, n, count):
                rsqrt_begin(sums, n, count)
                rsqrt_end(n)

            link(V.memset(pw[:, 0:16], 1.0))
            link(V.memset(pw[:, 16:24], -0.5))
            link(V.memset(scm[:, :], 0.0))
            dve.wait_ge(s_silu, 1)
            V.tensor_copy(view(scm, 0, P, 0, (1, 2), (32, KD)), view(sc, 0, P, 0, (KD, 2), (1, KD))).then_inc(s_scm, 1)
            for l in range(L):
                for j in range(2):
                    link(V.tensor_tensor(view(ar, 0, P, LAMP + l * 128 + 64 * j, (1, 32)), view(ar, 0, P, LAMP + l * 128 + 64 * j, (1, 32)),
                                         view(ar, 0, P, LAMP + l * 128 + 64 * j + 32, (1, 32)), ALU.mult))
                    link(V.reduce_sum(lam[:, l * 8 + j:l * 8 + j + 1], ar[:, LAMP + l * 128 + 64 * j:LAMP + l * 128 + 64 * j + 32], axis=AX.X))
            dve.sem_inc(s_lamx, 1)
            dve.wait_ge(s_lamx, 1 + L)
            for l in range(L):
                init = 0.8 - 0.6 * math.exp(-0.3 * l)
                link(V.tensor_tensor(lam[:, l * 8 + 4:l * 8 + 5], lam[:, l * 8 + 3:l * 8 + 4], lam[:, l * 8 + 2:l * 8 + 3], ALU.subtract))
                link(V.tensor_scalar(lam[:, l * 8 + 5:l * 8 + 6], lam[:, l * 8 + 4:l * 8 + 5], -init, None, ALU.add))
                link(V.tensor_scalar(gC[:, l * 64:l * 64 + 64], gC[:, l * 64:l * 64 + 64], 1 - init, None, ALU.mult))
                link(V.tensor_copy(view(sink, 0, P, l * 8, (2, 2), (1, 2)), view(sinkn, 0, P, l * 4, (1, 2), (2, 2))))
                link(V.tensor_scalar(sink[:, l * 8 + 4:l * 8 + 8], sink[:, l * 8:l * 8 + 4], -1.0, None, ALU.mult))

            def mod_rows(g):
                dve.wait_ge(s_bm, 16 * 8)
                dve.wait_ge(s_mused, KD * (g + 1))
                V.tensor_tensor(modrow[:, g * 512:(g + 1) * 512], modrow[:, g * 512:(g + 1) * 512], bank(2),
                                ALU.add).then_inc(s_mrow, 1)

            def mod_columns(g):
                l, r = divmod(g, 3)
                dve.wait_ge(s_mT, g + 1)
                for s in range(2):
                    last = V.tensor_copy(view(modcol, 0, P, l * 96 + 2 * r * 16 + s * 8, (16, 2), (4, 2), (1, 4)),
                                         bankv(2, 0, P, s, (64, 2), (32, 2), (P, 4)))
                last.then_inc(s_mcol, 1)
                if r != 1:
                    f = r // 2
                    dve.wait_ge(s_mcol, g + 1)
                    link(V.scalar_tensor_tensor(view(eff, 0, P, l * 32 + f * 16, (8, 2), (1, 8)),
                                                view(modcol, 0, P, l * 96 + (1 + 3 * f) * 16, (8, 2), (1, 8)), 1.0,
                                                view(gcol, 0, P, l * 16 + f * 8, (0, 2), (1, 8)), ALU.add, ALU.mult))
                    if f == 0:
                        dve.sem_inc(s_eff, 1)

            def rot(src, half, heads, lt):
                c = lt * 48 + (0 if half == 32 else 32)
                w = TL * 48
                V.tensor_tensor(view(ar, 0, P, T1, (2 * half, heads), (half, 2), (1, half)),
                                src(0, (2 * half, heads), (half, 2), (1, half)),
                                view(rope, 0, P, c, (0, heads), (0, 2), (1, half)), ALU.mult)
                V.tensor_tensor(view(ar, 0, P, T2, (2 * half, heads), (1, half)), src(half, (2 * half, heads), (1, half)),
                                view(rope, 0, P, 2 * w + c, (0, heads), (1, half)), ALU.mult)
                link(V.tensor_tensor(view(ar, 0, P, T2 + half, (2 * half, heads), (1, half)), src(0, (2 * half, heads), (1, half)),
                                     view(rope, 0, P, w + c, (0, heads), (1, half)), ALU.mult))

            for l in range(L):
                z = Z[l]
                dve.wait_ge(z["sq"], TT)
                rsqrt(ss[:, 0:TT], TT, D)
                for t in range(TT):
                    V.tensor_scalar(ar[:, XN + t * D:XN + (t + 1) * D], X[:, t * D:(t + 1) * D], pwr[:, t:t + 1], None,
                                    ALU.mult).then_inc(z["xn"], 1)
                if l == 0:
                    mod_rows(0)
                    mod_columns(0)
                for t in range(TT):
                    dve.wait_ge(z["ht"], 2 * t + 2)
                    s = 0 if t >= TC else 1
                    for k in range(4, 8):
                        h = HT0 + k * NTOK + t * P
                        last = V.tensor_scalar(ar[:, h:h + P], bank(5 + 2 * (t % 2), col=(k - 4) * P, w=P),
                                               eff[:, l * 32 + s * 8 + k:l * 32 + s * 8 + k + 1],
                                               modcol[:, l * 96 + s * 8 + k:l * 96 + s * 8 + k + 1], ALU.mult, ALU.add)
                    last.then_inc(z["htevd"], 1)
                dve.wait_ge(z["ht"], 2 * TT)
                for tau in range(NSTEP + 4):
                    if l == 0 and tau in MOD_ADD_AT:
                        mod_rows(MOD_ADD_AT[tau])
                    if l == 0 and tau in MOD_T_AT:
                        mod_columns(MOD_T_AT[tau])
                    if tau < NSTEP and uses_dve(*STEPS[tau]):
                        sec, t = STEPS[tau]
                        name = SECTIONS[sec][0]
                        b, lt = tau % PBANKS[l], t - TC
                        noq = l == L - 1 and t < TC
                        dve.wait_ge(z["proj"], tau + 1)
                        if name == "A":
                            dve.wait_ge(z["pact"], int(ACT_DONE[tau]))

                        def src(col, *dims, b=b):
                            return bankv(b, 0, P, col, *dims)

                        if name == "B":
                            dve.wait_ge(z["bsq"], 2 * (t + 1) if l == 0 else 2 * (t + 1) - min(t + 1, TC))
                            if not noq:
                                link(V.tensor_scalar(ss[:, 8:9], ss[:, 6:7], B_KVR / B_QR, None, ALU.mult))
                            else:
                                link(V.tensor_copy(ss[:, 8:9], ss[:, 7:8]))
                            link(V.tensor_copy(ss[:, 9:10], ss[:, 7:8]))
                            rsqrt(ss[:, 8:10], 2, B_KVR)
                            if t:
                                dve.wait_ge(z["bt"], t)
                            if not noq:
                                link(V.tensor_scalar(ar[:, BN:BN + B_QR], bank(b, w=B_QR), pwr[:, 0:1], None, ALU.mult))
                            link(V.tensor_scalar(ar[:, BN + B_QR:BN + 320], bank(b, col=B_QR, w=B_KVR), pwr[:, 1:2], None, ALU.mult))
                            dve.sem_inc(z["bn"], 1)
                            kr = KR + t % 3 * 32
                            if t >= TC:
                                rot(lambda col, *dims: src(320 + col, *dims), 16, 1, lt)
                                link(V.tensor_tensor(ar[:, kr:kr + 32], ar[:, T1:T1 + 32], ar[:, T2:T2 + 32], ALU.add))
                            else:
                                link(V.tensor_copy(ar[:, kr:kr + 32], bank(b, col=320, w=32)))
                            dve.sem_inc(z["pdve"], 1)
                        else:
                            heads, half = (16, 16) if name == "C1" else (6, 32)
                            nk = 256 if name == "C1" else 128
                            n = K_ORDER.index(tau)
                            kb = KN + n % 2 * 384
                            if name == "D":
                                q0 = 256 if noq else 0
                                hq = q0 // 64
                                dve.wait_ge(z["dsq"], 2 * t + 1)
                                if noq:
                                    link(V.memset(ss[:, 10:14], 64.0))
                                link(V.tensor_reduce(ss[:, 10 + hq:16], view(ar, 0, P, SQ + q0, (64, 6 - hq), (1, 64)), AX.X, ALU.add))
                                dve.sem_inc(z["dsq"], 1)
                                rsqrt_begin(ss[:, 10:16], 6, HD)
                                link(V.tensor_tensor(ar[:, T0 + q0:T0 + 384], bank(b, col=q0, w=384 - q0),
                                                     gD[:, l * 384 + q0:l * 384 + 384], ALU.mult))
                                rsqrt_end(6)
                                link(V.tensor_tensor(view(ar, 0, P, T0 + q0, (64, 6 - hq), (1, 64)), view(ar, 0, P, T0 + q0, (64, 6 - hq), (1, 64)),
                                                     view(pwr, 0, P, hq, (1, 6 - hq), (0, 64)), ALU.mult))

                                def src(col, *dims):
                                    return view(ar, 0, P, T0 + col, *dims)

                            if t >= TC:
                                rot(src, half, heads, lt)
                                in0, in1 = (lambda c, *d: view(ar, 0, P, T1 + c, *d)), (lambda c, *d: view(ar, 0, P, T2 + c, *d))
                            if n >= 2:
                                dve.wait_ge(z["kpe"], n - 1)
                            qa = QN + t * QNW + QN_AT[name]
                            if name == "C1":
                                qv, iv = (view(ar, 0, P, qa, (1, 256)), (0, (1, 256)))
                            else:
                                qv, iv = (view(ar, 0, P, qa, (64, 2), (128, 2), (1, 64)), (0, (128, 2), (64, 2), (1, 64)))
                            if t >= TC:
                                link(V.tensor_tensor(qv, in0(*iv), in1(*iv), ALU.add))
                                link(V.tensor_tensor(ar[:, kb:kb + nk], in0(256, (1, nk)), in1(256, (1, nk)), ALU.add))
                            else:
                                if not noq:
                                    link(V.tensor_copy(qv, src(*iv)))
                                link(V.tensor_copy(ar[:, kb:kb + nk], src(256, (1, nk))))
                            dve.sem_inc(z["pdve"], 1)
                            if n:
                                dve.wait_ge(z["kn"], n)
                            dve.sem_inc(z["kn"], 1)
                    b = tau - 2
                    if 0 <= b < TT:
                        n = K_ORDER.index(b)
                        noq = l == L - 1 and b < TC
                        dve.wait_ge(z["bs"], b + 1)
                        qa = QN + b * QNW + QN_AT["B"] + 64
                        if not noq:
                            link(V.tensor_copy(view(ar, 0, P, qa - 64, (96, 4), (1, 64)), bankv(6, 0, P, 0, (96, 4), (1, 64))))
                        if b >= TC:
                            rot(lambda col, *dims: bankv(6, 0, P, 64 + col, (96, 4), *dims[1:]), 16, 4, b - TC)
                            link(V.tensor_tensor(view(ar, 0, P, qa, (96, 4), (1, 32)), view(ar, 0, P, T1, (32, 4), (1, 32)),
                                                 view(ar, 0, P, T2, (32, 4), (1, 32)), ALU.add))
                        elif not noq:
                            link(V.tensor_copy(view(ar, 0, P, qa, (96, 4), (1, 32)), bankv(6, 0, P, 64, (96, 4), (1, 32))))
                        if n >= 2:
                            dve.wait_ge(z["kpe"], n - 1)
                        link(V.tensor_copy(view(ar, 0, P, KN + n % 2 * 384 + 64, (96, 4), (1, 32)),
                                           view(ar, 0, P, KR + b % 3 * 32, (0, 4), (1, 32))))
                        dve.sem_inc(z["bsd"], 1)
                        dve.wait_ge(z["bsa"], b + 1)
                        if n:
                            dve.wait_ge(z["kn"], n)
                        dve.sem_inc(z["kn"], 1)
                tiles, mj = TILES[l], 0

                def job(kind, i, r):
                    nonlocal mj
                    t = tiles[i]
                    mj += 1
                    if kind == "O":
                        dve.wait_ge(z["mj"], mj)
                        g = (0 if t >= TC else 1) * D + r * 512
                        link(V.tensor_tensor(bank(7), bank(7), gtb[:, g:g + 512], ALU.mult))
                        x = t * D + r * 512
                        V.tensor_tensor(X[:, x:x + 512], X[:, x:x + 512], bank(7), ALU.add).then_inc(z["me"], 1)

                mj = 3
                for s, v, pv, jobs, ahead in PLANS[l]:
                    if ahead is not None:
                        i, u = divmod(ahead, TURNS)
                        s1 = i * SLOTS + LAST_SLOT[u]
                        p1 = i % 2 * SLOTS + LAST_SLOT[u]
                        n = len(keys_of(tiles[i], LAST_SLOT[u])) * P
                        b = PB + s1 % 4 * NTOK
                        dve.wait_ge(z["P"], s1 + 1)
                        if u < 4:
                            link(V.tensor_tensor(rs[:, p1:p1 + 1], rs[:, p1:p1 + 1], esk[:, i % 2 * 4 + u:i % 2 * 4 + u + 1], ALU.add))
                        link(V.reciprocal(rr[:, p1:p1 + 1], rs[:, p1:p1 + 1]))
                        if 8 <= u < 12:
                            link(V.scalar_tensor_tensor(kk[:, 0:1], rr[:, p1:p1 + 1], lam[:, l * 8 + 5:l * 8 + 6], rs[:, p1 - 1:p1],
                                                        ALU.mult, ALU.mult))
                            a = PB + (s1 - 1) % 4 * NTOK
                            V.scalar_tensor_tensor(ar[:, a:a + n], ar[:, b:b + n], kk[:, 0:1], ar[:, a:a + n],
                                                   ALU.mult, ALU.add).then_inc(z["mixed"], 1)
                        else:
                            V.tensor_scalar(ar[:, b:b + n], ar[:, b:b + n], rr[:, p1:p1 + 1], None, ALU.mult).then_inc(z["mixed"], 1)
                    if s is not None:
                        i, slot = divmod(s, SLOTS)
                        par = i % 2 * SLOTS + slot
                        kt = keys_of(tiles[i], slot)
                        n = len(kt) * P
                        S = psS[s % 2]
                        dve.wait_ge(z["S"], s + 1)
                        if slot < 4 and tiles[i] >= TC:
                            b = tiles[i] - TC
                            if 0 < b < TL - 1:
                                link(V.tensor_tensor(view(S, 0, P, 256, (256, 2), (1, P)), view(S, 0, P, 256, (256, 2), (1, P)),
                                                     view(mask, 0, P, 0, (P, 2), (1, P)), ALU.add))
                            elif b > 0:
                                link(V.tensor_tensor(S[:, 256:384], S[:, 256:384], mask[:, 0:P], ALU.add))
                            else:
                                link(V.tensor_tensor(S[:, n - P:n], S[:, n - P:n], mask[:, P:2 * P], ALU.add))
                        link(V.reduce_max(mx[:, par:par + 1], S[:, 0:n], axis=AX.X))
                        if slot < 4:
                            V.tensor_scalar(nb[:, par:par + 1], mx[:, par:par + 1], -SCALE[slot], sink[:, l * 8 + 4 + slot:l * 8 + 5 + slot],
                                            ALU.mult, ALU.min).then_inc(z["nb"], 1)
                        else:
                            V.tensor_scalar(nb[:, par:par + 1], mx[:, par:par + 1], -SCALE[slot], None, ALU.mult).then_inc(z["nb"], 1)
                    if v is not None:
                        i, u = divmod(v, TURNS)
                        dve.wait_ge(z["T"], v + 1)
                        if v >= 3:
                            dve.wait_ge(z["O"], v - 2)
                        w = len(keys_of(tiles[i], LAST_SLOT[u])) * P
                        a = PT[v % 3]
                        if w > 512:
                            V.tensor_copy(ar[:, a + 512:a + w], psT[:, 512:w]).then_inc(z["PTd"], 1)
                        else:
                            dve.sem_inc(z["PTd"], 1)
                    if pv is not None and pv % 4 == 3:
                        i, u = divmod(pv, TURNS)
                        g = u // 4
                        p0 = i % 2 * SLOTS
                        dve.wait_ge(z["O"], pv + 1)
                        if g == 2:
                            if i:
                                dve.wait_ge(z["mj"], jobs_through_values(PLANS[l], i - 1))
                            link(V.reciprocal(view(rr, 0, P, p0 + 8, (2, 4)), view(rs, 0, P, p0 + 8, (2, 4))))
                            V.tensor_tensor(view(ar, 0, P, OS, (128, 2), (64, 2), (1, 64)),
                                            bankv(6, 0, P, 0, (256, 2), (192, 2), (1, 64)),
                                            view(rr, 0, P, p0 + 8, (4, 2), (2, 2), (0, 64)), ALU.mult).then_inc(z["Og"], 1)
                        else:
                            o = QN + tiles[i] * QNW + 2 * g * P
                            V.tensor_copy(ar[:, o:o + 256], bank(6, w=256)).then_inc(z["Og"], 1)
                        if g == 2:
                            dve.wait_ge(z["Og"], 4 * i + 3)
                            link(V.tensor_tensor(tmp[:, 0:256], ar[:, OS:OS + 256], ar[:, OS:OS + 256], ALU.mult))
                            link(V.tensor_reduce(ss[:, 8:12], view(ar, 0, P, TMP, (64, 4), (1, 64)), AX.X, ALU.add))
                            rsqrt_begin(ss[:, 8:12], 4, HD)
                    if pv is not None and pv % TURNS == 12:
                        o = OS
                        rsqrt_end(4)
                        link(V.tensor_tensor(view(ar, 0, P, o, (64, 4), (1, 64)), view(ar, 0, P, o, (64, 4), (1, 64)),
                                             view(pwr, 0, P, 0, (1, 4), (0, 64)), ALU.mult))
                        link(V.tensor_tensor(view(ar, 0, P, o, (64, 4), (1, 64)), view(ar, 0, P, o, (64, 4), (1, 64)),
                                             view(gC, 0, P, l * 64, (0, 4), (1, 64)), ALU.mult))
                        dve.sem_inc(z["Cn"], 1)
                    for j in jobs:
                        job(*j)
                tl = TILES[l]
                t0 = tl[0]
                F = FP[l]
                PRB, AFF, VAL, DUP, LGT, LG4 = (F[n] for n in ("PRB", "AFF", "VAL", "DUP", "LGT", "LG4"))
                dve.wait_ge(z["fxn_sq"], len(tl))
                rsqrt(ss[:, t0:TT], len(tl), D)
                for n, t in enumerate(tl):
                    V.tensor_scalar(ar[:, F["XN2"] + (t - t0) * D:F["XN2"] + (t - t0 + 1) * D], X[:, t * D:(t + 1) * D], pwr[:, n:n + 1], None,
                                    ALU.mult).then_inc(z["fxn"], 1)
                for n, t in enumerate(tl):
                    dve.wait_ge(z["fht"], 4 + 2 * n + 2)
                    s = 0 if t >= TC else 1
                    for k in range(4, 8):
                        h = F["HT2"] + k * F["n"] + (t - t0) * P
                        last = V.tensor_scalar(ar[:, h:h + P], bank((5 + 2 * n) % 8, col=(k - 4) * P, w=P),
                                               eff[:, l * 32 + 16 + s * 8 + k:l * 32 + 16 + s * 8 + k + 1],
                                               modcol[:, l * 96 + 48 + s * 8 + k:l * 96 + 48 + s * 8 + k + 1], ALU.mult, ALU.add)
                    last.then_inc(z["fhtevd"], 1)
                dve.wait_ge(z["lg"], l + 1)
                if l == 0:
                    V.tensor_copy(ar[:, LGT:LGT + CTX], bank(1, w=CTX))
                V.tensor_copy(ar[:, LGT + CTX:LGT + NTOK], bank(0)).then_inc(z["lgev"], 1)
                dve.wait_ge(z["lt"], l + 1)
                nt = len(tl)

                def pv3(a):
                    return view(ar, 0, P, a + t0 * NE, (NE, nt), (1, NE))

                def bc3(c):
                    return view(ar, 0, P, TMP + c, (1, nt), (0, NE))

                V.tensor_reduce(view(ar, 0, P, LG4 + t0 * NE, (NE, TL - t0), (1, NE)), bankv(2, 0, P, t0 * P, (P, TL - t0), (1, NE), (32, 4)),
                                AX.X, ALU.add)
                link(V.tensor_reduce(view(ar, 0, P, LG4 + TL * NE, (NE, TT - TL), (1, NE)), bankv(3, 0, P, 0, (P, TT - TL), (1, NE), (32, 4)),
                                     AX.X, ALU.add))
                lt_ = view(ar, 0, P, LG4 + t0 * NE, (NE, nt), (1, NE))
                link(V.tensor_reduce(tmp[:, 0:nt], lt_, AX.X, ALU.max))
                link(V.tensor_tensor(pv3(PRB), lt_, bc3(0), ALU.subtract))
                dve.sem_inc(z["pe_ex"], 1)
                dve.wait_ge(z["pe_ex"], 2 * l + 2)
                link(V.tensor_reduce(tmp[:, 8:8 + nt], pv3(PRB), AX.X, ALU.add))
                link(V.reciprocal(tmp[:, 16:16 + nt], tmp[:, 8:8 + nt]))
                V.tensor_tensor(pv3(PRB), pv3(PRB), bc3(16), ALU.mult).then_inc(z["prb"], 1)
                link(V.memset(ar[0:48, AFF:AFF + LAT], -1.0))
                link(V.memset(ar[0:48, DUP:DUP + 2 * P], 0.0))
                dve.wait_ge(z["at"], l + 1)
                link(V.tensor_copy(ar[0:NE, AFF:AFF + LAT], bank(0, 0, NE, 0, LAT)))
                if l == 0:
                    link(V.tensor_copy(ar[32:48, AFF:AFF + CTX], bank(1, 0, NE, 0, CTX)))
                for r in range(CAP_L // 8):
                    v8 = ar[0:48, VAL + 8 * r:VAL + 8 * r + 8]
                    link(V.max(v8, ar[0:48, AFF:AFF + LAT]))
                    last = V.max_index(idx[0:48, 8 * r:8 * r + 8], v8, ar[0:48, AFF:AFF + LAT])
                    if r < CAP_L // 8 - 1:
                        last = V.match_replace(ar[0:48, AFF:AFF + LAT], v8, ar[0:48, AFF:AFF + LAT], -2.0)
                    link(last)
                for n, dst in enumerate((LI, LG)):
                    o = DUP + n * P
                    srcs = [idx[0:NE, :], idx[32:48, :]] if n == 0 else [ar[0:NE, VAL:VAL + 64], ar[32:48, VAL:VAL + 64]]
                    for j in range(2):
                        last = V.tensor_copy(ar[0:NE, o + 64 * j:o + 64 * j + 64], srcs[0])
                    if l == 0:
                        for j in range(4):
                            last = V.tensor_copy(ar[32:48, o + 32 * j:o + 32 * j + 32], srcs[1][:, 0:32])
                    last.then_inc(z["dup"], 1)
                    dve.wait_ge(z["dupT"], 2 * l + n + 1)
                    if l == 0:
                        for j in range(4):
                            last = V.tensor_copy(view(dst, 32 * j, 32, 8, (1, 4)), bankv(5 + n, 32 * j, 32, 32 + j, (4, 4)))
                    for j in range(2):
                        last = V.tensor_copy(view(dst, 64 * j, 64, 0, (1, 8)), bankv(5 + n, 64 * j, 64, j, (2, 8)))
                    link(last)
                    if n == 0:
                        if l == 0:
                            V.tensor_copy(LIU[:, 8:12], LI[:, 8:12])
                        link(V.tensor_scalar(LIU[:, 0:8], LI[:, 0:8], float(CTX), None, ALU.add))
                        dve.sem_inc(z["want"], 1)
                dve.sem_inc(z["qd"], 1)
                wc = l == 0
                JL = jobs_of_quad(wc)
                NJ = len(JL)
                NX = SW[l] // P
                R = RSTAGES[l]
                ndve = NJ - KD
                STL, HID, HIDT = F["STL"], F["HID"], F["HIDT"]

                def selection(pairs, quads):
                    t, a = (stl_r, 0) if wc else (ar, STL)
                    for pr in range(2):
                        last = V.tensor_scalar(t[:, a + pr * LAT:a + (pr + 1) * LAT], iota[:, :], pairs(pr), None, ALU.is_equal)
                    if wc:
                        last = V.tensor_scalar(t[:, a + 2 * LAT:a + 2 * LAT + CTX], iota[:, 0:CTX], quads, None, ALU.is_equal)
                    last.then_inc(z["st"], 1)

                def quad(q, final, col):
                    def small(n):
                        kind, x = JL[n]
                        b = 6 + n % 2 if n < 16 else COMBINE_BANKS[(n - 16) % len(COMBINE_BANKS)]
                        dve.wait_ge(z["jp"], q * NJ + (n + 1 - (KD if final and n >= 16 else 0)))
                        if kind == "H":
                            ins = V.tensor_copy(ar[:, HIDT + x * SW[l]:HIDT + (x + 1) * SW[l]], bank(b, w=SW[l]))
                        else:
                            t, hf = x
                            a = t * D + hf * 512
                            ins = V.tensor_tensor(X[:, a:a + 512], X[:, a:a + 512], bank(b), ALU.add)
                        ins.then_inc(z["jd"], 1)

                    for hf in range(2):
                        dve.wait_ge(z["wused"], q * 12 + (R + 4 + 4 * hf))
                        dve.wait_ge(z["silu"], q * 2 + (hf + 1))
                        for i in range(NX):
                            a = HID + i * D + hf * 512
                            last = V.tensor_tensor(ar[:, a:a + 512], ar[:, a:a + 512], bank(3 + i), ALU.mult)
                        last.then_inc(z["prod"], 1)
                        for n in range(4):
                            small(4 * hf + n)
                    selection(lambda pr: col(LI, q * 2 + pr), col(LI, q + 8))
                    for hf in range(2):
                        dve.wait_ge(z["wused"], q * 12 + (R + 10 + 2 * hf))
                        for i in range(NX):
                            a = HID + i * D + hf * 512
                            g = (D if i == 2 else 0) + hf * 512
                            last = V.scalar_tensor_tensor(ar[:, a:a + 512], bank(3 * hf + i), col(LG, q + 8 if i == 2 else q * 2 + i),
                                                          gtb[:, g:g + 512], ALU.mult, ALU.mult)
                            if wc:
                                last.then_inc(yf, 1)
                        for i in range(NX if wc else 0):
                            a = i * D + hf * 512
                            dve.wait_ge(yh, q * (2 * NX) + (hf * NX + i + 1))
                            last = V.tensor_tensor(yl_r[:, a:a + 512], ar[:, HID + a:HID + a + 512],
                                                   yh_r[:, a:a + 512].bitcast(f32), ALU.subtract)
                        last.then_inc(z["y"], 1)
                    for n in range(16, NJ):
                        small(n)
                    dve.wait_ge(z["jd"], q * ndve + ndve)
                    dve.sem_inc(z["qd"], 1)

                for x in range(1, KD, 2):
                    dve.wait_ge(z["gt0"], x + 1)
                    a, k, m = F["XST"] + x * SW[l], l * 32 + 16 + x, l * 96 + 48 + x
                    if wc:
                        V.tensor_scalar(ar[:, a + 256:a + 384], bank(x % 4, col=256, w=P), eff[:, k + 8:k + 9],
                                        modcol[:, m + 8:m + 9], ALU.mult, ALU.add)
                    V.tensor_scalar(ar[:, a:a + 256], bank(x % 4, w=256), eff[:, k:k + 1], modcol[:, m:m + 1],
                                    ALU.mult, ALU.add).then_inc(z["jg"], 1)
                with dve.Fori(0, NQ - 1) as q:
                    quad(q, False, lambda t, c: t[:, bass.ds(c, 1)])
                quad(NQ - 1, True, lambda t, c: t[:, c:c + 1])
                dve.sem_inc(z["xready"], 1)
            dve.wait_ge(s_fin0, TL)
            rsqrt(ss[:, 0:TL], TL, D)
            dve.wait_ge(s_x, 16 * 5)
            for t in range(TL):
                V.scalar_tensor_tensor(ar[:, FIN + t * D:FIN + (t + 1) * D], X[:, (TC + t) * D:(TC + t + 1) * D],
                                       pwr[:, t:t + 1], gfin, ALU.mult, ALU.mult).then_inc(s_fin, 1)


INPUTS = ["x", "c", "ctx", "c_ctx", "w_mod", "b_mod", "g_attn", "g_ffn", "w_in", "a_sink", "b_q_norm", "b_w_uq", "b_kv_norm",
          "b_w_ukv", "c_lambda", "c_subln", "d_q_norm", "d_k_norm", "w_out", "w_router", "w_gate", "w_up", "w_down", "g_final"]


def shape_constants():
    col = np.arange(P)
    before = np.where(col[None, :] >= col[:, None], 0.0, NEG)
    after = np.where(col[None, :] <= col[:, None], 0.0, NEG)
    n = np.arange(LAT)
    tables = []
    for dim in (HD, B_ROPE):
        quarter = dim // 4
        inv = (np.float32(10000.0) ** (-np.arange(quarter, dtype=np.float32) / np.float32(quarter))).astype(np.float32)
        ang = np.concatenate([(n // GRID_W)[:, None].astype(np.float32) * inv, (n % GRID_W)[:, None].astype(np.float32) * inv], 1)
        tables.append(ang.astype(np.float64))
    ang = np.concatenate(tables, 1)
    rope = np.stack([np.cos(ang), np.sin(ang), -np.sin(ang)])
    rope = rope.reshape(3, TL, P, 48).transpose(2, 0, 1, 3).reshape(P, 3 * TL * 48)
    return {
        "ident": np.eye(P, dtype=np.float32),
        "iota": np.broadcast_to(np.arange(LAT, dtype=np.float32), (P, LAT)).copy(),
        "mask": np.concatenate([before, after], 1).astype(np.float32),
        "rope": rope.astype(np.float32),
    }


def kernel(**inputs):
    import numpy as _np
    import concourse.bacc as _bacc
    from concourse import mybir as _mybir
    from concourse.bass_utils import run_bass_kernel_spmd as _run

    nc = _bacc.Bacc("TRN2", target_bir_lowering=False, num_devices=1)
    given = {name: _np.ascontiguousarray(inputs[name]) for name in INPUTS}
    given.update(shape_constants())
    arrays, aps = {}, {}
    for name, a in given.items():
        arrays[f"in_{name}"] = a
        aps[name] = nc.dram_tensor(f"in_{name}", a.shape, _mybir.dt.from_np(a.dtype), kind="ExternalInput").ap()
    out = nc.dram_tensor("out_0", (1, LAT, D), _mybir.dt.float32, kind="ExternalOutput").ap()
    backbone_program(nc, aps, out)
    r = _run(nc, [arrays], core_ids=[0])
    return r.results[0]["out_0"]
```
